# Optimizing a Trainium2 kernel written in Bass

```python
import math
import jax
import jax.numpy as jnp
from jax import lax
import numpy as np
import jax, jax.numpy as jnp

D_MODEL = 1024
BATCH = 1
SEQ = 256
DEPTH = 1

CHUNK = 64
CONV_CH = D_MODEL
CONV_K = 31
D_INNER = 2 * D_MODEL
HEAD_DIM = 64
N_HEADS = D_INNER // HEAD_DIM
N_GROUPS = 8
HEADS_PER_GROUP = N_HEADS // N_GROUPS
D_STATE = 128
SSM_CONV_K = 4
XBC_CH = D_INNER + 2 * N_GROUPS * D_STATE
FFN_HIDDEN = ((8 * D_MODEL // 3 + 255) // 256) * 256
RMS_EPS = 1e-6
LN_EPS = 1e-5

OFF_Z = 2 * CONV_CH
OFF_XBC = OFF_Z + D_INNER
OFF_DT = OFF_XBC + XBC_CH
OFF_GATE = OFF_DT + N_HEADS
IN_COLS = OFF_GATE + 2 * D_MODEL


def rms_norm(x, g):
    xf = x.astype(jnp.float32)
    y = xf * lax.rsqrt(jnp.mean(xf * xf, axis=-1, keepdims=True) + RMS_EPS)
    return (y * g.astype(jnp.float32)).astype(x.dtype)

def layer_norm(x, g, b):
    xf = x.astype(jnp.float32)
    mu = jnp.mean(xf, axis=-1, keepdims=True)
    xc = xf - mu
    y = xc * lax.rsqrt(jnp.mean(xc * xc, axis=-1, keepdims=True) + LN_EPS)
    return (y * g.astype(jnp.float32) + b.astype(jnp.float32)).astype(x.dtype)

def causal_depthwise_conv(u, w, b):
    k, ch = w.shape
    y = lax.conv_general_dilated(
        u, w[:, None, :], window_strides=(1,), padding=[(k - 1, 0)],
        dimension_numbers=("NWC", "WIO", "NWC"), feature_group_count=ch)
    return y + b

def conformer_conv_branch(u_glu, glu_b, dw_w, dw_b, ln_g, ln_b, pw_w, pw_b):
    u = u_glu + glu_b
    val, gt = jnp.split(u, 2, axis=-1)
    v = val * jax.nn.sigmoid(gt)
    v = causal_depthwise_conv(v, dw_w, dw_b)
    v = jax.nn.silu(layer_norm(v, ln_g, ln_b))
    return v @ pw_w + pw_b

def ssd_chunked(x, dt, a, b_mat, c_mat, d_skip):
    bsz, seqlen = x.shape[0], x.shape[1]
    nc = seqlen // CHUNK
    G, R = N_GROUPS, HEADS_PER_GROUP
    x = x.reshape(bsz, nc, CHUNK, G, R, HEAD_DIM)
    dt = dt.reshape(bsz, nc, CHUNK, G, R)
    b_mat = b_mat.reshape(bsz, nc, CHUNK, G, D_STATE)
    c_mat = c_mat.reshape(bsz, nc, CHUNK, G, D_STATE)
    a_dt = jnp.transpose(dt * a.reshape(G, R), (0, 3, 4, 1, 2))
    a_cs = jnp.cumsum(a_dt, axis=-1)
    xdt = x * dt[..., None]
    causal = jnp.tril(jnp.ones((CHUNK, CHUNK), dtype=bool))
    seg = a_cs[..., :, None] - a_cs[..., None, :]
    decay_in = jnp.exp(jnp.where(causal, seg, -jnp.inf))
    cb = jnp.einsum("bclgn,bcsgn->bgcls", c_mat, b_mat)
    y_diag = jnp.einsum("bgcls,bgrcls,bcsgrp->bclgrp", cb, decay_in, xdt)
    decay_to_end = jnp.exp(a_cs[..., -1:] - a_cs)
    chunk_states = jnp.einsum("bclgn,bgrcl,bclgrp->bcgrpn", b_mat, decay_to_end, xdt)
    chunk_decay = jnp.exp(a_cs[..., -1])

    def step(carry, inp):
        s_c, dec_c = inp
        return carry * dec_c[..., None, None] + s_c, carry

    init = jnp.zeros((bsz, G, R, HEAD_DIM, D_STATE), jnp.float32)
    _, prev = lax.scan(step, init, (jnp.moveaxis(chunk_states, 1, 0),
                                    jnp.moveaxis(chunk_decay, -1, 0)))
    prev = jnp.moveaxis(prev, 0, 1)
    y_off = jnp.einsum("bclgn,bcgrpn,bgrcl->bclgrp", c_mat, prev, jnp.exp(a_cs))
    y = y_diag + y_off + x * d_skip.reshape(G, R)[..., None]
    return y.reshape(bsz, seqlen, N_HEADS * HEAD_DIM)

def ssd_branch(z, xbc, dt_raw, conv_w, conv_b, dt_bias, a_log, d_skip, norm_g, out_w):
    f32 = jnp.float32
    bsz, seqlen = z.shape[0], z.shape[1]
    xbc = jax.nn.silu(causal_depthwise_conv(xbc, conv_w, conv_b))
    gn = N_GROUPS * D_STATE
    xs = xbc[..., :D_INNER]
    bm = xbc[..., D_INNER:D_INNER + gn]
    cm = xbc[..., D_INNER + gn:]
    dt = jax.nn.softplus(dt_raw.astype(f32) + dt_bias.astype(f32))
    a = -jnp.exp(a_log.astype(f32))
    y = ssd_chunked(xs.astype(f32).reshape(bsz, seqlen, N_HEADS, HEAD_DIM), dt, a,
                    bm.astype(f32).reshape(bsz, seqlen, N_GROUPS, D_STATE),
                    cm.astype(f32).reshape(bsz, seqlen, N_GROUPS, D_STATE),
                    d_skip.astype(f32))
    y = y * jax.nn.silu(z.astype(f32))
    yg = y.reshape(bsz, seqlen, N_GROUPS, D_INNER // N_GROUPS)
    yg = yg * lax.rsqrt(jnp.mean(yg * yg, axis=-1, keepdims=True) + RMS_EPS)
    y = (yg.reshape(bsz, seqlen, D_INNER) * norm_g.astype(f32)).astype(z.dtype)
    return y @ out_w

def first_inputs(seed: int = 0) -> dict:
    key = jax.random.key(seed)
    ks = jax.random.split(key, 24)
    f32 = jnp.float32

    def nrm(k, shape, scale):
        return jax.random.normal(k, shape, f32) * scale

    def gain(k, n):
        return 1.0 + 0.05 * jax.random.normal(k, (DEPTH, n), f32)

    u = jax.random.uniform(ks[13], (DEPTH, N_HEADS), f32)
    dt0 = jnp.exp(u * (math.log(0.1) - math.log(1e-3)) + math.log(1e-3))
    dt_bias = dt0 + jnp.log(-jnp.expm1(-dt0))
    a_log = jnp.log(jax.random.uniform(ks[14], (DEPTH, N_HEADS), f32, 1.0, 16.0))
    return {
        "x": nrm(ks[0], (BATCH, SEQ, D_MODEL), 1.0),
        "mix_pre_g": gain(ks[1], D_MODEL),
        "w_in": nrm(ks[2], (DEPTH, D_MODEL, IN_COLS), D_MODEL ** -0.5),
        "gate_b": nrm(ks[3], (DEPTH, 2 * D_MODEL), 0.02),
        "glu_b": nrm(ks[4], (DEPTH, 2 * CONV_CH), 0.02),
        "conv_dw_w": nrm(ks[5], (DEPTH, CONV_K, CONV_CH), CONV_K ** -0.5),
        "conv_dw_b": nrm(ks[6], (DEPTH, CONV_CH), 0.02),
        "conv_ln_g": gain(ks[7], CONV_CH),
        "conv_ln_b": nrm(ks[8], (DEPTH, CONV_CH), 0.02),
        "conv_pw_w": nrm(ks[9], (DEPTH, CONV_CH, D_MODEL), CONV_CH ** -0.5),
        "conv_pw_b": nrm(ks[10], (DEPTH, D_MODEL), 0.02),
        "ssm_conv_w": nrm(ks[11], (DEPTH, SSM_CONV_K, XBC_CH), SSM_CONV_K ** -0.5),
        "ssm_conv_b": nrm(ks[12], (DEPTH, XBC_CH), 0.02),
        "dt_bias": dt_bias,
        "a_log": a_log,
        "d_skip": 1.0 + 0.1 * jax.random.normal(ks[15], (DEPTH, N_HEADS), f32),
        "ssm_norm_g": gain(ks[16], D_INNER),
        "ssm_out_w": nrm(ks[17], (DEPTH, D_INNER, D_MODEL), D_INNER ** -0.5),
        "w_out": nrm(ks[18], (DEPTH, D_MODEL, D_MODEL), D_MODEL ** -0.5),
        "mix_post_g": gain(ks[19], D_MODEL),
        "ffn_pre_g": gain(ks[20], D_MODEL),
        "w_gate_up": nrm(ks[21], (DEPTH, D_MODEL, 2 * FFN_HIDDEN), D_MODEL ** -0.5),
        "w_down": nrm(ks[22], (DEPTH, FFN_HIDDEN, D_MODEL), FFN_HIDDEN ** -0.5),
        "ffn_post_g": gain(ks[23], D_MODEL),
    }

def first_block(x, mix_pre_g, w_in, gate_b, glu_b, conv_dw_w, conv_dw_b, conv_ln_g,
              conv_ln_b, conv_pw_w, conv_pw_b, ssm_conv_w, ssm_conv_b, dt_bias, a_log,
              d_skip, ssm_norm_g, ssm_out_w, w_out, mix_post_g, ffn_pre_g, w_gate_up,
              w_down, ffn_post_g):
    for i in range(DEPTH):
        h = rms_norm(x, mix_pre_g[i])
        proj = h @ w_in[i]
        u_glu = proj[..., :OFF_Z]
        z = proj[..., OFF_Z:OFF_XBC]
        xbc = proj[..., OFF_XBC:OFF_DT]
        dt_raw = proj[..., OFF_DT:OFF_GATE]
        gates = jax.nn.sigmoid(proj[..., OFF_GATE:] + gate_b[i])
        g_conv, g_ssm = jnp.split(gates, 2, axis=-1)
        conv_out = conformer_conv_branch(u_glu, glu_b[i], conv_dw_w[i], conv_dw_b[i],
                                         conv_ln_g[i], conv_ln_b[i], conv_pw_w[i],
                                         conv_pw_b[i])
        ssm_out = ssd_branch(z, xbc, dt_raw, ssm_conv_w[i], ssm_conv_b[i], dt_bias[i],
                             a_log[i], d_skip[i], ssm_norm_g[i], ssm_out_w[i])
        mixed = (g_conv * conv_out + g_ssm * ssm_out) @ w_out[i]
        x = x + rms_norm(mixed, mix_post_g[i])
        h = rms_norm(x, ffn_pre_g[i])
        gt, up = jnp.split(h @ w_gate_up[i], 2, axis=-1)
        f = (jax.nn.silu(gt) * up) @ w_down[i]
        x = x + rms_norm(f, ffn_post_g[i])
    return x


LRU_HEADS = 16
LRU_HEAD_DIM = 64
D_LRU = LRU_HEADS * LRU_HEAD_DIM
SC_GROUPS = 8
SC_GROUP_DIM = 64
D_SC = SC_GROUPS * SC_GROUP_DIM
D_MIX = D_LRU + D_SC
D_IN = 2 * D_LRU + 3 * D_SC
LRU_CONV_WIDTH = 4
SC_CONV_WIDTH = 3
RG_C = 8.0
D_FF = 3 * D_MODEL
FFN_CONV_WIDTH = 3
EPS = 1e-6


def rms_norm_2(x, g):
    xf = x.astype(jnp.float32)
    y = xf * lax.rsqrt(jnp.mean(xf * xf, axis=-1, keepdims=True) + EPS)
    return (y * g.astype(jnp.float32)).astype(x.dtype)

def causal_dwconv(x, w):
    k_width = w.shape[0]
    s = x.shape[1]
    xp = jnp.pad(x, ((0, 0), (k_width - 1, 0), (0, 0)))
    y = xp[:, 0:s] * w[0]
    for k in range(1, k_width):
        y = y + xp[:, k:k + s] * w[k]
    return y

def rg_lru(x, wa, ba, wx, bx, lam):
    bsz, s, c = x.shape
    xh = x.reshape(bsz, s, LRU_HEADS, LRU_HEAD_DIM)
    r = jax.nn.sigmoid(jnp.einsum('bshi,hij->bshj', xh, wa).reshape(bsz, s, c) + ba)
    i = jax.nn.sigmoid(jnp.einsum('bshi,hij->bshj', xh, wx).reshape(bsz, s, c) + bx)
    log_a = -RG_C * r.astype(jnp.float32) * jax.nn.softplus(-lam.astype(jnp.float32))
    a = jnp.exp(log_a)
    mult = jnp.sqrt(-jnp.expm1(2.0 * log_a))
    b = mult * (i * x).astype(jnp.float32)

    def combine(left, right):
        a1, b1 = left
        a2, b2 = right
        return a1 * a2, a2 * b1 + b2

    _, h = lax.associative_scan(combine, (a, b), axis=1)
    return h.astype(x.dtype)

def second_inputs(seed: int = 0) -> dict:
    key = jax.random.key(seed)
    ks = jax.random.split(key, 20)
    f32 = jnp.float32
    res_scale = (2.0 * DEPTH) ** -0.5
    x = jax.random.normal(ks[0], (BATCH, SEQ, D_MODEL), f32)
    norm1_g = 1.0 + 0.02 * jax.random.normal(ks[1], (DEPTH, D_MODEL), f32)
    w_in = jax.random.normal(ks[2], (DEPTH, D_MODEL, D_IN), f32) * D_MODEL ** -0.5
    lru_conv_w = jax.random.normal(ks[3], (DEPTH, LRU_CONV_WIDTH, D_LRU), f32) * LRU_CONV_WIDTH ** -0.5
    lru_conv_b = 0.02 * jax.random.normal(ks[4], (DEPTH, D_LRU), f32)
    lru_wa = jax.random.normal(ks[5], (DEPTH, LRU_HEADS, LRU_HEAD_DIM, LRU_HEAD_DIM), f32) * LRU_HEAD_DIM ** -0.5
    lru_ba = 0.02 * jax.random.normal(ks[6], (DEPTH, D_LRU), f32)
    lru_wx = jax.random.normal(ks[7], (DEPTH, LRU_HEADS, LRU_HEAD_DIM, LRU_HEAD_DIM), f32) * LRU_HEAD_DIM ** -0.5
    lru_bx = 0.02 * jax.random.normal(ks[8], (DEPTH, D_LRU), f32)
    u = jax.random.uniform(ks[9], (DEPTH, D_LRU), f32, minval=0.9, maxval=0.999)
    a0 = u ** (1.0 / RG_C)
    lru_lambda = jnp.log(a0) - jnp.log1p(-a0)
    sc_conv_w = jax.random.normal(ks[10], (DEPTH, SC_CONV_WIDTH, D_SC), f32) * SC_CONV_WIDTH ** -0.5
    w_out = jax.random.normal(ks[11], (DEPTH, D_MIX, D_MODEL), f32) * D_MIX ** -0.5 * res_scale
    norm2_g = 1.0 + 0.02 * jax.random.normal(ks[12], (DEPTH, D_MODEL), f32)
    w_up = jax.random.normal(ks[13], (DEPTH, D_MODEL, 2 * D_FF), f32) * D_MODEL ** -0.5
    ffn_conv_w = jax.random.normal(ks[14], (DEPTH, FFN_CONV_WIDTH, 2 * D_FF), f32) * FFN_CONV_WIDTH ** -0.5
    w_down = jax.random.normal(ks[15], (DEPTH, D_FF, D_MODEL), f32) * D_FF ** -0.5 * res_scale
    final_g = 1.0 + 0.02 * jax.random.normal(ks[16], (D_MODEL,), f32)
    return {"x": x, "norm1_g": norm1_g, "w_in": w_in, "lru_conv_w": lru_conv_w,
            "lru_conv_b": lru_conv_b, "lru_wa": lru_wa, "lru_ba": lru_ba, "lru_wx": lru_wx,
            "lru_bx": lru_bx, "lru_lambda": lru_lambda, "sc_conv_w": sc_conv_w, "w_out": w_out,
            "norm2_g": norm2_g, "w_up": w_up, "ffn_conv_w": ffn_conv_w, "w_down": w_down,
            "final_g": final_g}

def second_block(x, norm1_g, w_in, lru_conv_w, lru_conv_b, lru_wa, lru_ba, lru_wx, lru_bx,
              lru_lambda, sc_conv_w, w_out, norm2_g, w_up, ffn_conv_w, w_down, final_g):
    splits = [D_LRU, 2 * D_LRU, 2 * D_LRU + D_SC, 2 * D_LRU + 2 * D_SC]
    for l in range(DEPTH):
        h = rms_norm_2(x, norm1_g[l])
        z = jnp.einsum('bsd,de->bse', h, w_in[l])
        lru_x, lru_gate, sc_b, sc_c, sc_x = jnp.split(z, splits, axis=-1)
        lru_x = causal_dwconv(lru_x, lru_conv_w[l]) + lru_conv_b[l]
        y_lru = rg_lru(lru_x, lru_wa[l], lru_ba[l], lru_wx[l], lru_bx[l], lru_lambda[l]) \
            * jax.nn.gelu(lru_gate)
        y_sc = sc_b * causal_dwconv(sc_c * sc_x, sc_conv_w[l])
        y_mix = jnp.concatenate([y_lru, y_sc], axis=-1)
        x = x + jnp.einsum('bse,ed->bsd', y_mix, w_out[l])
        h = rms_norm_2(x, norm2_g[l])
        u = causal_dwconv(jnp.einsum('bsd,df->bsf', h, w_up[l]), ffn_conv_w[l])
        gate, up = jnp.split(u, 2, axis=-1)
        x = x + jnp.einsum('bsf,fd->bsd', jax.nn.gelu(gate) * up, w_down[l])
    return rms_norm_2(x, final_g)


def setup_inputs(seed=0):
    out = dict(first_inputs(seed))
    for name, value in second_inputs(seed + 1).items():
        if name != "x":
            out[name + "_2"] = value
    return out


def reference(
    x, mix_pre_g, w_in, gate_b, glu_b, conv_dw_w, conv_dw_b, conv_ln_g, conv_ln_b, conv_pw_w,
    conv_pw_b, ssm_conv_w, ssm_conv_b, dt_bias, a_log, d_skip, ssm_norm_g, ssm_out_w, w_out,
    mix_post_g, ffn_pre_g, w_gate_up, w_down, ffn_post_g, norm1_g_2, w_in_2, lru_conv_w_2,
    lru_conv_b_2, lru_wa_2, lru_ba_2, lru_wx_2, lru_bx_2, lru_lambda_2, sc_conv_w_2, w_out_2,
    norm2_g_2, w_up_2, ffn_conv_w_2, w_down_2, final_g_2,
):
    x = first_block(
        x, mix_pre_g, w_in, gate_b, glu_b, conv_dw_w, conv_dw_b, conv_ln_g, conv_ln_b,
        conv_pw_w, conv_pw_b, ssm_conv_w, ssm_conv_b, dt_bias, a_log, d_skip, ssm_norm_g,
        ssm_out_w, w_out, mix_post_g, ffn_pre_g, w_gate_up, w_down, ffn_post_g,
    )
    return second_block(
        x, norm1_g_2, w_in_2, lru_conv_w_2, lru_conv_b_2, lru_wa_2, lru_ba_2, lru_wx_2,
        lru_bx_2, lru_lambda_2, sc_conv_w_2, w_out_2, norm2_g_2, w_up_2, ffn_conv_w_2, w_down_2,
        final_g_2,
    )


_drawn_inputs = setup_inputs


def setup_inputs(seed=0):
    import zlib

    import numpy as np

    out = dict(_drawn_inputs(seed))
    spreads = {}
    factors = {'gate_b': 8.0,
     'glu_b': 4.783,
     'conv_ln_b': 5.726,
     'conv_pw_b': 3.452,
     'ssm_conv_b': 2.689,
     'norm1_g_2': 5.926,
     'lru_conv_b_2': 27.568,
     'lru_ba_2': 64.0,
     'lru_bx_2': 64.0,
     'norm2_g_2': 46.376,
     'final_g_2': 7.493}
    for name, (base, spread) in spreads.items():
        noise = np.random.default_rng([zlib.crc32(name.encode()), seed]).standard_normal(out[name].shape)
        drawn = base * np.exp(spread * noise) if base else spread * noise
        out[name] = jnp.asarray(drawn.astype(out[name].dtype))
    for name, factor in factors.items():
        out[name] = (out[name] * factor).astype(out[name].dtype)
    return out
```

```python
from contextlib import ExitStack

import numpy as np

import concourse.bass as bass
from concourse import mybir

F32 = mybir.dt.float32
F32R = mybir.dt.float32r
ALU = mybir.AluOpType
ACT = mybir.ActivationFunctionType

P = 128
T = 256
D = 1024
KD = D // P
TT = T // P
PIECE = 8 * P
RING = 8
LEAD = 6
PAIRS = RING // 2

CONV_K = 31
PAD = CONV_K - 1
GROUPS = 8
HEADS = 32
HPG = HEADS // GROUPS
HD = 64
D_INNER = 2 * D
SSM_K = 4
FFN = 2816
KF = FFN // P
D_LRU = 1024
D_SC = 512
KSC = D_SC // P
LRU_K = 4
SC_K = 3
FFN2 = 3 * D
KF2 = FFN2 // P
FFN_K = 3
RMS_EPS = 1e-6
LN_EPS = 1e-5
RG_C = 8.0

GLU0 = 0
SSM0 = GLU0 + 2 * KD
LOOP0 = SSM0 + 6
GATES0 = LOOP0 + 8 * (GROUPS - 1)
TAIL0 = GATES0 + 2 * KD
PW0 = TAIL0 + 2
MIX0 = PW0 + KD
UP1 = MIX0 + KD
DOWN1 = UP1 + 2 * KF
LRUX0 = DOWN1 + KF
SC0 = LRUX0 + KD
LRUG0 = SC0 + 3 * KSC
OUT2 = LRUG0 + KD
UP2 = OUT2 + KD + KSC
DOWN2 = UP2 + 2 * KF2
PIECES = DOWN2 + KF2
UP1_TURNS = 2 * KF // RING
UP2_TURNS = 2 * KF2 // RING
DOWN1_REST = KF - 2 * KD

PARAMS = [("mix_pre_g", KD), ("glu_b", 2 * KD), ("conv_dw_w", KD * CONV_K), ("conv_dw_b", KD),
          ("conv_ln_g", KD), ("conv_ln_b", KD), ("conv_pw_b", KD), ("ssm_conv_w", 32 * SSM_K),
          ("ssm_conv_b", 32), ("d_skip", 16), ("ssm_norm_g", 16), ("gate_b", 2 * KD), ("mix_post_g", KD),
          ("ffn_pre_g", KD), ("ffn_post_g", KD), ("norm1_g_2", KD), ("lru_conv_w_2", KD * LRU_K),
          ("lru_conv_b_2", KD), ("lru_ba_2", KD), ("lru_bx_2", KD), ("lru_lambda_2", KD),
          ("sc_conv_w_2", KSC * SC_K), ("norm2_g_2", KD), ("ffn_conv_w_2", 2 * KF2 * FFN_K),
          ("final_g_2", KD), ("dt_bias", 1), ("a_log", 1)]
AT = {}
NPAR = 0
for _name, _n in PARAMS:
    AT[_name] = NPAR
    NPAR += _n


STAGED_MIX = KD
STAGED_FFN1 = STAGED_MIX + 2 * KD
STAGED_SC = STAGED_FFN1 + KF + KD
STAGED_LRU = STAGED_SC + KSC


class Count:

    def __init__(self, sem):
        self.sem, self.n, self.turn = sem, 0, None

    def value(self):
        return self.n if self.turn is None else self.n + self.per * self.turn

    def up(self, instruction):
        instruction.then_inc(self.sem, 1)
        self.n += 1
        return self.value()

    def enter(self, turn, per):
        self.turn, self.per, self.start = turn, per, self.n

    def leave(self, turns):
        assert self.n - self.start == self.per, (self.n - self.start, self.per)
        self.n, self.turn = self.start + self.per * turns, None


def hybrid_kernel(nc, x_in, weights, params_in, w_dt, lru_w, consts, out):
    cs_dram = nc.dram_tensor("cs_dram", [HEADS, T], F32).ap()
    stack = ExitStack()
    with stack:
        def sb(name, shape, dt=F32, scope=stack):
            return scope.enter_context(nc.sbuf_tensor(name, shape, dt))

        def sem(name):
            return stack.enter_context(nc.semaphore(name))

        raw = sb("raw", [P, RING, PIECE])
        w_hi = sb("w_hi", [P, RING, PIECE], F32R)
        w_lo = sb("w_lo", [P, RING, PIECE], F32R)
        x = sb("x", [P, KD, T])
        h_hi = sb("h_hi", [P, KD, T], F32R)
        h_lo = sb("h_lo", [P, KD, T], F32R)
        par = sb("par", [P, NPAR])
        cst = sb("cst", [P, 5 * P])
        half = sb("half", [P, 1])
        zero = sb("zero", [P, P], F32R)
        mean = sb("mean", [P, T])
        rstd = sb("rstd", [P, T])
        stage = sb("stage", [P, 2, T])
        stage2 = sb("stage2", [P, 2, T])
        ident = cst[:, 0:P]
        ones = cst[:, P:2 * P]
        mask = cst[:, 2 * P:5 * P]

        s1 = ExitStack()
        v = sb("v", [P, KD, PAD + T], scope=s1)
        acc = sb("acc", [P, KD, T], scope=s1)
        s1.close()
        s2 = ExitStack()
        conv_hi = sb("conv_hi", [P, KD, T], F32R, s2)
        conv_lo_pad = sb("conv_lo_pad", [P, KD * PAD], scope=s2)
        conv_lo = sb("conv_lo", [P, KD, T], F32R, s2)
        s2.close()
        sq_wide = sb("sq_wide", [P, KD, PAD + T])
        m_wide = sb("m_wide", [P, KD, T])

        s3 = ExitStack()
        gates = sb("gates", [P, 2 * KD, T], scope=s3)
        ubuf = sb("ubuf", [P, 4, SSM_K - 1 + T], scope=s3)
        gb = sb("gb", [P, 4, T], scope=s3)
        zs = sb("zs", [P, 2, T], scope=s3)
        csrow = sb("csrow", [P, HPG, T], scope=s3)
        dec = sb("dec", [P, HPG, 3 * P], scope=s3)
        xdt = sb("xdt", [P, TT, HPG, HD], scope=s3)
        cbm = sb("cbm", [P, 3 * P], scope=s3)
        y = sb("y", [P, 2, T], scope=s3)
        yn_hi = sb("yn_hi", [P, 2, T], F32R, s3)
        yn_lo = sb("yn_lo", [P, 2, T], F32R, s3)
        part_a = sb("part_a", [P, T], scope=s3)
        part_b = sb("part_b", [P, T], scope=s3)
        wdt = sb("wdt", [P, KD, HEADS], scope=s3)
        tok = sb("tok", [P, 5, HEADS], scope=s3)
        s3.close()
        s4 = ExitStack()
        hid_hi = sb("hid_hi", [P, KF2, T], F32R, s4)
        hid_lo = sb("hid_lo", [P, KF2, T], F32R, s4)
        stage3 = sb("stage3", [P, 2, T], scope=s4)
        s4.close()
        s5 = ExitStack()
        ig = sb("ig", [P, KD, T], scope=s5)
        a_t = sb("a_t", [P, KD, T], scope=s5)
        th = sb("th", [P, KD, T], scope=s5)
        bd = sb("bd", [P, KD, 2, P], scope=s5)
        sc_hi = sb("sc_hi", [P, KSC, T], F32R, s5)
        sc_lo = sb("sc_lo", [P, KSC, T], F32R, s5)
        sc_sum = sb("sc_sum", [P, T], scope=s5)
        u2 = sb("u2", [P, 2, LRU_K - 1 + T], scope=s5)
        sp = sb("sp", [P, 8, KD], scope=s5)
        s5.close()
        s6 = ExitStack()
        lru_hi = sb("lru_hi", [P, KD, T], F32R, s6)
        lru_lo = sb("lru_lo", [P, KD, T], F32R, s6)
        s6.close()
        xp, rg = sq_wide, m_wide

        A = [stack.enter_context(nc.psum_tensor(f"A{i}", [P, 512], F32)) for i in range(4)]
        B = stack.enter_context(nc.psum_tensor("B", [P, 4, 512], F32))

        def acc_out(m):
            return B[:, m // 2, (m % 2) * T:(m % 2 + 1) * T]

        loaded = [sem(f"loaded{i}") for i in range(PAIRS)]
        x_loaded, const_loaded = sem("x_loaded"), sem("const_loaded")
        hi_ready, lo_ready, pieces_done = sem("hi_ready"), sem("lo_ready"), sem("pieces_done")
        pad_ready = sem("pad_ready")
        squares_ready, sums_ready = sem("squares_ready"), sem("sums_ready")
        mean_ready, rstd_ready = sem("mean_ready"), sem("rstd_ready")
        staged, stage_hi, operand_ready = sem("staged"), sem("stage_hi"), sem("operand_ready")
        act_steps, dve_steps = sem("act_steps"), sem("dve_steps")
        dt_raw_ready, dt_raw_used, cs_ready, tok_psum, tok_ready = (
            sem("dt_raw_ready"), sem("dt_raw_used"), sem("cs_ready"), sem("tok_psum"), sem("tok_ready"))
        dt_abs, dt_exp = sem("dt_abs"), sem("dt_exp")
        cs_stored, csrow_loaded = sem("cs_stored"), sem("csrow_loaded")
        gate_ready, pairs_drained, drained = sem("gate_ready"), sem("pairs_drained"), sem("drained")
        conv_ready, silu_ready = sem("conv_ready"), sem("silu_ready")
        cb_ready, cb_used, xt_ready, xdt_ready = sem("cb_ready"), sem("cb_used"), sem("xt_ready"), sem("xdt_ready")
        seg_ready, dec_ready, m_ready, y_ready, yz_ready = (
            sem("seg_ready"), sem("dec_ready"), sem("m_ready"), sem("y_ready"), sem("yz_ready"))
        ysq_ready, yn32_ready, ynhi_ready, yn_ready = (
            sem("ysq_ready"), sem("yn32_ready"), sem("ynhi_ready"), sem("yn_ready"))
        conv_sum_ready, centred, conv_norm, mix_drained = (
            sem("conv_sum_ready"), sem("centred"), sem("conv_norm"), sem("mix_drained"))
        x_new, lru_w_loaded, c_ready, sp_exp = sem("x_new"), sem("lru_w_loaded"), sem("c_ready"), sem("sp_exp")
        copied, xp_ready, bd_ready, bd_drained, a_ready, m2_ready, mult_ready, gelu_ready = (
            sem("copied"), sem("xp_ready"), sem("bd_ready"), sem("bd_drained"), sem("a_ready"), sem("m2_ready"),
            sem("mult_ready"), sem("gelu_ready"))
        sc_copied, tap_ready, conv2_ready = sem("sc_copied"), sem("tap_ready"), sem("conv2_ready")
        out_ready, stored = sem("out_ready"), sem("stored")

        def col(name, c, n=1):
            return par[:, AT[name] + c:AT[name] + c + n]

        def dcol(name, c):
            return par[:, bass.ds(c + AT[name], 1)]

        block = stack.enter_context(nc.Block())

        @block.sync
        def _(sp_):
            sp_.dma_start(x[:, :, :], x_in).then_inc(x_loaded, 16)
            sp_.dma_start(par[:, :], params_in).then_inc(const_loaded, 16)
            sp_.dma_start(cst[:, :], consts).then_inc(const_loaded, 16)
            sp_.dma_start(wdt[:, :, :], w_dt).then_inc(const_loaded, 16)
            for q in range(PAIRS):
                sp_.dma_start(raw[:, 2 * q:2 * q + 2, :], weights[q]).then_inc(loaded[q], 16)
            rounds = PIECES // RING
            with sp_.Fori(1, rounds) as r:
                for q in range(PAIRS):
                    sp_.wait_ge(lo_ready, r * RING + (2 * q + 2 - RING))
                    sp_.dma_start(raw[:, 2 * q:2 * q + 2, :],
                                  weights[bass.ds(r * PAIRS + q, 1)].rearrange("a p s n -> p (a s) n")
                                  ).then_inc(loaded[q], 16)
            for q in range(rounds * PAIRS, PIECES // 2):
                s = q % PAIRS
                sp_.wait_ge(lo_ready, 2 * (q - PAIRS) + 2)
                sp_.dma_start(raw[:, 2 * s:2 * s + 2, :], weights[q]).then_inc(loaded[s], 16)
            for c in range(KD):
                sp_.wait_ge(out_ready, c + 1)
                sp_.dma_start(out[:, c, :], m_wide[:, c, :]).then_inc(stored, 16)
            sp_.wait_ge(stored, 16 * KD)

        @block.gpsimd
        def _(pool):
            nc.gpsimd.memset(half[:, :], -0.5).then_inc(pad_ready, 1)
            nc.gpsimd.memset(zero[:, :].bitcast(F32), 0.0).then_inc(pad_ready, 1)
            nc.gpsimd.memset(v[:, :, 0:PAD], 0.0).then_inc(pad_ready, 1)
            nc.gpsimd.memset(ubuf[:, :, 0:SSM_K - 1], 0.0).then_inc(pad_ready, 1)
            pool.wait_ge(pad_ready, 4)

            def rsqrt(n):
                pool.wait_ge(mean_ready, n)
                nc.gpsimd.tensor_tensor(rstd[:, :], mean[:, :], half[:, 0:1].to_broadcast([P, T]),
                                        ALU.pow).then_inc(rstd_ready, 1)

            rsqrt(1)
            with pool.Fori(0, GROUPS) as g:
                rsqrt(g + 2)
            for n in range(10, 17):
                rsqrt(n)

        @block.tensor
        def _(pe):
            mm = nc.tensor.matmul

            def tile(slot, j, hi, lo, dst, first, last, free=False):
                wh = w_hi[:, slot, j * P:(j + 1) * P]
                wl = w_lo[:, slot, j * P:(j + 1) * P]
                mm(dst, wh, lo, start=first, stop=False, skip_group_check=free)
                mm(dst, wh, hi, start=False, stop=False, skip_group_check=free)
                return mm(dst, wl, hi, start=False, stop=last, skip_group_check=free)

            def chunk_piece(p, turn, dst, hi, lo, operand=0):
                pe.wait_ge(lo_ready, p + 1 + 8 * turn)
                for k in range(KD):
                    if operand:
                        pe.wait_ge(operand_ready, operand + k + 1)
                    ins = tile(p % RING, k, hi[:, k, :], lo[:, k, :], dst, k == 0, k == KD - 1)
                ins.then_inc(pieces_done, 1)

            def clear_accumulators():
                for b in range(4):
                    mm(B[:, b, :], zero[:, :], zero[:, :].unsqueeze(1).to_broadcast([P, 4, P]), start=True,
                       stop=False, skip_group_check=True)

            def channel_sums(bank, src, n0):
                for c in range(KD):
                    if n0 is not None:
                        pe.wait_ge(squares_ready, n0 + c + 1)
                    ins = mm(bank[:, 0:T], ones, src[:, c, 0:T], start=c == 0, stop=c == KD - 1)
                ins.then_inc(sums_ready, 1)

            pe.wait_ge(const_loaded, 48)
            channel_sums(A[3], acc, 0)
            for k in range(KD):
                pe.wait_ge(operand_ready, k + 1)
                ins = mm(A[2][0:HEADS, 0:T], wdt[:, k, :], acc[:, k, :], start=k == 0, stop=k == KD - 1)
            ins.then_inc(dt_raw_ready, 1)
            pe.wait_ge(pad_ready, 4)
            clear_accumulators()
            for c in range(KD):
                for j in range(2):
                    if c >= 2:
                        pe.wait_ge(pairs_drained, c - 1)
                    elif c == 1:
                        pe.wait_ge(dt_raw_used, 1)
                    chunk_piece(GLU0 + 2 * c + j, 0, A[2 * (c % 2) + j][:, 0:T], h_hi, h_lo)
            pe.wait_ge(cs_ready, 1)
            pe.wait_ge(pairs_drained, KD)
            dtw = gates
            for n, src in enumerate([dtw[0:HEADS, 0, 0:P], dtw[0:HEADS, 0, P:T], dtw[0:HEADS, 1, 0:P],
                                     dtw[0:HEADS, 1, P:T], dtw[0:HEADS, 2, 0:P]]):
                ins = nc.tensor.transpose(A[3][:, n * HEADS:(n + 1) * HEADS], src, ident[0:HEADS, 0:HEADS])
            ins.then_inc(tok_psum, 1)

            def ring_bank(o):
                return A[o % 3][:, 0:T]

            def single(p, o, turn=0, per=0):
                if o >= 3 or per:
                    pe.wait_ge(drained, o - 2 + per * turn)
                chunk_piece(p, turn, ring_bank(o), h_hi, h_lo)

            for o in range(6):
                single(SSM0 + o, o)
            pe.wait_ge(tok_ready, 1)

            def cb(g):
                pe.wait_ge(silu_ready, 4 * g + 2)
                pe.wait_ge(mean_ready, g + 1)
                mm(A[3][:, 0:T], gb[:, 0, 0:P], gb[:, 1, :], start=True, stop=True)
                mm(A[3][:, T:T + P], gb[:, 0, P:T], gb[:, 1, P:T], start=True, stop=True).then_inc(cb_ready, 1)

            def x_transposes(g):
                pe.wait_ge(silu_ready, 4 * g + 4)
                pe.wait_ge(cb_used, g + 1)
                for t in range(TT):
                    for c in range(2):
                        ins = nc.tensor.transpose(A[3][:, t * T + c * P:t * T + (c + 1) * P],
                                                  gb[:, 2 + c, t * P:(t + 1) * P], ident)
                ins.then_inc(xt_ready, 1)

            def y_products(g):
                pe.wait_ge(m_ready, g + 1)
                for r in range(HPG):
                    rows = slice(HD * (r % 2), HD * (r % 2) + HD)
                    at = (r // 2) * T
                    mm(A[3][rows, at:at + T], xdt[:, 0, r, :], dec[:, r, 0:T], start=True, stop=False)
                    ins = mm(A[3][rows, at + P:at + T], xdt[:, 1, r, :], dec[:, r, T:T + P], start=False, stop=True)
                ins.then_inc(y_ready, 1)

            def y_sums(g):
                pe.wait_ge(ysq_ready, g + 1)
                mm(A[3][:, 0:T], ones, dec[:, :, :].rearrange("p a b -> p (a b)")[:, 0:T], start=True, stop=False)
                mm(A[3][:, 0:T], ones, dec[:, :, :].rearrange("p a b -> p (a b)")[:, T:2 * T], start=False,
                   stop=True).then_inc(sums_ready, 1)

            def out_piece(p, turn, g, c):
                pe.wait_ge(lo_ready, p + 1 + 8 * turn)
                pe.wait_ge(yn_ready, 2 * g + c + 1)
                for m in range(KD):
                    ins = tile(p % RING, m, yn_hi[:, c, :], yn_lo[:, c, :], acc_out(m), False, False, True)
                ins.then_inc(pieces_done, 1)

            with pe.Fori(0, GROUPS - 1) as i:
                for s in range(6):
                    single(LOOP0 + s, 6 + s, i, 6)
                    {0: cb, 1: x_transposes, 3: y_products, 4: y_sums}.get(s, lambda g: None)(i)
                out_piece(LOOP0 + 6, i, i, 0)
                out_piece(LOOP0 + 7, i, i, 1)
            g = GROUPS - 1
            for s in range(2 * KD):
                single(GATES0 + s, 6 * GROUPS + s)
                {0: cb, 1: x_transposes, 3: y_products, 5: y_sums}.get(s, lambda g: None)(g)
                if s == 8:
                    pe.wait_ge(conv_sum_ready, 1)
                    channel_sums(A[3], acc, None)
                if s == 12:
                    channel_sums(A[3], v, KD)
            out_piece(TAIL0, 0, g, 0)
            out_piece(TAIL0 + 1, 0, g, 1)
            for m in range(KD):
                if m < 3:
                    pe.wait_ge(drained, 6 * GROUPS + 2 * KD - 2 + m)
                else:
                    pe.wait_ge(mix_drained, m - 2)
                chunk_piece(PW0 + m, 0, ring_bank(64 + m), conv_hi, conv_lo, KD if m == 0 else 0)
            for m in range(KD):
                if m < 3:
                    pe.wait_ge(mix_drained, KD - 2 + m)
                else:
                    pe.wait_ge(squares_ready, 2 * KD + m - 2)
                chunk_piece(MIX0 + m, 0, ring_bank(72 + m), h_hi, h_lo, 2 * KD if m == 0 else 0)
            channel_sums(A[3], sq_wide, 2 * KD)
            channel_sums(A[3], sq_wide, 3 * KD)

            def up_pair(base, j, turn, read=None, n=None, first_operand=0):
                for half_ in range(2):
                    if n is not None:
                        pe.wait_ge(read, n)
                    chunk_piece(base + 2 * j + half_, turn, A[j % 2 * 2 + half_][:, 0:T], h_hi, h_lo,
                                first_operand if half_ == 0 else 0)

            up_pair(UP1, 0, 0, first_operand=3 * KD)
            up_pair(UP1, 1, 0)
            for j in range(2, 4):
                up_pair(UP1, j, 0, staged, STAGED_FFN1 + j - 1)
            with pe.Fori(1, UP1_TURNS) as i:
                for j in range(4):
                    up_pair(UP1, j, i, staged, i * 4 + (STAGED_FFN1 + j - 1))
            for j in range(UP1_TURNS * 4, KF):
                up_pair(UP1, j, 0, staged, STAGED_FFN1 + j - 1)

            def down_turns(p, turns, operand):
                with pe.Fori(0, turns) as i:
                    for m in range(KD):
                        pe.wait_ge(lo_ready, p + m + 1 + 8 * i)
                        if m == 0:
                            pe.wait_ge(operand_ready, i * 8 + (operand + 8))
                        for k in range(8):
                            ins = tile((p + m) % RING, k, hid_hi[:, bass.ds(i * 8 + k, 1), :].rearrange("p a t -> p (a t)"),
                                       hid_lo[:, bass.ds(i * 8 + k, 1), :].rearrange("p a t -> p (a t)"),
                                       acc_out(m), False, False, True)
                        ins.then_inc(pieces_done, 1)

            clear_accumulators()
            done1 = 4 * KD
            down_turns(DOWN1, 2, done1)
            for n in range(DOWN1_REST * KD):
                p = DOWN1 + 2 * KD + n // 8
                m, k = n // DOWN1_REST, n % DOWN1_REST
                if n % 8 == 0:
                    pe.wait_ge(lo_ready, p + 1)
                if m == 0:
                    pe.wait_ge(operand_ready, done1 + 2 * KD + k + 1)
                ins = tile(p % RING, n % 8, hid_hi[:, 2 * KD + k, :], hid_lo[:, 2 * KD + k, :], acc_out(m),
                           False, False, True)
                if n % 8 == 7:
                    ins.then_inc(pieces_done, 1)
            channel_sums(A[3], sq_wide, 4 * KD)
            channel_sums(A[3], sq_wide, 5 * KD)

            ops = done1 + KF

            def block_gates(c):
                pe.wait_ge(xp_ready, c + 1)
                if c == 0:
                    pe.wait_ge(lru_w_loaded, 16)
                if c >= 2:
                    pe.wait_ge(bd_drained, c - 1)
                mm(B[:, 2 * (c % 2), 0:T], bd[:, c, 0, :], xp[:, c, 0:T], start=True, stop=True)
                mm(B[:, 2 * (c % 2) + 1, 0:T], bd[:, c, 1, :], xp[:, c, 0:T], start=True,
                   stop=True).then_inc(bd_ready, 1)

            for c in range(KD):
                if c >= 3:
                    pe.wait_ge(copied, c - 2)
                chunk_piece(LRUX0 + c, 0, A[c % 3][:, 0:T], h_hi, h_lo, ops if c == 0 else 0)
                if c >= 1:
                    block_gates(c - 1)
            for n in range(3 * KSC):
                bank = [0, 1, 2, 3][n % 4]
                if n < 3:
                    pe.wait_ge(copied, KD)
                if n >= 4:
                    pe.wait_ge(staged, STAGED_SC + (n - 4) // 3 + 1)
                chunk_piece(SC0 + n, 0, A[bank][:, 0:T], h_hi, h_lo)
                if n == 0:
                    block_gates(KD - 1)
            for c in range(KD):
                if c < 4:
                    pe.wait_ge(staged, STAGED_LRU)
                else:
                    pe.wait_ge(gelu_ready, c - 3)
                chunk_piece(LRUG0 + c, 0, A[c % 4][:, 0:T], h_hi, h_lo)
            pe.wait_ge(bd_drained, KD)
            clear_accumulators()
            ops += KD
            for n in range(KSC * KD):
                p = OUT2 + n // 8
                m, k = n // KSC, n % KSC
                if n % 8 == 0:
                    pe.wait_ge(lo_ready, p + 1)
                if m == 0:
                    pe.wait_ge(operand_ready, ops + k + 1)
                ins = tile(p % RING, n % 8, sc_hi[:, k, :], sc_lo[:, k, :], acc_out(m), False, False, True)
                if n % 8 == 7:
                    ins.then_inc(pieces_done, 1)
            ops += KSC
            for m in range(KD):
                p = OUT2 + KSC + m
                pe.wait_ge(lo_ready, p + 1)
                for k in range(KD):
                    if m == 0:
                        pe.wait_ge(operand_ready, ops + k + 1)
                    ins = tile(p % RING, k, lru_hi[:, k, :], lru_lo[:, k, :], acc_out(m), False, False, True)
                ins.then_inc(pieces_done, 1)
            ops += KD
            channel_sums(A[3], sq_wide, 6 * KD)
            up_pair(UP2, 0, 0, first_operand=ops)
            up_pair(UP2, 1, 0)
            for j in range(2, 4):
                up_pair(UP2, j, 0, pairs_drained, KD + j - 1)
            with pe.Fori(1, UP2_TURNS) as i:
                for j in range(4):
                    up_pair(UP2, j, i, pairs_drained, i * 4 + (KD + j - 1))
            clear_accumulators()
            down_turns(DOWN2, KF2 // 8, ops + KD)
            channel_sums(A[3], sq_wide, 7 * KD)

        @block.scalar
        def _(act):
            F = nc.scalar.activation
            own = Count(act_steps)

            def split_hi(p, turn=0):
                if p >= PIECES:
                    return
                s = p % RING
                if p % 2 == 0:
                    act.wait_ge(loaded[s // 2], 16 * (p // RING + 1) + 16 * turn)
                if p >= RING:
                    act.wait_ge(pieces_done, p + 1 - RING + 8 * turn)
                F(w_hi[:, s, :], raw[:, s, :], ACT.Copy).then_inc(hi_ready, 1)

            def split_stage(n, dst, turn=0, per=0):
                act.wait_ge(staged, n + 1 + per * turn)
                F(dst, stage[:, n % 2, :], ACT.Copy).then_inc(stage_hi, 1)

            act.wait_ge(x_loaded, 16)
            for c in range(KD):
                F(acc[:, c, :], x[:, c, :], ACT.Square).then_inc(squares_ready, 1)
            for p in range(2):
                split_hi(p)
            for k in range(KD):
                act.wait_ge(staged, k + 1)
                F(h_hi[:, k, :], acc[:, k, :], ACT.Copy).then_inc(stage_hi, 1)
            for p in range(2, LEAD):
                split_hi(p)
            dtw = gates
            act.wait_ge(dt_abs, 1)
            n = own.up(F(dtw[0:HEADS, 4, :], dtw[0:HEADS, 3, :], ACT.Abs))
            act.wait_ge(act_steps, n)
            F(dtw[0:HEADS, 5, :], dtw[0:HEADS, 4, :], ACT.Exp, scale=-1.0).then_inc(dt_exp, 1)
            act.wait_ge(const_loaded, 48)
            F(dtw[0:HEADS, 6, 0:1], par[0:HEADS, AT["a_log"]:AT["a_log"] + 1], ACT.Exp).then_inc(dt_exp, 1)
            for c in range(KD):
                p = GLU0 + 2 * c
                split_hi(p + LEAD)
                act.wait_ge(pieces_done, p + 1)
                if c >= 2:
                    act.wait_ge(pairs_drained, c - 1)
                F(stage2[:, c % 2, :], A[2 * (c % 2)][:, 0:T], ACT.Sigmoid,
                  bias=col("glu_b", KD + c)).then_inc(gate_ready, 1)
                split_hi(p + 1 + LEAD)
                if c == 3:
                    act.wait_ge(cs_ready, 1)
                    act.dma_start(cs_dram, dtw[0:HEADS, 1, :]).then_inc(cs_stored, 16)
                    act.wait_ge(cs_stored, 16)

            def load_csrow(g, dynamic):
                src = cs_dram[bass.ds(g * HPG, HPG), :] if dynamic else cs_dram[g * HPG:(g + 1) * HPG, :]
                act.dma_start(csrow[:, :, :], src.partition_broadcast(P)).then_inc(csrow_loaded, 16)

            def drain_input(s, g, p, turn):
                act.wait_ge(pieces_done, p + 1 + 8 * turn)
                if s < 4:
                    F(ubuf[:, s, SSM_K - 1:], ring(s), ACT.Copy).then_inc(drained, 1)
                else:
                    F(zs[:, s - 4, :], ring(s), ACT.Silu).then_inc(drained, 1)

            def ring(o):
                return A[o % 3][:, 0:T]

            load_csrow(0, False)
            act.wait_ge(pad_ready, 4)
            for s in range(6):
                split_hi(SSM0 + s + LEAD)
                drain_input(s, 0, SSM0 + s, 0)

            def silu_inputs(g, js):
                for j in js:
                    act.wait_ge(conv_ready, 4 * g + j + 1)
                    F(gb[:, j, :], gb[:, j, :], ACT.Silu).then_inc(silu_ready, 1)

            def decay(g):
                act.wait_ge(seg_ready, g + 1)
                F(dec[:, :, :], dec[:, :, :], ACT.Exp).then_inc(dec_ready, 1)

            def y_squares(g):
                act.wait_ge(yz_ready, g + 1)
                F(dec[:, :, :].rearrange("p a b -> p (a b)")[:, 0:2 * T], y[:, :, :].rearrange("p a b -> p (a b)"),
                  ACT.Square).then_inc(ysq_ready, 1)

            def yn_high(g):
                act.wait_ge(yn32_ready, g + 1)
                F(yn_hi[:, :, :], y[:, :, :], ACT.Copy).then_inc(ynhi_ready, 1)

            with act.Fori(0, GROUPS - 1) as i:
                p = LOOP0
                silu_inputs(i, (0, 1))
                split_hi(p + LEAD, i)
                silu_inputs(i, (2, 3))
                drain_input(0, i, p, i)
                split_hi(p + 1 + LEAD, i)
                drain_input(1, i, p + 1, i)
                decay(i)
                load_csrow(i + 1, True)
                split_hi(p + 2 + LEAD, i)
                drain_input(2, i, p + 2, i)
                split_hi(p + 3 + LEAD, i)
                drain_input(3, i, p + 3, i)
                y_squares(i)
                split_hi(p + 4 + LEAD, i)
                drain_input(4, i, p + 4, i)
                split_hi(p + 5 + LEAD, i)
                yn_high(i)
                drain_input(5, i, p + 5, i)
                split_hi(p + 6 + LEAD, i)
                split_hi(p + 7 + LEAD, i)

            g = GROUPS - 1
            silu_inputs(g, (0, 1, 2, 3))
            for s in range(2 * KD):
                split_hi(GATES0 + s + LEAD)
                act.wait_ge(pieces_done, GATES0 + s + 1)
                F(gates[:, s, :], ring(s), ACT.Sigmoid, bias=col("gate_b", s)).then_inc(drained, 1)
                if s == 1:
                    decay(g)
                if s == 4:
                    y_squares(g)
                if s == 7:
                    yn_high(g)
                if s == 10:
                    act.wait_ge(centred, 1)
                    for c in range(KD):
                        F(v[:, c, 0:T], acc[:, c, :], ACT.Square).then_inc(squares_ready, 1)
            for c in range(KD):
                act.wait_ge(conv_norm, c + 1)
                if c >= 2:
                    act.wait_ge(operand_ready, KD + c - 1)
                n = own.up(F(stage[:, c % 2, :], acc[:, c, :], ACT.Silu, bias=col("conv_ln_b", c)))
                act.wait_ge(act_steps, n)
                F(conv_hi[:, c, :], stage[:, c % 2, :], ACT.Copy).then_inc(stage_hi, 1)
                if c == 3:
                    split_hi(TAIL0 + LEAD)
                if c == 7:
                    split_hi(TAIL0 + 1 + LEAD)
            staged_n = KD
            for m in range(KD):
                split_hi(PW0 + m + LEAD)
                split_stage(staged_n + m, h_hi[:, m, :])
            staged_n += KD

            def copy_and_square(src, dst_copy, dst_square):
                if dst_copy is not None:
                    F(dst_copy, src, ACT.Copy).then_inc(act_steps, 1)
                    own.n += 1
                F(dst_square, src, ACT.Square).then_inc(squares_ready, 1)

            for m in range(KD):
                split_hi(MIX0 + m + LEAD)
                act.wait_ge(pieces_done, MIX0 + m + 1)
                copy_and_square(A[(72 + m) % 3][:, 0:T], m_wide[:, m, :], sq_wide[:, m, 0:T])

            def residual_squares(n):
                for c in range(KD):
                    act.wait_ge(x_new, n + c + 1)
                    F(sq_wide[:, c, 0:T], x[:, c, :], ACT.Square).then_inc(squares_ready, 1)

            residual_squares(0)
            for k in range(KD):
                split_stage(staged_n + k, h_hi[:, k, :])
            staged_n += KD

            def ffn_pair(p, turn, n, dst, dyn):
                split_hi(p + LEAD, turn)
                act.wait_ge(pieces_done, p + 1 + 8 * turn)
                F(stage2[:, (p // 2) % 2, :], A[(p // 2) % 2 * 2][:, 0:T], ACT.Silu).then_inc(gate_ready, 1)
                split_hi(p + 1 + LEAD, turn)
                act.wait_ge(staged, n + 1)
                F(dst, stage[:, (p // 2) % 2, :], ACT.Copy).then_inc(stage_hi, 1)

            with act.Fori(0, UP1_TURNS) as i:
                for j in range(4):
                    ffn_pair(UP1 + 2 * j, i, i * 4 + (staged_n + j),
                             hid_hi[:, bass.ds(i * 4 + j, 1), :].rearrange("p a t -> p (a t)"), True)
            for j in range(4 * UP1_TURNS, KF):
                ffn_pair(UP1 + 2 * j, 0, staged_n + j, hid_hi[:, j, :], False)
            staged_n += KF
            for p in range(DOWN1, LRUX0):
                split_hi(p + LEAD)
            for m in range(KD):
                act.wait_ge(pieces_done, DOWN1 + 2 * KD + (DOWN1_REST * (m | 1) + DOWN1_REST - 1) // 8 + 1)
                copy_and_square(acc_out(m), m_wide[:, m, :], sq_wide[:, m, 0:T])
            act.dma_start(bd[:, :, :, :], lru_w).then_inc(lru_w_loaded, 16)
            n = own.up(F(sp[:, 0, :], col("lru_lambda_2", 0, KD), ACT.Abs))
            act.wait_ge(act_steps, n)
            F(sp[:, 1, :], sp[:, 0, :], ACT.Exp, scale=-1.0).then_inc(sp_exp, 1)
            residual_squares(KD)
            for k in range(KD):
                split_stage(staged_n + k, h_hi[:, k, :])
            staged_n += KD

            def lru_gates(c):
                act.wait_ge(bd_ready, c + 1)
                F(rg[:, c, :], B[:, 2 * (c % 2), 0:T], ACT.Sigmoid, bias=col("lru_ba_2", c)).then_inc(act_steps, 1)
                own.n += 1
                F(ig[:, c, :], B[:, 2 * (c % 2) + 1, 0:T], ACT.Sigmoid, bias=col("lru_bx_2", c)).then_inc(bd_drained, 1)

            for c in range(KD):
                split_hi(LRUX0 + c + LEAD)
                act.wait_ge(pieces_done, LRUX0 + c + 1)
                if c >= 2:
                    act.wait_ge(xp_ready, c - 1)
                F(u2[:, c % 2, LRU_K - 1:], A[c % 3][:, 0:T], ACT.Copy).then_inc(copied, 1)
                if c >= 1:
                    lru_gates(c - 1)
            for n in range(3 * KSC):
                split_hi(SC0 + n + LEAD)
                k, j = n // 3, n % 3
                if j == 0:
                    act.wait_ge(pieces_done, SC0 + n + 1)
                    if k >= 2:
                        act.wait_ge(staged, STAGED_SC + k - 1)
                    F(stage2[:, k % 2, :], A[n % 4][:, 0:T], ACT.Copy).then_inc(sc_copied, 1)
                if j == 2:
                    split_stage(staged_n + k, sc_hi[:, k, :])
                if n == 1:
                    lru_gates(KD - 1)
                if n == 4:
                    act.wait_ge(c_ready, 1)
                    act.wait_ge(bd_drained, KD)
                    for c in range(KD):
                        last = own.up(F(a_t[:, c, :], rg[:, c, :], ACT.Exp, scale=sp[:, 7, c:c + 1]))
                        F(th[:, c, :], rg[:, c, :], ACT.Tanh, scale=sp[:, 7, c:c + 1]).then_inc(act_steps, 1)
                        own.n += 1
                    act.wait_ge(act_steps, own.n)
                    F(rg[:, :, :], a_t[:, :, :], ACT.Square).then_inc(a_ready, 1)
                if n == 7:
                    act.wait_ge(m2_ready, 1)
                    F(th[:, :, :], th[:, :, :], ACT.Sqrt, scale=-1.0).then_inc(mult_ready, 1)
            staged_n += KSC
            for c in range(KD):
                split_hi(LRUG0 + c + LEAD)
                act.wait_ge(pieces_done, LRUG0 + c + 1)
                if c >= 2:
                    act.wait_ge(staged, staged_n + c - 1)
                F(stage2[:, c % 2, :], A[c % 4][:, 0:T], ACT.Gelu_apprx_tanh).then_inc(gelu_ready, 1)
                split_stage(staged_n + c, lru_hi[:, c, :])
            staged_n += KD
            for p in range(OUT2, UP2):
                split_hi(p + LEAD)
            residual_squares(2 * KD)
            for k in range(KD):
                split_stage(staged_n + k, h_hi[:, k, :])
            staged_n += KD

            def ffn2_pair(j, i):
                p = UP2 + 2 * j
                b = j % 2
                for half_, split in ((0, p), (1, p + 1)):
                    split_hi(split + LEAD, i)
                    act.wait_ge(pieces_done, split + 1 + 8 * i)
                    if half_ == 0:
                        act.wait_ge(staged, i * 4 + (staged_n + j - 1))
                    w2 = dcol("ffn_conv_w_2", (i * 4 + j) * (2 * FFN_K) + (half_ * FFN_K + 2))
                    F(tap[half_][:, b, :], A[2 * b + half_][:, 0:T], ACT.Identity, scale=w2).then_inc(tap_ready, 1)
                act.wait_ge(conv2_ready, i * 4 + (j + 1))
                F(tap[0][:, b, :], tap[0][:, b, :], ACT.Gelu_apprx_tanh).then_inc(gelu_ready, 1)
                act.wait_ge(staged, i * 4 + (staged_n + j + 1))
                F(hid_hi[:, bass.ds(i * 4 + j, 1), :].rearrange("p a t -> p (a t)"), stage[:, b, :],
                  ACT.Copy).then_inc(stage_hi, 1)

            tap = (stage2, stage3)
            with act.Fori(0, UP2_TURNS) as i:
                for j in range(4):
                    ffn2_pair(j, i)
            staged_n += KF2
            for p in range(DOWN2, PIECES):
                split_hi(p + LEAD)
            residual_squares(3 * KD)

        @block.vector
        def _(dve):
            V = nc.vector
            own = Count(dve_steps)

            def after(value):
                dve.wait_ge(dve_steps, value)

            def split_lo(p, turn=0):
                if p >= PIECES:
                    return
                s = p % RING
                dve.wait_ge(hi_ready, p + 1 + 8 * turn)
                V.tensor_tensor(w_lo[:, s, :], raw[:, s, :], w_hi[:, s, :].bitcast(F32), ALU.subtract).then_inc(lo_ready, 1)

            def operand_low(n, src, hi, lo):
                dve.wait_ge(stage_hi, n + 1)
                V.tensor_tensor(lo, src, hi.bitcast(F32), ALU.subtract).then_inc(operand_ready, 1)

            def mean_of(n, count, eps):
                dve.wait_ge(sums_ready, n)
                return V.tensor_scalar(mean[:, :], A[3][:, 0:T], 1.0 / count, eps, ALU.mult, ALU.add)

            def taps(c, name, ks, bias=None):
                dyn = not isinstance(c, int)

                def vs(k):
                    if dyn:
                        return v[:, bass.ds(c, 1), k:k + T].rearrange("p a t -> p (a t)")
                    return v[:, c, k:k + T]

                def w(k):
                    return dcol(name, c * CONV_K + k) if dyn else col(name, c * CONV_K + k)

                parts = (part_a, part_b)
                last = [None, None]
                for n, k in enumerate(ks):
                    dst = parts[n % 2]
                    if n < 2:
                        b = bias if n == 0 else None
                        ins = V.tensor_scalar(dst[:, :], vs(k), w(k), b, ALU.mult,
                                              ALU.add if b is not None else ALU.bypass)
                    else:
                        after(last[n % 2])
                        ins = V.scalar_tensor_tensor(dst[:, :], vs(k), w(k), dst[:, :], ALU.mult, ALU.add)
                    last[n % 2] = own.up(ins)
                after(last[(len(ks) - 1) % 2])
                return own.value()

            def add_parts(c, first=False):
                dyn = not isinstance(c, int)
                a = acc[:, bass.ds(c, 1), :].rearrange("p a t -> p (a t)") if dyn else acc[:, c, :]
                if first:
                    own.up(V.tensor_tensor(a, part_a[:, :], part_b[:, :], ALU.add))
                    return
                n = own.up(V.tensor_tensor(part_a[:, :], part_a[:, :], part_b[:, :], ALU.add))
                after(n)
                n = own.up(V.tensor_tensor(a, a, part_a[:, :], ALU.add))
                after(n)

            dve.wait_ge(x_loaded, 16)
            dve.wait_ge(const_loaded, 48)
            mean_of(1, D, RMS_EPS).then_inc(mean_ready, 1)
            dve.wait_ge(rstd_ready, 1)
            for k in range(KD):
                V.scalar_tensor_tensor(acc[:, k, :], x[:, k, :], col("mix_pre_g", k), rstd[:, :], ALU.mult,
                                       ALU.mult).then_inc(staged, 1)
            for k in range(KD):
                operand_low(k, acc[:, k, :], h_hi[:, k, :], h_lo[:, k, :])
            for p in range(LEAD):
                split_lo(p)

            def log1p_terms(e, t1, t2, t3, t4, dst):
                after(own.up(V.tensor_scalar(t1, e, 2.0, None, ALU.add)))
                after(own.up(V.reciprocal(t2, t1)))
                after(own.up(V.tensor_tensor(t3, e, t2, ALU.mult)))
                own.up(V.tensor_scalar(t1, t3, 2.0, None, ALU.mult))
                after(own.up(V.tensor_tensor(t4, t3, t3, ALU.mult)))
                after(own.up(V.tensor_scalar(t2, t4, 1.0 / 15, None, ALU.mult)))
                for d in (13, 11, 9, 7, 5, 3):
                    after(own.up(V.scalar_tensor_tensor(t2, t2, 1.0 / d, t4, ALU.add, ALU.mult)))
                after(own.up(V.scalar_tensor_tensor(dst, t2, 1.0, t1, ALU.add, ALU.mult)))

            dw = [gates[0:HEADS, j, :] for j in range(2 * KD)]
            dve.wait_ge(dt_raw_ready, 1)
            n = own.up(V.tensor_scalar(dw[3], A[2][0:HEADS, 0:T], par[0:HEADS, AT["dt_bias"]:AT["dt_bias"] + 1], None,
                                       ALU.add))
            after(n)
            V.tensor_copy(dw[7], dw[3]).then_inc(dt_abs, 1)
            own.up(V.memset(dw[8], 1.0))
            V.memset(dw[9], 0.0).then_inc(dt_raw_used, 1)
            dve.wait_ge(dt_exp, 1)
            log1p_terms(dw[5], dw[10], dw[11], dw[12], dw[13], dw[14])
            after(own.up(V.scalar_tensor_tensor(dw[0], dw[3], 0.0, dw[14], ALU.max, ALU.add)))
            dve.wait_ge(dt_exp, 2)
            after(own.up(V.tensor_scalar(dw[15], dw[0], dw[6][:, 0:1], -1.0, ALU.mult, ALU.mult)))
            for t in range(TT):
                own.up(V.tensor_tensor_scan(dw[1][:, t * P:(t + 1) * P], dw[8][:, 0:P], dw[15][:, t * P:(t + 1) * P],
                                            0.0, ALU.mult, ALU.add))
            after(own.value())
            V.tensor_scalar(dw[2][:, 0:P], dw[1][:, 0:P], dw[1][:, P - 1:P], -1.0, ALU.subtract,
                            ALU.mult).then_inc(cs_ready, 1)

            GLU_TAPS = tuple(range(11))
            LOOP_TAPS = tuple(range(11, 19))
            GATE_TAPS = tuple(range(19, CONV_K))
            dve.wait_ge(pad_ready, 4)
            for c in range(KD):
                p = GLU0 + 2 * c
                split_lo(p + LEAD)
                dve.wait_ge(pieces_done, p + 2)
                dve.wait_ge(gate_ready, c + 1)
                V.scalar_tensor_tensor(v[:, c, PAD:], A[2 * (c % 2) + 1][:, 0:T], col("glu_b", c), stage2[:, c % 2, :],
                                       ALU.add, ALU.mult).then_inc(pairs_drained, 1)
                split_lo(p + 1 + LEAD)
                dve.wait_ge(pairs_drained, c + 1)
                taps(c, "conv_dw_w", GLU_TAPS, col("conv_dw_b", c))
                add_parts(c, True)
                after(own.value())
            dve.wait_ge(tok_psum, 1)
            V.tensor_copy(tok[:, :, :], A[3][:, 0:5 * HEADS].rearrange("p (a b) -> p a b", a=5)).then_inc(tok_ready, 1)
            for s in range(6):
                split_lo(SSM0 + s + LEAD)

            def conv_inputs(g, js, drained_n):
                dyn = not isinstance(g, int)

                def w(j, k):
                    at = (g * 4 + j) * SSM_K + k
                    return dcol("ssm_conv_w", at) if dyn else col("ssm_conv_w", at)

                last = {}
                for k in range(SSM_K):
                    for j in js:
                        src = ubuf[:, j, k:k + T]
                        if k == 0:
                            dve.wait_ge(drained, drained_n + j + 1)
                            b = dcol("ssm_conv_b", g * 4 + j) if dyn else col("ssm_conv_b", g * 4 + j)
                            ins = V.tensor_scalar(gb[:, j, :], src, w(j, k), b, ALU.mult, ALU.add)
                        else:
                            after(last[j])
                            ins = V.scalar_tensor_tensor(gb[:, j, :], src, w(j, k), gb[:, j, :], ALU.mult, ALU.add)
                        if k < SSM_K - 1:
                            last[j] = own.up(ins)
                        else:
                            ins.then_inc(conv_ready, 1)

            def heads(k, g):
                t = tok[:, k, bass.ds(g * HPG, HPG)] if not isinstance(g, int) else tok[:, k, g * HPG:(g + 1) * HPG]
                return t.unsqueeze(2)

            def segments(g):
                dve.wait_ge(csrow_loaded, 16 * g + 16)
                if g is not None:
                    own.up(V.tensor_tensor(dec[:, :, 0:P], csrow[:, :, 0:P], heads(2, g).to_broadcast([P, HPG, P]),
                                           ALU.subtract))
                own.up(V.tensor_tensor(dec[:, :, P:2 * P], csrow[:, :, P:T], heads(4, g).to_broadcast([P, HPG, P]),
                                       ALU.add))
                n = own.up(V.tensor_tensor(dec[:, :, 2 * P:3 * P], csrow[:, :, P:T],
                                           heads(3, g).to_broadcast([P, HPG, P]), ALU.subtract))
                after(n)
                V.tensor_scalar(dec[:, :, :], dec[:, :, :], 0.0, None, ALU.min).then_inc(seg_ready, 1)

            def masked_scores(g):
                dve.wait_ge(cb_ready, g + 1)
                V.tensor_tensor(cbm[:, :], A[3][:, 0:3 * P], mask, ALU.mult).then_inc(cb_used, 1)

            def x_by_dt(g):
                dve.wait_ge(xt_ready, g + 1)
                for t in range(TT):
                    ins = V.tensor_tensor(xdt[:, t, :, :], A[3][:, t * T:(t + 1) * T].rearrange("p (a b) -> p a b", a=HPG),
                                          heads(t, g).to_broadcast([P, HPG, HD]), ALU.mult)
                    ins.then_inc(xdt_ready, 1)

            def decayed_scores(g):
                dve.wait_ge(dec_ready, g + 1)
                dve.wait_ge(cb_used, g + 1)
                V.tensor_tensor(dec[:, :, :], dec[:, :, :], cbm[:, :].unsqueeze(1).to_broadcast([P, HPG, 3 * P]),
                                ALU.mult).then_inc(m_ready, 1)

            def y_gated(g):
                dyn = not isinstance(g, int)
                dve.wait_ge(y_ready, g + 1)
                for c in range(2):
                    d = dcol("d_skip", g * 2 + c) if dyn else col("d_skip", g * 2 + c)
                    own.up(V.scalar_tensor_tensor(y[:, c, :], gb[:, 2 + c, :], d, A[3][:, c * T:(c + 1) * T],
                                                  ALU.mult, ALU.add))
                after(own.value())
                dve.wait_ge(drained, g * 6 + 6)
                V.tensor_tensor(y[:, :, :], y[:, :, :], zs[:, :, :], ALU.mult).then_inc(yz_ready, 1)

            def y_mean(g):
                mean_of(g + 2, 2 * P, RMS_EPS).then_inc(mean_ready, 1)

            def y_normed(g):
                dyn = not isinstance(g, int)
                dve.wait_ge(rstd_ready, g + 2)
                for c in range(2):
                    w = dcol("ssm_norm_g", g * 2 + c) if dyn else col("ssm_norm_g", g * 2 + c)
                    ins = V.scalar_tensor_tensor(y[:, c, :], y[:, c, :], w, rstd[:, :], ALU.mult, ALU.mult)
                    if c == 0:
                        own.up(ins)
                ins.then_inc(yn32_ready, 1)

            def y_low(g):
                dve.wait_ge(ynhi_ready, g + 1)
                for c in range(2):
                    V.tensor_tensor(yn_lo[:, c, :], y[:, c, :], yn_hi[:, c, :].bitcast(F32),
                                    ALU.subtract).then_inc(yn_ready, 1)

            loop_steps = 2 * 2 * (SSM_K - 1) + 3 + len(LOOP_TAPS) + 2 + 2 + 1
            with dve.Fori(0, GROUPS - 1) as i:
                own.enter(i, loop_steps)
                p = LOOP0
                conv_inputs(i, (0, 1), i * 6)
                split_lo(p + LEAD, i)
                conv_inputs(i, (2, 3), i * 6)
                segments(i)
                split_lo(p + 1 + LEAD, i)
                masked_scores(i)
                taps(i, "conv_dw_w", LOOP_TAPS)
                x_by_dt(i)
                decayed_scores(i)
                split_lo(p + 2 + LEAD, i)
                add_parts(i)
                split_lo(p + 3 + LEAD, i)
                y_gated(i)
                split_lo(p + 4 + LEAD, i)
                y_mean(i)
                split_lo(p + 5 + LEAD, i)
                y_normed(i)
                y_low(i)
                split_lo(p + 6 + LEAD, i)
                split_lo(p + 7 + LEAD, i)
                own.leave(GROUPS - 1)

            g = GROUPS - 1
            conv_inputs(g, (0, 1), 6 * g)
            conv_inputs(g, (2, 3), 6 * g)
            for s in range(2 * KD):
                split_lo(GATES0 + s + LEAD)
                if s == 0:
                    segments(g)
                    masked_scores(g)
                if s == 1:
                    x_by_dt(g)
                    decayed_scores(g)
                if s == 4:
                    y_gated(g)
                if s == 6:
                    y_mean(g)
                    y_normed(g)
                if s == 7:
                    y_low(g)
                if s < KD:
                    taps(s, "conv_dw_w", (LOOP_TAPS if s == g else ()) + GATE_TAPS)
                    add_parts(s)
                if s == KD - 1:
                    V.memset(part_a[:, :], 0.0).then_inc(conv_sum_ready, 1)
                if s == 10:
                    after(own.up(mean_of(10, D, 0.0)))
                    V.tensor_tensor(acc[:, :, :], acc[:, :, :], mean[:, :].unsqueeze(1).to_broadcast([P, KD, T]),
                                    ALU.subtract).then_inc(centred, 1)
                if s == 13:
                    mean_of(11, D, LN_EPS).then_inc(mean_ready, 1)
            dve.wait_ge(rstd_ready, 10)
            for c in range(KD):
                V.scalar_tensor_tensor(acc[:, c, :], acc[:, c, :], col("conv_ln_g", c), rstd[:, :], ALU.mult,
                                       ALU.mult).then_inc(conv_norm, 1)
            for c in range(KD):
                operand_low(KD + c, stage[:, c % 2, :], conv_hi[:, c, :], conv_lo[:, c, :])
            split_lo(TAIL0 + LEAD)
            split_lo(TAIL0 + 1 + LEAD)

            dve.wait_ge(pieces_done, PW0)
            staged_n = KD
            hi_n = 2 * KD
            for m in range(KD):
                split_lo(PW0 + m + LEAD)
                dve.wait_ge(pieces_done, PW0 + m + 1)
                n = own.up(V.tensor_tensor(stage2[:, 0, :], acc_out(m), gates[:, KD + m, :], ALU.mult))
                V.scalar_tensor_tensor(stage2[:, 1, :], A[(64 + m) % 3][:, 0:T], col("conv_pw_b", m), gates[:, m, :],
                                       ALU.add, ALU.mult).then_inc(mix_drained, 1)
                after(n)
                dve.wait_ge(mix_drained, m + 1)
                V.tensor_tensor(stage[:, m % 2, :], stage2[:, 0, :], stage2[:, 1, :], ALU.add).then_inc(staged, 1)
                operand_low(hi_n + m, stage[:, m % 2, :], h_hi[:, m, :], h_lo[:, m, :])
            staged_n += KD
            hi_n += KD
            for m in range(KD):
                split_lo(MIX0 + m + LEAD)

            def residual_norm(sums_n, norm_n, gain):
                mean_of(sums_n, D, RMS_EPS).then_inc(mean_ready, 1)
                dve.wait_ge(rstd_ready, norm_n)
                last = []
                for c in range(KD):
                    last.append(own.up(V.scalar_tensor_tensor(m_wide[:, c, :], m_wide[:, c, :], col(gain, c),
                                                              rstd[:, :], ALU.mult, ALU.mult)))
                for c in range(KD):
                    after(last[c])
                    V.tensor_tensor(x[:, c, :], x[:, c, :], m_wide[:, c, :], ALU.add).then_inc(x_new, 1)

            def normed_operand(sums_n, norm_n, gain, hi_n):
                mean_of(sums_n, D, RMS_EPS).then_inc(mean_ready, 1)
                dve.wait_ge(rstd_ready, norm_n)

                def low(k):
                    operand_low(hi_n + k, stage[:, k % 2, :], h_hi[:, k, :], h_lo[:, k, :])

                for k in range(KD):
                    if k >= 2:
                        dve.wait_ge(operand_ready, hi_n + k - 1)
                    V.scalar_tensor_tensor(stage[:, k % 2, :], x[:, k, :], col(gain, k), rstd[:, :], ALU.mult,
                                           ALU.mult).then_inc(staged, 1)
                    if k >= 1:
                        low(k - 1)
                low(KD - 1)

            dve.wait_ge(squares_ready, 3 * KD)
            residual_norm(12, 11, "mix_post_g")
            normed_operand(13, 12, "ffn_pre_g", hi_n)
            hi_n += KD
            staged_n += KD

            def ffn_pair(p, turn, pair, hi, lo):
                b = (p // 2) % 2
                split_lo(p + LEAD, turn)
                dve.wait_ge(pieces_done, p + 2 + 8 * turn)
                dve.wait_ge(gate_ready, pair + (KD + 1))
                V.tensor_tensor(stage[:, b, :], stage2[:, b, :], A[2 * b + 1][:, 0:T], ALU.mult).then_inc(staged, 1)
                split_lo(p + 1 + LEAD, turn)
                dve.wait_ge(stage_hi, pair + (hi_n + 1))
                V.tensor_tensor(lo, stage[:, b, :], hi.bitcast(F32), ALU.subtract).then_inc(operand_ready, 1)

            with dve.Fori(0, UP1_TURNS) as i:
                for j in range(4):
                    at = bass.ds(i * 4 + j, 1)
                    ffn_pair(UP1 + 2 * j, i, i * 4 + j, hid_hi[:, at, :].rearrange("p a t -> p (a t)"),
                             hid_lo[:, at, :].rearrange("p a t -> p (a t)"))
            for j in range(4 * UP1_TURNS, KF):
                ffn_pair(UP1 + 2 * j, 0, j, hid_hi[:, j, :], hid_lo[:, j, :])
            hi_n += KF
            staged_n += KF
            for p in range(DOWN1, LRUX0):
                split_lo(p + LEAD)
            dve.wait_ge(squares_ready, 5 * KD)
            residual_norm(14, 13, "ffn_post_g")

            dve.wait_ge(sp_exp, 1)
            log1p_terms(sp[:, 1, :], sp[:, 2, :], sp[:, 3, :], sp[:, 4, :], sp[:, 5, :], sp[:, 6, :])
            n = own.up(V.tensor_scalar(sp[:, 2, :], col("lru_lambda_2", 0, KD), -1.0, 0.0, ALU.mult, ALU.max))
            after(n)
            n = own.up(V.tensor_tensor(sp[:, 3, :], sp[:, 2, :], sp[:, 6, :], ALU.add))
            after(n)
            V.tensor_scalar(sp[:, 7, :], sp[:, 3, :], -RG_C, None, ALU.mult).then_inc(c_ready, 1)
            n = own.up(V.memset(u2[:, :, 0:LRU_K - 1], 0.0))
            after(n)
            normed_operand(15, 14, "norm1_g_2", hi_n)
            hi_n += KD
            staged_n += KD

            def lru_conv(c):
                dve.wait_ge(copied, c + 1)
                n = own.up(V.tensor_scalar(xp[:, c, 0:T], u2[:, c % 2, 0:T], col("lru_conv_w_2", c * LRU_K),
                                           col("lru_conv_b_2", c), ALU.mult, ALU.add))
                for k in range(1, LRU_K):
                    after(n)
                    ins = V.scalar_tensor_tensor(xp[:, c, 0:T], u2[:, c % 2, k:k + T], col("lru_conv_w_2", c * LRU_K + k),
                                                 xp[:, c, 0:T], ALU.mult, ALU.add)
                    if k < LRU_K - 1:
                        n = own.up(ins)
                    else:
                        ins.then_inc(xp_ready, 1)

            for c in range(KD):
                split_lo(LRUX0 + c + LEAD)
                lru_conv(c)
            prod = u2
            for n_ in range(3 * KSC):
                split_lo(SC0 + n_ + LEAD)
                k, j = n_ // 3, n_ % 3
                if j == 1:
                    dve.wait_ge(sc_copied, k + 1)
                    dve.wait_ge(pieces_done, SC0 + n_ + 1)
                    if k == 0:
                        dve.wait_ge(xp_ready, KD)
                    n = own.up(V.tensor_tensor(prod[:, 0, SC_K:SC_K + T], stage2[:, k % 2, :], A[n_ % 4][:, 0:T],
                                               ALU.mult))
                    after(n)
                    n = own.up(V.tensor_scalar(sc_sum[:, :], prod[:, 0, 1:1 + T], col("sc_conv_w_2", k * SC_K), None,
                                               ALU.mult))
                    for q in range(1, SC_K):
                        after(n)
                        n = own.up(V.scalar_tensor_tensor(sc_sum[:, :], prod[:, 0, 1 + q:1 + q + T],
                                                          col("sc_conv_w_2", k * SC_K + q), sc_sum[:, :], ALU.mult,
                                                          ALU.add))
                if j == 2:
                    dve.wait_ge(pieces_done, SC0 + n_ + 1)
                    after(n)
                    V.tensor_tensor(stage[:, (staged_n + k) % 2, :], sc_sum[:, :], A[n_ % 4][:, 0:T],
                                    ALU.mult).then_inc(staged, 1)
                    operand_low(hi_n + k, stage[:, (staged_n + k) % 2, :], sc_hi[:, k, :], sc_lo[:, k, :])
                if n_ == 6:
                    dve.wait_ge(a_ready, 1)
                    own.up(V.tensor_tensor(ig[:, :, :], ig[:, :, :], xp[:, :, 0:T], ALU.mult))
                    V.scalar_tensor_tensor(th[:, :, :], rg[:, :, :], 1.0, th[:, :, :], ALU.add,
                                           ALU.mult).then_inc(m2_ready, 1)
                if n_ == 9:
                    dve.wait_ge(mult_ready, 1)
                    after(own.up(V.tensor_tensor(ig[:, :, :], ig[:, :, :], th[:, :, :], ALU.mult)))
                    for c in range(KD):
                        last = own.up(V.tensor_tensor_scan(xp[:, c, 0:T], a_t[:, c, :], ig[:, c, :], 0.0, ALU.mult,
                                                           ALU.add))
                    lru_scanned = last
            hi_n += KSC
            staged_n += KSC
            after(lru_scanned)
            for c in range(KD):
                split_lo(LRUG0 + c + LEAD)
                dve.wait_ge(gelu_ready, c + 1)
                V.tensor_tensor(stage[:, (staged_n + c) % 2, :], xp[:, c, 0:T], stage2[:, c % 2, :],
                                ALU.mult).then_inc(staged, 1)
                operand_low(hi_n + c, stage[:, (staged_n + c) % 2, :], lru_hi[:, c, :], lru_lo[:, c, :])
            hi_n += KD
            staged_n += KD
            for p in range(OUT2, UP2):
                split_lo(p + LEAD)

            def add_accumulated(p_last):
                for m in range(KD):
                    dve.wait_ge(pieces_done, p_last + (m | 1) + 1)
                    V.tensor_tensor(x[:, m, :], x[:, m, :], acc_out(m), ALU.add).then_inc(x_new, 1)

            add_accumulated(OUT2 + KSC)
            normed_operand(16, 15, "norm2_g_2", hi_n)
            hi_n += KD
            staged_n += KD

            tap = (stage2, stage3)

            def ffn2_pair(j, i):
                p = UP2 + 2 * j
                b = j % 2
                split_lo(p + LEAD, i)
                last = {}
                for k in (1, 0):
                    for half_ in range(2):
                        if k == 1:
                            dve.wait_ge(tap_ready, i * 8 + (2 * j + half_ + 1))
                        else:
                            after(last[half_])
                        sh = FFN_K - 1 - k
                        w = dcol("ffn_conv_w_2", (i * 4 + j) * (2 * FFN_K) + (half_ * FFN_K + k))
                        ins = V.scalar_tensor_tensor(tap[half_][:, b, sh:], A[2 * b + half_][:, 0:T - sh], w,
                                                     tap[half_][:, b, sh:], ALU.mult, ALU.add)
                        if k == 1:
                            last[half_] = own.up(ins)
                        elif half_ == 0:
                            ins.then_inc(conv2_ready, 1)
                        else:
                            ins.then_inc(pairs_drained, 1)
                split_lo(p + 1 + LEAD, i)
                dve.wait_ge(gelu_ready, i * 4 + (KD + j + 1))
                dve.wait_ge(pairs_drained, i * 4 + (KD + j + 1))
                V.tensor_tensor(stage[:, b, :], tap[0][:, b, :], tap[1][:, b, :], ALU.mult).then_inc(staged, 1)
                dve.wait_ge(stage_hi, i * 4 + (hi_n + j + 1))
                at = bass.ds(i * 4 + j, 1)
                V.tensor_tensor(hid_lo[:, at, :].rearrange("p a t -> p (a t)"), stage[:, b, :],
                                hid_hi[:, at, :].rearrange("p a t -> p (a t)").bitcast(F32),
                                ALU.subtract).then_inc(operand_ready, 1)

            with dve.Fori(0, UP2_TURNS) as i:
                own.enter(i, 8)
                for j in range(4):
                    ffn2_pair(j, i)
                own.leave(UP2_TURNS)
            for p in range(DOWN2, PIECES):
                split_lo(p + LEAD)
            add_accumulated(DOWN2 + 2 * KD)
            mean_of(17, D, RMS_EPS).then_inc(mean_ready, 1)
            dve.wait_ge(rstd_ready, 16)
            dve.wait_ge(x_new, 4 * KD)
            for c in range(KD):
                V.scalar_tensor_tensor(m_wide[:, c, :], x[:, c, :], col("final_g_2", c), rstd[:, :], ALU.mult,
                                       ALU.mult).then_inc(out_ready, 1)


def _pieces(w):
    m = w.shape[1] // P
    return [w[:, c * P:(c + 1) * P].reshape(8, P, P).transpose(1, 0, 2).reshape(P, PIECE) for c in range(m)]


def _tiles(w, ks, by_row=False):
    order = [(k, m) for k in ks for m in range(8)] if by_row else [(k, m) for m in range(8) for k in ks]
    cut = [w[k * P:(k + 1) * P, m * P:(m + 1) * P] for k, m in order]
    return [np.concatenate(cut[i:i + 8], axis=1) for i in range(0, len(cut), 8)]


def pack_weights(a):
    w_in, w2 = a["w_in"][0], a["w_in_2"][0]
    w_ssm = a["ssm_out_w"][0]

    def chunk(w, at):
        return _pieces(w[:, at:at + P])

    def group(g):
        xbc = 2 * D + D_INNER
        s = chunk(w_in, xbc + D_INNER + g * P) + chunk(w_in, xbc + D_INNER + GROUPS * P + g * P)
        for base in (xbc, 2 * D):
            for c in range(2):
                s += chunk(w_in, base + (2 * g + c) * P)
        return s

    s = []
    for c in range(KD):
        s += chunk(w_in, D + c * P) + chunk(w_in, c * P)
    s += group(0)
    for i in range(GROUPS - 1):
        s += group(i + 1) + _tiles(w_ssm, (2 * i, 2 * i + 1), True)
    at = w_in.shape[1] - 2 * D
    s += _pieces(w_in[:, at:])
    s += _tiles(w_ssm, (2 * GROUPS - 2, 2 * GROUPS - 1), True)
    s += _pieces(a["conv_pw_w"][0]) + _pieces(a["w_out"][0])
    wu = a["w_gate_up"][0]
    for j in range(KF):
        s += chunk(wu, j * P) + chunk(wu, FFN + j * P)
    wd = a["w_down"][0]
    for t in range(KF // 8):
        s += _tiles(wd, range(8 * t, 8 * t + 8))
    s += _tiles(wd, range(8 * (KF // 8), KF))
    s += _pieces(w2[:, :D_LRU])
    for k in range(KSC):
        for part in (1, 2, 0):
            s += chunk(w2, 2 * D_LRU + part * D_SC + k * P)
    s += _pieces(w2[:, D_LRU:2 * D_LRU])
    wo = a["w_out_2"][0]
    s += _tiles(wo, range(KD, KD + KSC)) + _tiles(wo, range(KD))
    wu = a["w_up_2"][0]
    for j in range(KF2):
        s += chunk(wu, j * P) + chunk(wu, FFN2 + j * P)
    wd = a["w_down_2"][0]
    for t in range(KF2 // 8):
        s += _tiles(wd, range(8 * t, 8 * t + 8))
    assert len(s) == PIECES
    return np.stack(s).reshape(PIECES // 2, 2, P, PIECE).transpose(0, 2, 1, 3)


def pack_params(a):
    def cols(v):
        return v.reshape(-1, P).T

    def taps(w):
        return w.reshape(w.shape[0], -1, P).transpose(2, 1, 0).reshape(P, -1)

    def grouped(w):
        t = w.reshape(w.shape[0], -1, P)
        nx = D_INNER // P
        order = [c for g in range(GROUPS) for c in (nx + g, nx + GROUPS + g, 2 * g, 2 * g + 1)]
        return t[:, order].transpose(2, 1, 0).reshape(P, -1)

    def head_column(v):
        return np.concatenate([v, np.zeros(P - HEADS, v.dtype)]).reshape(P, 1)

    made = {
        "conv_dw_w": taps(a["conv_dw_w"][0]), "ssm_conv_w": grouped(a["ssm_conv_w"][0]),
        "ssm_conv_b": grouped(a["ssm_conv_b"]), "d_skip": cols(np.repeat(a["d_skip"][0], HD)),
        "lru_conv_w_2": taps(a["lru_conv_w_2"][0]), "sc_conv_w_2": taps(a["sc_conv_w_2"][0]),
        "dt_bias": head_column(a["dt_bias"][0]), "a_log": head_column(a["a_log"][0]),
        "ffn_conv_w_2": a["ffn_conv_w_2"][0].reshape(FFN_K, 2, KF2, P).transpose(3, 2, 1, 0).reshape(P, -1),
    }
    return np.concatenate([made[n] if n in made else cols(a[n]) for n, _ in PARAMS], axis=1)


def kernel(**inputs):
    import concourse.bacc as _bacc
    from concourse.bass_utils import run_bass_kernel_spmd as _run

    a = {k: np.asarray(v) for k, v in inputs.items()}
    at = 2 * D + D_INNER + 2 * D_INNER
    lru = np.zeros((P, KD, 2, P), np.float32)
    for j, name in enumerate(("lru_wa_2", "lru_wx_2")):
        for h in range(2 * KD):
            o = HD * (h % 2)
            lru[o:o + HD, h // 2, j, o:o + HD] = a[name][0, h]
    tri = np.triu(np.ones((P, P), np.float32))
    one = np.ones((P, P), np.float32)
    arrays = {
        "x": a["x"][0].T.reshape(KD, P, T).transpose(1, 0, 2),
        "weights": pack_weights(a),
        "params": pack_params(a),
        "w_dt": a["w_in"][0][:, at:at + HEADS].reshape(KD, P, HEADS).transpose(1, 0, 2),
        "lru_w": lru,
        "consts": np.concatenate([np.eye(P, dtype=np.float32), one, tri, one, tri], axis=1),
    }
    arrays = {f"in_{k}_dram": np.ascontiguousarray(v) for k, v in arrays.items()}
    nc = _bacc.Bacc("TRN2", target_bir_lowering=False, num_devices=1)
    args = [nc.dram_tensor(k, v.shape, mybir.dt.from_np(v.dtype), kind="ExternalInput").ap() for k, v in arrays.items()]
    args.append(nc.dram_tensor("out_0_dram", (P, KD, T), F32, kind="ExternalOutput").ap())
    hybrid_kernel(nc, *args)
    r = _run(nc, [arrays], core_ids=[0])
    got = r.results[0]["out_0_dram"]
    return np.ascontiguousarray(got.transpose(2, 1, 0).reshape(1, T, D))
```

```python
from contextlib import ExitStack

import numpy as np

import concourse.bass as bass
from concourse import mybir

F32 = mybir.dt.float32
F32R = mybir.dt.float32r
ALU = mybir.AluOpType
ACT = mybir.ActivationFunctionType

P = 128
T = 256
D = 1024
KD = D // P
TT = T // P
PIECE = 8 * P
RING = 8
LEAD = 6
PAIRS = RING // 2

CONV_K = 31
PAD = CONV_K - 1
GROUPS = 8
HEADS = 32
HPG = HEADS // GROUPS
HD = 64
D_INNER = 2 * D
SSM_K = 4
FFN = 2816
KF = FFN // P
D_LRU = 1024
D_SC = 512
KSC = D_SC // P
LRU_K = 4
SC_K = 3
FFN2 = 3 * D
KF2 = FFN2 // P
FFN_K = 3
RMS_EPS = 1e-6
LN_EPS = 1e-5
RG_C = 8.0

GLU0 = 0
SSM0 = GLU0 + 2 * KD
TURN0 = SSM0 + 6
LOOP0 = TURN0 + 6
GATES0 = LOOP0 + 8 * (GROUPS - 2)
TAIL0 = GATES0 + 2 * KD + 2
IN_AT, OUT_AT = (0, 1, 3, 4, 6, 7), (2, 5)
PW0 = TAIL0 + 2
MIX0 = PW0 + KD
UP1 = MIX0 + KD
DOWN1 = UP1 + 2 * KF
LRUX0 = DOWN1 + KF
SC0 = LRUX0 + KD
LRUG0 = SC0 + 3 * KSC
OUT2 = LRUG0 + KD
UP2 = OUT2 + KD + KSC
DOWN2 = UP2 + 2 * KF2
PIECES = DOWN2 + KF2
UP1_TURNS = 2 * KF // RING
UP2_TURNS = 2 * KF2 // RING
DOWN1_REST = KF - 2 * KD

PARAMS = [("mix_pre_g", KD), ("glu_b", 2 * KD), ("conv_dw_w", KD * CONV_K), ("conv_dw_b", KD),
          ("conv_ln_g", KD), ("conv_ln_b", KD), ("conv_pw_b", KD), ("ssm_conv_w", 32 * SSM_K),
          ("ssm_conv_b", 32), ("d_skip", 16), ("ssm_norm_g", 16), ("gate_b", 2 * KD), ("mix_post_g", KD),
          ("ffn_pre_g", KD), ("ffn_post_g", KD), ("norm1_g_2", KD), ("lru_conv_w_2", KD * LRU_K),
          ("lru_conv_b_2", KD), ("lru_ba_2", KD), ("lru_bx_2", KD), ("lru_lambda_2", KD),
          ("sc_conv_w_2", KSC * SC_K), ("norm2_g_2", KD), ("ffn_conv_w_2", 2 * KF2 * FFN_K),
          ("final_g_2", KD), ("dt_bias", 1), ("a_log", 1)]
AT = {}
NPAR = 0
for _name, _n in PARAMS:
    AT[_name] = NPAR
    NPAR += _n


STAGED_MIX = KD
STAGED_FFN1 = STAGED_MIX + 2 * KD
STAGED_SC = STAGED_FFN1 + KF + KD
STAGED_LRU = STAGED_SC + KSC


class Count:

    def __init__(self, sem):
        self.sem, self.n, self.turn = sem, 0, None

    def value(self):
        return self.n if self.turn is None else self.n + self.per * self.turn

    def up(self, instruction):
        instruction.then_inc(self.sem, 1)
        self.n += 1
        return self.value()

    def enter(self, turn, per):
        self.turn, self.per, self.start = turn, per, self.n

    def leave(self, turns):
        assert self.n - self.start == self.per, (self.n - self.start, self.per)
        self.n, self.turn = self.start + self.per * turns, None


def hybrid_kernel(nc, x_in, weights, params_in, w_dt, lru_w, consts, out):
    cs_dram = nc.dram_tensor("cs_dram", [HEADS + HPG, T], F32).ap()
    stack = ExitStack()
    with stack:
        def sb(name, shape, dt=F32, scope=stack):
            return scope.enter_context(nc.sbuf_tensor(name, shape, dt))

        def sem(name):
            return stack.enter_context(nc.semaphore(name))

        raw = sb("raw", [P, RING, PIECE])
        w_hi = sb("w_hi", [P, RING, PIECE], F32R)
        w_lo = sb("w_lo", [P, RING, PIECE], F32R)
        x = sb("x", [P, KD, T])
        h_hi = sb("h_hi", [P, KD, T], F32R)
        h_lo = sb("h_lo", [P, KD, T], F32R)
        par = sb("par", [P, NPAR])
        cst = sb("cst", [P, 5 * P])
        half = sb("half", [P, TT])
        zero = sb("zero", [P, P], F32R)
        mean = sb("mean", [P, T])
        moment = sb("moment", [P, TT])
        scale = sb("scale", [P, TT])
        stage = sb("stage", [P, 2, T])
        stage2 = sb("stage2", [P, 2, T])
        ident = cst[:, 0:P]
        ones = cst[:, P:2 * P]
        mask = cst[:, 2 * P:5 * P]

        s1 = ExitStack()
        v = sb("v", [P, KD, PAD + T], scope=s1)
        acc = sb("acc", [P, KD, T], scope=s1)
        s1.close()
        s2 = ExitStack()
        conv_hi = sb("conv_hi", [P, KD, T], F32R, s2)
        conv_lo_pad = sb("conv_lo_pad", [P, KD * PAD], scope=s2)
        conv_lo = sb("conv_lo", [P, KD, T], F32R, s2)
        s2.close()
        sq_wide = sb("sq_wide", [P, KD, PAD + T])
        m_wide = sb("m_wide", [P, KD, T])

        s3 = ExitStack()
        gates = sb("gates", [P, 2 * KD, T], scope=s3)
        ubuf = sb("ubuf", [P, 4, SSM_K - 1 + T], scope=s3)
        gb = sb("gb", [P, 4, T], scope=s3)
        zs = sb("zs", [P, 2, T], scope=s3)
        csrow = sb("csrow", [P, HPG, T], scope=s3)
        dec = sb("dec", [P, HPG, 3 * P], scope=s3)
        xdt = sb("xdt", [P, TT, HPG, HD], scope=s3)
        cbm = sb("cbm", [P, 3 * P], scope=s3)
        y = sb("y", [P, 2, T], scope=s3)
        ysq = sb("ysq", [P, 2, T], scope=s3)
        yn_hi = sb("yn_hi", [P, 2, T], F32R, s3)
        yn_lo = sb("yn_lo", [P, 2, T], F32R, s3)
        part = sb("part", [P, 2, T], scope=s3)
        wdt = sb("wdt", [P, KD, HEADS], scope=s3)
        tok = sb("tok", [P, 5, HEADS], scope=s3)
        s3.close()
        s4 = ExitStack()
        hid_hi = sb("hid_hi", [P, KF2, T], F32R, s4)
        hid_lo = sb("hid_lo", [P, KF2, T], F32R, s4)
        stage3 = sb("stage3", [P, 2, T], scope=s4)
        s4.close()
        s5 = ExitStack()
        ig = sb("ig", [P, KD, T], scope=s5)
        a_t = sb("a_t", [P, KD, T], scope=s5)
        th = sb("th", [P, KD, T], scope=s5)
        bd = sb("bd", [P, KD, 2, P], scope=s5)
        sc_hi = sb("sc_hi", [P, KSC, T], F32R, s5)
        sc_lo = sb("sc_lo", [P, KSC, T], F32R, s5)
        sc_sum = sb("sc_sum", [P, T], scope=s5)
        u2 = sb("u2", [P, 2, LRU_K - 1 + T], scope=s5)
        sp = sb("sp", [P, 8, KD], scope=s5)
        s5.close()
        s6 = ExitStack()
        lru_hi = sb("lru_hi", [P, KD, T], F32R, s6)
        lru_lo = sb("lru_lo", [P, KD, T], F32R, s6)
        s6.close()
        xp, rg = sq_wide, m_wide

        A = [stack.enter_context(nc.psum_tensor(f"A{i}", [P, 512], F32)) for i in range(4)]
        B = stack.enter_context(nc.psum_tensor("B", [P, 4, 512], F32))

        sums = A[3][:, 0:TT]
        rstd = A[3][:, T:2 * T]

        A_SUMS, B_SUMS = (A[0], A[1]), (B[:, 0, :], B[:, 1, :])

        def acc_out(m):
            return B[:, m // 2, (m % 2) * T:(m % 2 + 1) * T]

        loaded = [sem(f"loaded{i}") for i in range(PAIRS)]
        x_loaded, const_loaded = sem("x_loaded"), sem("const_loaded")
        hi_ready, lo_ready, pieces_done = sem("hi_ready"), sem("lo_ready"), sem("pieces_done")
        pad_ready = sem("pad_ready")
        squares_ready, sums_ready = sem("squares_ready"), sem("sums_ready")
        mean_ready, scale_ready, rstd_ready = sem("mean_ready"), sem("scale_ready"), sem("rstd_ready")
        staged, stage_hi, operand_ready = sem("staged"), sem("stage_hi"), sem("operand_ready")
        act_steps, dve_steps = sem("act_steps"), sem("dve_steps")
        dt_raw_ready, dt_raw_used, cs_ready, tok_psum, scale_read = (
            sem("dt_raw_ready"), sem("dt_raw_used"), sem("cs_ready"), sem("tok_psum"), sem("scale_read"))
        dt_abs, dt_exp = sem("dt_abs"), sem("dt_exp")
        cs_stored, csrow_loaded = sem("cs_stored"), sem("csrow_loaded")
        gate_ready, pairs_drained, drained = sem("gate_ready"), sem("pairs_drained"), sem("drained")
        conv_ready, silu_ready = sem("conv_ready"), sem("silu_ready")
        cb_ready, cb_used, xt_ready, xdt_ready = sem("cb_ready"), sem("cb_used"), sem("xt_ready"), sem("xdt_ready")
        seg_ready, dec_ready, m_ready, y_ready, yz_ready = (
            sem("seg_ready"), sem("dec_ready"), sem("m_ready"), sem("y_ready"), sem("yz_ready"))
        ysq_ready, ynhi_ready, yn_ready = (
            sem("ysq_ready"), sem("ynhi_ready"), sem("yn_ready"))
        conv_sum_ready, centred, conv_norm, mix_drained = (
            sem("conv_sum_ready"), sem("centred"), sem("conv_norm"), sem("mix_drained"))
        x_new, lru_w_loaded, c_ready, sp_exp = sem("x_new"), sem("lru_w_loaded"), sem("c_ready"), sem("sp_exp")
        copied, xp_ready, bd_ready, bd_drained, a_ready, m2_ready, mult_ready, gelu_ready = (
            sem("copied"), sem("xp_ready"), sem("bd_ready"), sem("bd_drained"), sem("a_ready"), sem("m2_ready"),
            sem("mult_ready"), sem("gelu_ready"))
        sc_copied, tap_ready, conv2_ready = sem("sc_copied"), sem("tap_ready"), sem("conv2_ready")
        out_ready, stored = sem("out_ready"), sem("stored")

        def col(name, c, n=1):
            return par[:, AT[name] + c:AT[name] + c + n]

        def dcol(name, c):
            return par[:, bass.ds(c + AT[name], 1)]

        block = stack.enter_context(nc.Block())

        @block.sync
        def _(sp_):
            sp_.dma_start(x[:, :, :], x_in).then_inc(x_loaded, 16)
            sp_.dma_start(par[:, :], params_in).then_inc(const_loaded, 16)
            sp_.dma_start(cst[:, :], consts).then_inc(const_loaded, 16)
            sp_.dma_start(wdt[:, :, :], w_dt).then_inc(const_loaded, 16)
            for q in range(PAIRS):
                sp_.dma_start(raw[:, 2 * q:2 * q + 2, :], weights[q]).then_inc(loaded[q], 16)
            rounds = PIECES // RING
            with sp_.Fori(1, rounds) as r:
                for q in range(PAIRS):
                    sp_.wait_ge(lo_ready, r * RING + (2 * q + 2 - RING))
                    sp_.dma_start(raw[:, 2 * q:2 * q + 2, :],
                                  weights[bass.ds(r * PAIRS + q, 1)].rearrange("a p s n -> p (a s) n")
                                  ).then_inc(loaded[q], 16)
            for q in range(rounds * PAIRS, PIECES // 2):
                s = q % PAIRS
                sp_.wait_ge(lo_ready, 2 * (q - PAIRS) + 2)
                sp_.dma_start(raw[:, 2 * s:2 * s + 2, :], weights[q]).then_inc(loaded[s], 16)
            for c in range(KD):
                sp_.wait_ge(out_ready, c + 1)
                sp_.dma_start(out[:, c, :], m_wide[:, c, :]).then_inc(stored, 16)
            sp_.wait_ge(stored, 16 * KD)

        @block.gpsimd
        def _(pool):
            nc.gpsimd.memset(half[:, :], -0.5).then_inc(pad_ready, 1)
            nc.gpsimd.memset(zero[:, :].bitcast(F32), 0.0).then_inc(pad_ready, 1)
            nc.gpsimd.memset(v[:, :, 0:PAD], 0.0).then_inc(pad_ready, 1)
            nc.gpsimd.memset(ubuf[:, :, 0:SSM_K - 1], 0.0).then_inc(pad_ready, 1)
            pool.wait_ge(pad_ready, 4)

            def rsqrt(n):
                pool.wait_ge(mean_ready, n)
                nc.gpsimd.tensor_tensor(scale[:, :], moment[:, :], half[:, :], ALU.pow).then_inc(scale_ready, 1)

            def split_lo(p, turn=0):
                s = p % RING
                pool.wait_ge(hi_ready, p + 1 + 8 * turn)
                nc.gpsimd.tensor_tensor(w_lo[:, s, :], raw[:, s, :], w_hi[:, s, :].bitcast(F32),
                                        ALU.subtract).then_inc(lo_ready, 1)

            rsqrt(1)
            pool.wait_ge(lo_ready, LEAD)
            for p in range(GLU0 + LEAD, TURN0 + LEAD):
                split_lo(p)
            for p in range(TURN0, LOOP0):
                split_lo(p + LEAD)
                if p == TURN0 + 4:
                    rsqrt(2)
            with pool.Fori(0, GROUPS - 2) as i:
                for n in range(8):
                    split_lo(LOOP0 + n + LEAD, i)
                    if n == 5:
                        rsqrt(i + 3)
            for p in range(GATES0, UP1):
                split_lo(p + LEAD)
                if p == GATES0 + 7:
                    rsqrt(GROUPS + 1)
                if p == GATES0 + 14:
                    rsqrt(10)
            for n in range(11, 15):
                rsqrt(n)
            pool.wait_ge(lo_ready, LRUX0 + LEAD)
            for p in range(LRUX0, OUT2):
                split_lo(p + LEAD)
            for n in range(15, 17):
                rsqrt(n)

        @block.tensor
        def _(pe):
            mm = nc.tensor.matmul

            def tile(slot, j, hi, lo, dst, first, last, free=False):
                wh = w_hi[:, slot, j * P:(j + 1) * P]
                wl = w_lo[:, slot, j * P:(j + 1) * P]
                mm(dst, wh, lo, start=first, stop=False, skip_group_check=free)
                mm(dst, wh, hi, start=False, stop=False, skip_group_check=free)
                return mm(dst, wl, hi, start=False, stop=last, skip_group_check=free)

            def chunk_piece(p, turn, dst, hi, lo, operand=0):
                pe.wait_ge(lo_ready, p + 1 + 8 * turn)
                for k in range(KD):
                    if operand:
                        pe.wait_ge(operand_ready, operand + k + 1)
                    ins = tile(p % RING, k, hi[:, k, :], lo[:, k, :], dst, k == 0, k == KD - 1)
                ins.then_inc(pieces_done, 1)

            def clear_accumulators():
                for b in range(4):
                    mm(B[:, b, :], zero[:, :], zero[:, :].unsqueeze(1).to_broadcast([P, 4, P]), start=True,
                       stop=False, skip_group_check=True)

            def square_sums(src, n0, banks=None):
                order = [(t, c) for c in range(KD) for t in range(TT)] if banks else \
                    [(t, c) for t in range(TT) for c in range(KD)]
                for t, c in order:
                    if t == 0:
                        pe.wait_ge(squares_ready, n0 + c + 1)
                    dst = banks[t][:, 0:1] if banks else sums[:, t:t + 1]
                    ins = mm(dst, src[:, c, t * P:(t + 1) * P], ones[:, 0:1], start=c == 0, stop=c == KD - 1)
                ins.then_inc(sums_ready, 1)

            def spread_scale(n):
                pe.wait_ge(scale_ready, n)
                for t in range(TT):
                    ins = mm(rstd[:, t * P:(t + 1) * P], scale[:, t:t + 1].to_broadcast([P, P]), ident, start=True,
                             stop=True)
                ins.then_inc(rstd_ready, 1)

            pe.wait_ge(const_loaded, 48)
            square_sums(acc, 0, A_SUMS)
            spread_scale(1)
            for k in range(KD):
                pe.wait_ge(operand_ready, k + 1)
                ins = mm(A[2][0:HEADS, 0:T], wdt[:, k, :], acc[:, k, :], start=k == 0, stop=k == KD - 1)
            ins.then_inc(dt_raw_ready, 1)
            pe.wait_ge(pad_ready, 4)
            clear_accumulators()
            for c in range(KD):
                for j in range(2):
                    if c >= 2:
                        pe.wait_ge(pairs_drained, c - 1)
                    elif c == 1:
                        pe.wait_ge(dt_raw_used, 1)
                    chunk_piece(GLU0 + 2 * c + j, 0, A[2 * (c % 2) + j][:, 0:T], h_hi, h_lo)
            pe.wait_ge(cs_ready, 1)
            pe.wait_ge(pairs_drained, KD)
            dtw = gates
            for n, src in enumerate([dtw[0:HEADS, 0, 0:P], dtw[0:HEADS, 0, P:T], dtw[0:HEADS, 1, 0:P],
                                     dtw[0:HEADS, 1, P:T], dtw[0:HEADS, 2, 0:P]]):
                ins = nc.tensor.transpose(A[3][:, n * HEADS:(n + 1) * HEADS], src, ident[0:HEADS, 0:HEADS])
            ins.then_inc(tok_psum, 1)

            def ring_bank(o):
                return A[o % 3][:, 0:T]

            def single(p, o, turn=0, g=0):
                if o >= 3:
                    pe.wait_ge(drained, o - 2 + 6 * g)
                chunk_piece(p, turn, ring_bank(o), h_hi, h_lo)

            for o in range(6):
                single(SSM0 + o, o)

            def cb(g):
                pe.wait_ge(silu_ready, 4 * g + 2)
                pe.wait_ge(scale_read, g + 1)
                mm(A[3][:, 0:T], gb[:, 0, 0:P], gb[:, 1, :], start=True, stop=True)
                mm(A[3][:, T:T + P], gb[:, 0, P:T], gb[:, 1, P:T], start=True, stop=True).then_inc(cb_ready, 1)

            def x_transposes(g):
                pe.wait_ge(silu_ready, 4 * g + 4)
                pe.wait_ge(cb_used, g + 1)
                for t in range(TT):
                    for c in range(2):
                        ins = nc.tensor.transpose(A[3][:, t * T + c * P:t * T + (c + 1) * P],
                                                  gb[:, 2 + c, t * P:(t + 1) * P], ident)
                ins.then_inc(xt_ready, 1)

            def y_products(g):
                pe.wait_ge(m_ready, g + 1)
                for r in range(HPG):
                    rows = slice(HD * (r % 2), HD * (r % 2) + HD)
                    at = (r // 2) * T
                    mm(A[3][rows, at:at + T], xdt[:, 0, r, :], dec[:, r, 0:T], start=True, stop=False)
                    ins = mm(A[3][rows, at + P:at + T], xdt[:, 1, r, :], dec[:, r, T:T + P], start=False, stop=True)
                ins.then_inc(y_ready, 1)

            def y_sums(g):
                pe.wait_ge(ysq_ready, g + 1)
                for t in range(TT):
                    for c in range(2):
                        ins = mm(sums[:, t:t + 1], ysq[:, c, t * P:(t + 1) * P], ones[:, 0:1],
                                 start=c == 0, stop=c == 1)
                ins.then_inc(sums_ready, 1)

            def y_scale(g):
                spread_scale(g + 2)

            def out_piece(p, turn, g, c):
                pe.wait_ge(lo_ready, p + 1 + 8 * turn)
                pe.wait_ge(yn_ready, 2 * g + c + 1)
                for m in range(KD):
                    ins = tile(p % RING, m, yn_hi[:, c, :], yn_lo[:, c, :], acc_out(m), False, False, True)
                ins.then_inc(pieces_done, 1)

            chain = {1: cb, 2: x_transposes, 3: y_products, 4: y_sums, 5: y_scale}

            def group_turn(g, base, t):
                for s in range(6):
                    single(base + IN_AT[s], 6 + s, t, g)
                    if s in (1, 3):
                        out_piece(base + OUT_AT[s // 2], t, g - 1, s // 2)
                    if s in chain:
                        chain[s](g)

            for s in range(6):
                single(TURN0 + s, 6 + s)
                if s in chain:
                    chain[s](0)
            with pe.Fori(0, GROUPS - 2) as i:
                group_turn(i + 1, LOOP0, i)
            g = GROUPS - 1
            for s in range(2 * KD):
                single(GATES0 + s + (s >= 2) + (s >= 4), 6 * GROUPS + s)
                if s in (1, 3):
                    out_piece(GATES0 + OUT_AT[s // 2], 0, g - 1, s // 2)
                if s in chain:
                    chain[s](g)
                if s == 8:
                    pe.wait_ge(scale_read, GROUPS + 1)
                    pe.wait_ge(conv_sum_ready, 1)
                    for c in range(KD):
                        ins = mm(A[3][:, 0:T], ones, acc[:, c, :], start=c == 0, stop=c == KD - 1)
                    ins.then_inc(sums_ready, 1)
                if s == 12:
                    square_sums(v, KD)
                if s == 2 * KD - 2:
                    spread_scale(10)
            out_piece(TAIL0, 0, g, 0)
            out_piece(TAIL0 + 1, 0, g, 1)
            for m in range(KD):
                if m < 3:
                    pe.wait_ge(drained, 6 * GROUPS + 2 * KD - 2 + m)
                else:
                    pe.wait_ge(mix_drained, m - 2)
                chunk_piece(PW0 + m, 0, ring_bank(64 + m), conv_hi, conv_lo, KD if m == 0 else 0)
            for m in range(KD):
                if m < 3:
                    pe.wait_ge(mix_drained, KD - 2 + m)
                else:
                    pe.wait_ge(squares_ready, 2 * KD + m - 2)
                chunk_piece(MIX0 + m, 0, ring_bank(72 + m), h_hi, h_lo, 2 * KD if m == 0 else 0)
            square_sums(sq_wide, 2 * KD, B_SUMS)
            spread_scale(11)
            square_sums(sq_wide, 3 * KD, B_SUMS)
            spread_scale(12)

            def up_pair(base, j, turn, read=None, n=None, first_operand=0):
                for half_ in range(2):
                    if n is not None:
                        pe.wait_ge(read, n)
                    chunk_piece(base + 2 * j + half_, turn, A[j % 2 * 2 + half_][:, 0:T], h_hi, h_lo,
                                first_operand if half_ == 0 else 0)

            up_pair(UP1, 0, 0, first_operand=3 * KD)
            up_pair(UP1, 1, 0)
            for j in range(2, 4):
                up_pair(UP1, j, 0, staged, STAGED_FFN1 + j - 1)
            with pe.Fori(1, UP1_TURNS) as i:
                for j in range(4):
                    up_pair(UP1, j, i, staged, i * 4 + (STAGED_FFN1 + j - 1))
            for j in range(UP1_TURNS * 4, KF):
                up_pair(UP1, j, 0, staged, STAGED_FFN1 + j - 1)

            def down_turns(p, turns, operand):
                with pe.Fori(0, turns) as i:
                    for m in range(KD):
                        pe.wait_ge(lo_ready, p + m + 1 + 8 * i)
                        if m == 0:
                            pe.wait_ge(operand_ready, i * 8 + (operand + 8))
                        for k in range(8):
                            ins = tile((p + m) % RING, k, hid_hi[:, bass.ds(i * 8 + k, 1), :].rearrange("p a t -> p (a t)"),
                                       hid_lo[:, bass.ds(i * 8 + k, 1), :].rearrange("p a t -> p (a t)"),
                                       acc_out(m), False, False, True)
                        ins.then_inc(pieces_done, 1)

            clear_accumulators()
            done1 = 4 * KD
            down_turns(DOWN1, 2, done1)
            for n in range(DOWN1_REST * KD):
                p = DOWN1 + 2 * KD + n // 8
                m, k = n // DOWN1_REST, n % DOWN1_REST
                if n % 8 == 0:
                    pe.wait_ge(lo_ready, p + 1)
                if m == 0:
                    pe.wait_ge(operand_ready, done1 + 2 * KD + k + 1)
                ins = tile(p % RING, n % 8, hid_hi[:, 2 * KD + k, :], hid_lo[:, 2 * KD + k, :], acc_out(m),
                           False, False, True)
                if n % 8 == 7:
                    ins.then_inc(pieces_done, 1)
            square_sums(sq_wide, 4 * KD, A_SUMS)
            spread_scale(13)
            square_sums(sq_wide, 5 * KD, A_SUMS)
            spread_scale(14)

            ops = done1 + KF

            def block_gates(c):
                pe.wait_ge(xp_ready, c + 1)
                if c == 0:
                    pe.wait_ge(lru_w_loaded, 16)
                if c >= 2:
                    pe.wait_ge(bd_drained, c - 1)
                mm(B[:, 2 * (c % 2), 0:T], bd[:, c, 0, :], xp[:, c, 0:T], start=True, stop=True)
                mm(B[:, 2 * (c % 2) + 1, 0:T], bd[:, c, 1, :], xp[:, c, 0:T], start=True,
                   stop=True).then_inc(bd_ready, 1)

            for c in range(KD):
                if c >= 3:
                    pe.wait_ge(copied, c - 2)
                chunk_piece(LRUX0 + c, 0, A[c % 3][:, 0:T], h_hi, h_lo, ops if c == 0 else 0)
                if c >= 1:
                    block_gates(c - 1)
            for n in range(3 * KSC):
                bank = [0, 1, 2, 3][n % 4]
                if n < 3:
                    pe.wait_ge(copied, KD)
                if n >= 4:
                    pe.wait_ge(staged, STAGED_SC + (n - 4) // 3 + 1)
                chunk_piece(SC0 + n, 0, A[bank][:, 0:T], h_hi, h_lo)
                if n == 0:
                    block_gates(KD - 1)
            for c in range(KD):
                if c < 4:
                    pe.wait_ge(staged, STAGED_LRU)
                else:
                    pe.wait_ge(gelu_ready, c - 3)
                chunk_piece(LRUG0 + c, 0, A[c % 4][:, 0:T], h_hi, h_lo)
            pe.wait_ge(bd_drained, KD)
            clear_accumulators()
            ops += KD
            for n in range(KSC * KD):
                p = OUT2 + n // 8
                m, k = n // KSC, n % KSC
                if n % 8 == 0:
                    pe.wait_ge(lo_ready, p + 1)
                if m == 0:
                    pe.wait_ge(operand_ready, ops + k + 1)
                ins = tile(p % RING, n % 8, sc_hi[:, k, :], sc_lo[:, k, :], acc_out(m), False, False, True)
                if n % 8 == 7:
                    ins.then_inc(pieces_done, 1)
            ops += KSC
            for m in range(KD):
                p = OUT2 + KSC + m
                pe.wait_ge(lo_ready, p + 1)
                for k in range(KD):
                    if m == 0:
                        pe.wait_ge(operand_ready, ops + k + 1)
                    ins = tile(p % RING, k, lru_hi[:, k, :], lru_lo[:, k, :], acc_out(m), False, False, True)
                ins.then_inc(pieces_done, 1)
            ops += KD
            square_sums(sq_wide, 6 * KD, A_SUMS)
            spread_scale(15)
            up_pair(UP2, 0, 0, first_operand=ops)
            up_pair(UP2, 1, 0)
            for j in range(2, 4):
                up_pair(UP2, j, 0, pairs_drained, KD + j - 1)
            with pe.Fori(1, UP2_TURNS) as i:
                for j in range(4):
                    up_pair(UP2, j, i, pairs_drained, i * 4 + (KD + j - 1))
            clear_accumulators()
            down_turns(DOWN2, KF2 // 8, ops + KD)
            square_sums(sq_wide, 7 * KD, A_SUMS)
            spread_scale(16)

        @block.scalar
        def _(act):
            F = nc.scalar.activation
            own = Count(act_steps)

            def split_hi(p, turn=0):
                if p >= PIECES:
                    return
                s = p % RING
                if p % 2 == 0:
                    act.wait_ge(loaded[s // 2], 16 * (p // RING + 1) + 16 * turn)
                if p >= RING:
                    act.wait_ge(pieces_done, p + 1 - RING + 8 * turn)
                F(w_hi[:, s, :], raw[:, s, :], ACT.Copy).then_inc(hi_ready, 1)

            def split_stage(n, dst, turn=0, per=0):
                act.wait_ge(staged, n + 1 + per * turn)
                F(dst, stage[:, n % 2, :], ACT.Copy).then_inc(stage_hi, 1)

            act.wait_ge(x_loaded, 16)
            for c in range(KD):
                F(acc[:, c, :], x[:, c, :], ACT.Square).then_inc(squares_ready, 1)
            for p in range(2):
                split_hi(p)
            for k in range(KD):
                act.wait_ge(staged, k + 1)
                F(h_hi[:, k, :], acc[:, k, :], ACT.Copy).then_inc(stage_hi, 1)
            for p in range(2, LEAD):
                split_hi(p)
            dtw = gates
            act.wait_ge(dt_abs, 1)
            n = own.up(F(dtw[0:HEADS, 4, :], dtw[0:HEADS, 3, :], ACT.Abs))
            act.wait_ge(act_steps, n)
            F(dtw[0:HEADS, 5, :], dtw[0:HEADS, 4, :], ACT.Exp, scale=-1.0).then_inc(dt_exp, 1)
            act.wait_ge(const_loaded, 48)
            F(dtw[0:HEADS, 6, 0:1], par[0:HEADS, AT["a_log"]:AT["a_log"] + 1], ACT.Exp).then_inc(dt_exp, 1)
            for c in range(KD):
                p = GLU0 + 2 * c
                split_hi(p + LEAD)
                act.wait_ge(pieces_done, p + 1)
                if c >= 2:
                    act.wait_ge(pairs_drained, c - 1)
                F(stage2[:, c % 2, :], A[2 * (c % 2)][:, 0:T], ACT.Sigmoid,
                  bias=col("glu_b", KD + c)).then_inc(gate_ready, 1)
                split_hi(p + 1 + LEAD)
                if c == 3:
                    act.wait_ge(cs_ready, 1)
                    act.dma_start(cs_dram[0:HEADS, :], dtw[0:HEADS, 1, :]).then_inc(cs_stored, 16)
                    act.dma_start(cs_dram[HEADS:, :], dtw[0:HPG, 1, :]).then_inc(cs_stored, 16)
                    act.wait_ge(cs_stored, 32)

            def load_csrow(g):
                at = slice(g * HPG, (g + 1) * HPG) if isinstance(g, int) else bass.ds(g * HPG, HPG)
                src = cs_dram[at, :]
                act.dma_start(csrow[:, :, :], src.partition_broadcast(P)).then_inc(csrow_loaded, 16)

            def drain_input(s, g, p, turn):
                act.wait_ge(pieces_done, p + 1 + 8 * turn)
                if s < 4:
                    F(ubuf[:, s, SSM_K - 1:], ring(s), ACT.Copy).then_inc(drained, 1)
                else:
                    F(zs[:, s - 4, :], ring(s), ACT.Silu).then_inc(drained, 1)

            def ring(o):
                return A[o % 3][:, 0:T]

            load_csrow(0)
            act.wait_ge(pad_ready, 4)
            for s in range(6):
                split_hi(SSM0 + s + LEAD)
                drain_input(s, 0, SSM0 + s, 0)

            def silu_bc(g):
                for j in (0, 1):
                    act.wait_ge(conv_ready, 4 * g + (j + 1))
                    F(gb[:, j, :], gb[:, j, :], ACT.Silu).then_inc(silu_ready, 1)

            def silu_x(g):
                for j in (2, 3):
                    act.wait_ge(conv_ready, 4 * g + (j + 1))
                    F(gb[:, j, :], gb[:, j, :], ACT.Silu).then_inc(silu_ready, 1)

            def exponents(g):
                act.wait_ge(csrow_loaded, 16 * g + 16)
                for b, (k, cols) in enumerate(((2, slice(0, P)), (4, slice(P, T)), (3, slice(P, T)))):
                    for r_ in range(HPG):
                        h = g * HPG + r_
                        cs = tok[:, k, h:h + 1] if isinstance(g, int) else tok[:, k, bass.ds(h, 1)]
                        n = own.up(F(dec[:, r_, b * P:(b + 1) * P], csrow[:, r_, cols], ACT.Relu, bias=cs, scale=-1.0))
                act.wait_ge(act_steps, n)
                load_csrow(g + 1)

            def decays(g):
                F(dec[:, :, :], dec[:, :, :], ACT.Exp, scale=-1.0).then_inc(dec_ready, 1)

            def y_squares(g):
                act.wait_ge(yz_ready, g + 1)
                F(ysq[:, :, :], y[:, :, :], ACT.Square).then_inc(ysq_ready, 1)

            def yn_high(g):
                act.wait_ge(scale_read, g + 2)
                F(yn_hi[:, :, :], y[:, :, :], ACT.Copy).then_inc(ynhi_ready, 1)

            act.wait_ge(scale_read, 1)
            exponents(0)

            def group_turn(g, base, t, at, count):
                left = list(range(count))

                def split():
                    if left:
                        split_hi(base + left.pop(0) + LEAD, t)

                silu_bc(g)
                split()
                drain_input(0, g, base + at[0], t)
                silu_x(g)
                split()
                drain_input(1, g, base + at[1], t)
                decays(g)
                split()
                if count == 8:
                    split()
                drain_input(2, g, base + at[2], t)
                split()
                drain_input(3, g, base + at[3], t)
                split()
                if count == 8:
                    split()
                y_squares(g)
                drain_input(4, g, base + at[4], t)
                exponents(g + 1)
                split()
                yn_high(g)
                drain_input(5, g, base + at[5], t)
                while left:
                    split()

            group_turn(0, TURN0, 0, range(6), 6)
            with act.Fori(0, GROUPS - 2) as i:
                own.enter(i, 3 * HPG)
                group_turn(i + 1, LOOP0, i, IN_AT, 8)
                own.leave(GROUPS - 2)

            g = GROUPS - 1
            act.wait_ge(csrow_loaded, 16 * (GROUPS + 1))
            silu_bc(g)
            silu_x(g)
            decays(g)
            for s in range(2 * KD):
                p = GATES0 + s + (s >= 2) + (s >= 4)
                split_hi(p + LEAD)
                act.wait_ge(pieces_done, p + 1)
                F(gates[:, s, :], ring(s), ACT.Sigmoid, bias=col("gate_b", s)).then_inc(drained, 1)
                if s in (1, 3):
                    split_hi(p + 1 + LEAD)
                if s == 4:
                    y_squares(g)
                if s == 7:
                    yn_high(g)
                if s == 10:
                    for c in range(KD):
                        act.wait_ge(centred, c + 1)
                        F(v[:, c, 0:T], acc[:, c, :], ACT.Square).then_inc(squares_ready, 1)
            for c in range(KD):
                act.wait_ge(conv_norm, c + 1)
                if c >= 2:
                    act.wait_ge(operand_ready, KD + c - 1)
                n = own.up(F(stage[:, c % 2, :], acc[:, c, :], ACT.Silu, bias=col("conv_ln_b", c)))
                act.wait_ge(act_steps, n)
                F(conv_hi[:, c, :], stage[:, c % 2, :], ACT.Copy).then_inc(stage_hi, 1)
                if c == 3:
                    split_hi(TAIL0 + LEAD)
                if c == 7:
                    split_hi(TAIL0 + 1 + LEAD)
            staged_n = KD
            for m in range(KD):
                split_hi(PW0 + m + LEAD)
                split_stage(staged_n + m, h_hi[:, m, :])
            staged_n += KD

            def copy_and_square(src, dst_copy, dst_square):
                if dst_copy is not None:
                    F(dst_copy, src, ACT.Copy).then_inc(act_steps, 1)
                    own.n += 1
                F(dst_square, src, ACT.Square).then_inc(squares_ready, 1)

            for m in range(KD):
                split_hi(MIX0 + m + LEAD)
                act.wait_ge(pieces_done, MIX0 + m + 1)
                copy_and_square(A[(72 + m) % 3][:, 0:T], m_wide[:, m, :], sq_wide[:, m, 0:T])

            def residual_squares(n):
                for c in range(KD):
                    act.wait_ge(x_new, n + c + 1)
                    F(sq_wide[:, c, 0:T], x[:, c, :], ACT.Square).then_inc(squares_ready, 1)

            residual_squares(0)
            for k in range(KD):
                split_stage(staged_n + k, h_hi[:, k, :])
            staged_n += KD

            def ffn_pair(p, turn, n, dst, dyn):
                split_hi(p + LEAD, turn)
                act.wait_ge(pieces_done, p + 1 + 8 * turn)
                F(stage2[:, (p // 2) % 2, :], A[(p // 2) % 2 * 2][:, 0:T], ACT.Silu).then_inc(gate_ready, 1)
                split_hi(p + 1 + LEAD, turn)
                act.wait_ge(staged, n + 1)
                F(dst, stage[:, (p // 2) % 2, :], ACT.Copy).then_inc(stage_hi, 1)

            with act.Fori(0, UP1_TURNS) as i:
                for j in range(4):
                    ffn_pair(UP1 + 2 * j, i, i * 4 + (staged_n + j),
                             hid_hi[:, bass.ds(i * 4 + j, 1), :].rearrange("p a t -> p (a t)"), True)
            for j in range(4 * UP1_TURNS, KF):
                ffn_pair(UP1 + 2 * j, 0, staged_n + j, hid_hi[:, j, :], False)
            staged_n += KF
            for p in range(DOWN1, LRUX0):
                split_hi(p + LEAD)
            for m in range(KD):
                act.wait_ge(pieces_done, DOWN1 + 2 * KD + (DOWN1_REST * (m | 1) + DOWN1_REST - 1) // 8 + 1)
                copy_and_square(acc_out(m), m_wide[:, m, :], sq_wide[:, m, 0:T])
            act.dma_start(bd[:, :, :, :], lru_w).then_inc(lru_w_loaded, 16)
            n = own.up(F(sp[:, 0, :], col("lru_lambda_2", 0, KD), ACT.Abs))
            act.wait_ge(act_steps, n)
            F(sp[:, 1, :], sp[:, 0, :], ACT.Exp, scale=-1.0).then_inc(sp_exp, 1)
            residual_squares(KD)
            for k in range(KD):
                split_stage(staged_n + k, h_hi[:, k, :])
            staged_n += KD

            def lru_gates(c):
                act.wait_ge(bd_ready, c + 1)
                F(rg[:, c, :], B[:, 2 * (c % 2), 0:T], ACT.Sigmoid, bias=col("lru_ba_2", c)).then_inc(act_steps, 1)
                own.n += 1
                F(ig[:, c, :], B[:, 2 * (c % 2) + 1, 0:T], ACT.Sigmoid, bias=col("lru_bx_2", c)).then_inc(bd_drained, 1)

            for c in range(KD):
                split_hi(LRUX0 + c + LEAD)
                act.wait_ge(pieces_done, LRUX0 + c + 1)
                if c >= 2:
                    act.wait_ge(xp_ready, c - 1)
                F(u2[:, c % 2, LRU_K - 1:], A[c % 3][:, 0:T], ACT.Copy).then_inc(copied, 1)
                if c >= 1:
                    lru_gates(c - 1)
            for n in range(3 * KSC):
                split_hi(SC0 + n + LEAD)
                k, j = n // 3, n % 3
                if j == 0:
                    act.wait_ge(pieces_done, SC0 + n + 1)
                    if k >= 2:
                        act.wait_ge(staged, STAGED_SC + k - 1)
                    F(stage2[:, k % 2, :], A[n % 4][:, 0:T], ACT.Copy).then_inc(sc_copied, 1)
                if j == 2:
                    split_stage(staged_n + k, sc_hi[:, k, :])
                if n == 1:
                    lru_gates(KD - 1)
                if 2 <= n < 6:
                    act.wait_ge(c_ready, 1)
                    act.wait_ge(bd_drained, KD)
                    for c in range(2 * n - 4, 2 * n - 2):
                        last = own.up(F(a_t[:, c, :], rg[:, c, :], ACT.Exp, scale=sp[:, 7, c:c + 1]))
                        F(th[:, c, :], rg[:, c, :], ACT.Tanh, scale=sp[:, 7, c:c + 1]).then_inc(act_steps, 1)
                        own.n += 1
                if n == 5:
                    act.wait_ge(act_steps, own.n)
                    F(rg[:, :, :], a_t[:, :, :], ACT.Square).then_inc(a_ready, 1)
                if n == 7:
                    act.wait_ge(m2_ready, 1)
                    F(th[:, :, :], th[:, :, :], ACT.Sqrt, scale=-1.0).then_inc(mult_ready, 1)
            staged_n += KSC
            for c in range(KD):
                split_hi(LRUG0 + c + LEAD)
                act.wait_ge(pieces_done, LRUG0 + c + 1)
                if c >= 2:
                    act.wait_ge(staged, staged_n + c - 1)
                F(stage2[:, c % 2, :], A[c % 4][:, 0:T], ACT.Gelu_apprx_tanh).then_inc(gelu_ready, 1)
                split_stage(staged_n + c, lru_hi[:, c, :])
            staged_n += KD
            for p in range(OUT2, UP2):
                split_hi(p + LEAD)
            residual_squares(2 * KD)
            for k in range(KD):
                split_stage(staged_n + k, h_hi[:, k, :])
            staged_n += KD

            def hid2_high(n, b):
                act.wait_ge(staged, n + (staged_n + 1))
                at = slice(n, n + 1) if isinstance(n, int) else bass.ds(n, 1)
                F(hid_hi[:, at, :].rearrange("p a t -> p (a t)"), stage[:, b, :], ACT.Copy).then_inc(stage_hi, 1)

            def gelu2(n, b):
                act.wait_ge(conv2_ready, n + 1)
                F(tap[0][:, b, :], tap[0][:, b, :], ACT.Gelu_apprx_tanh).then_inc(gelu_ready, 1)

            def ffn2_pair(j, i, first=False):
                p = UP2 + 2 * j
                b = j % 2
                n = i * 4 + j
                for half_ in range(2):
                    act.wait_ge(pieces_done, p + half_ + 1 + 8 * i)
                    if half_ == 0:
                        act.wait_ge(staged, n + (staged_n - 1))
                    at = n * (2 * FFN_K) + (half_ * FFN_K + 2)
                    w2 = col("ffn_conv_w_2", at) if isinstance(n, int) else dcol("ffn_conv_w_2", at)
                    F(tap[half_][:, b, :], A[2 * b + half_][:, 0:T], ACT.Identity, scale=w2).then_inc(tap_ready, 1)
                    if half_ == 0 and not first:
                        gelu2(n - 1, 1 - b)
                    if half_ == 1 and not first:
                        hid2_high(n - 1, 1 - b)
                    split_hi(p + half_ + LEAD, i)

            tap = (stage2, stage3)
            for j in range(4):
                ffn2_pair(j, 0, j == 0)
            with act.Fori(1, UP2_TURNS) as i:
                for j in range(4):
                    ffn2_pair(j, i)
            gelu2(KF2 - 1, 1)
            hid2_high(KF2 - 1, 1)
            staged_n += KF2
            for p in range(DOWN2, PIECES):
                split_hi(p + LEAD)
            residual_squares(3 * KD)

        @block.vector
        def _(dve):
            V = nc.vector
            own = Count(dve_steps)

            def after(value):
                dve.wait_ge(dve_steps, value)

            def split_lo(p, turn=0):
                if p >= PIECES:
                    return
                s = p % RING
                dve.wait_ge(hi_ready, p + 1 + 8 * turn)
                V.tensor_tensor(w_lo[:, s, :], raw[:, s, :], w_hi[:, s, :].bitcast(F32), ALU.subtract).then_inc(lo_ready, 1)

            def operand_low(n, src, hi, lo):
                dve.wait_ge(stage_hi, n + 1)
                V.tensor_tensor(lo, src, hi.bitcast(F32), ALU.subtract).then_inc(operand_ready, 1)

            def mean_of(n, count, eps, banks=None):
                dve.wait_ge(sums_ready, n)
                if banks:
                    V.tensor_scalar(moment[:, 0:1], banks[0][:, 0:1], 1.0 / count, eps, ALU.mult, ALU.add)
                    return V.tensor_scalar(moment[:, 1:2], banks[1][:, 0:1], 1.0 / count, eps, ALU.mult, ALU.add)
                return V.tensor_scalar(moment[:, :], sums, 1.0 / count, eps, ALU.mult, ALU.add)

            def taps(c, ks, bias=None, fresh=True):
                dyn = not isinstance(c, int)

                def vs(k):
                    if dyn:
                        return v[:, bass.ds(c, 1), k:k + T].rearrange("p a t -> p (a t)")
                    return v[:, c, k:k + T]

                def w(k):
                    return dcol("conv_dw_w", c * CONV_K + k) if dyn else col("conv_dw_w", c * CONV_K + k)

                parts = (part[:, 0], part[:, 1])
                last = [None, None] if fresh else [own.value()] * 2
                for n, k in enumerate(ks):
                    dst = parts[n % 2]
                    if n < 2 and fresh:
                        b = bias if n == 0 else None
                        ins = V.tensor_scalar(dst, vs(k), w(k), b, ALU.mult,
                                              ALU.add if b is not None else ALU.bypass)
                    else:
                        after(last[n % 2])
                        ins = V.scalar_tensor_tensor(dst, vs(k), w(k), dst, ALU.mult, ALU.add)
                    last[n % 2] = own.up(ins)
                after(last[(len(ks) - 1) % 2])
                return own.value()

            def more_taps(c, ks):
                taps(c, ks, fresh=False)

            def add_parts(c, first=False):
                dyn = not isinstance(c, int)
                a = acc[:, bass.ds(c, 1), :].rearrange("p a t -> p (a t)") if dyn else acc[:, c, :]
                if first:
                    own.up(V.tensor_tensor(a, part[:, 0], part[:, 1], ALU.add))
                    return
                n = own.up(V.tensor_tensor(part[:, 0], part[:, 0], part[:, 1], ALU.add))
                after(n)
                n = own.up(V.tensor_tensor(a, a, part[:, 0], ALU.add))
                after(n)

            dve.wait_ge(x_loaded, 16)
            dve.wait_ge(const_loaded, 48)
            mean_of(1, D, RMS_EPS, A_SUMS).then_inc(mean_ready, 1)
            dve.wait_ge(rstd_ready, 1)
            for k in range(KD):
                V.scalar_tensor_tensor(acc[:, k, :], x[:, k, :], col("mix_pre_g", k), rstd, ALU.mult,
                                       ALU.mult).then_inc(staged, 1)
            for k in range(KD):
                operand_low(k, acc[:, k, :], h_hi[:, k, :], h_lo[:, k, :])
            for p in range(LEAD):
                split_lo(p)

            def log1p_terms(e, t1, t2, t3, t4, dst):
                after(own.up(V.tensor_scalar(t1, e, 2.0, None, ALU.add)))
                after(own.up(V.reciprocal(t2, t1)))
                after(own.up(V.tensor_tensor(t3, e, t2, ALU.mult)))
                own.up(V.tensor_scalar(t1, t3, 2.0, None, ALU.mult))
                after(own.up(V.tensor_tensor(t4, t3, t3, ALU.mult)))
                after(own.up(V.tensor_scalar(t2, t4, 1.0 / 15, None, ALU.mult)))
                for d in (13, 11, 9, 7, 5, 3):
                    after(own.up(V.scalar_tensor_tensor(t2, t2, 1.0 / d, t4, ALU.add, ALU.mult)))
                after(own.up(V.scalar_tensor_tensor(dst, t2, 1.0, t1, ALU.add, ALU.mult)))

            dw = [gates[0:HEADS, j, :] for j in range(2 * KD)]
            dve.wait_ge(dt_raw_ready, 1)
            n = own.up(V.tensor_scalar(dw[3], A[2][0:HEADS, 0:T], par[0:HEADS, AT["dt_bias"]:AT["dt_bias"] + 1], None,
                                       ALU.add))
            after(n)
            V.tensor_copy(dw[7], dw[3]).then_inc(dt_abs, 1)
            own.up(V.memset(dw[8], 1.0))
            V.memset(dw[9], 0.0).then_inc(dt_raw_used, 1)
            dve.wait_ge(dt_exp, 1)
            log1p_terms(dw[5], dw[10], dw[11], dw[12], dw[13], dw[14])
            after(own.up(V.scalar_tensor_tensor(dw[0], dw[3], 0.0, dw[14], ALU.max, ALU.add)))
            dve.wait_ge(dt_exp, 2)
            after(own.up(V.tensor_scalar(dw[15], dw[0], dw[6][:, 0:1], -1.0, ALU.mult, ALU.mult)))
            for t in range(TT):
                own.up(V.tensor_tensor_scan(dw[1][:, t * P:(t + 1) * P], dw[8][:, 0:P], dw[15][:, t * P:(t + 1) * P],
                                            0.0, ALU.mult, ALU.add))
            after(own.value())
            V.tensor_scalar(dw[2][:, 0:P], dw[1][:, 0:P], dw[1][:, P - 1:P], None,
                            ALU.subtract).then_inc(cs_ready, 1)

            GLU_TAPS, LOOP_TAPS = tuple(range(11)), tuple(range(11, CONV_K))
            dve.wait_ge(pad_ready, 4)
            for c in range(KD):
                p = GLU0 + 2 * c
                dve.wait_ge(pieces_done, p + 2)
                dve.wait_ge(gate_ready, c + 1)
                V.scalar_tensor_tensor(v[:, c, PAD:], A[2 * (c % 2) + 1][:, 0:T], col("glu_b", c), stage2[:, c % 2, :],
                                       ALU.add, ALU.mult).then_inc(pairs_drained, 1)
                dve.wait_ge(pairs_drained, c + 1)
                taps(c, GLU_TAPS, col("conv_dw_b", c))
                add_parts(c, True)
            dve.wait_ge(tok_psum, 1)
            V.tensor_copy(tok[:, :, :], A[3][:, 0:5 * HEADS].rearrange("p (a b) -> p a b", a=5)).then_inc(scale_read, 1)

            def conv_inputs(g, js, drained_n):
                dyn = not isinstance(g, int)

                def w(j, k):
                    at = (g * 4 + j) * SSM_K + k
                    return dcol("ssm_conv_w", at) if dyn else col("ssm_conv_w", at)

                last = {}
                for k in range(SSM_K):
                    for j in js:
                        src = ubuf[:, j, k:k + T]
                        if k == 0:
                            dve.wait_ge(drained, drained_n + j + 1)
                            b = dcol("ssm_conv_b", g * 4 + j) if dyn else col("ssm_conv_b", g * 4 + j)
                            ins = V.tensor_scalar(gb[:, j, :], src, w(j, k), b, ALU.mult, ALU.add)
                        else:
                            after(last[j])
                            ins = V.scalar_tensor_tensor(gb[:, j, :], src, w(j, k), gb[:, j, :], ALU.mult, ALU.add)
                        if k < SSM_K - 1:
                            last[j] = own.up(ins)
                        else:
                            ins.then_inc(conv_ready, 1)

            def heads(k, g):
                t = tok[:, k, bass.ds(g * HPG, HPG)] if not isinstance(g, int) else tok[:, k, g * HPG:(g + 1) * HPG]
                return t.unsqueeze(2)

            def masked_scores(g):
                dve.wait_ge(cb_ready, g + 1)
                V.tensor_tensor(cbm[:, :], A[3][:, 0:3 * P], mask, ALU.mult).then_inc(cb_used, 1)

            def x_by_dt(g):
                dve.wait_ge(xt_ready, g + 1)
                for t in range(TT):
                    ins = V.tensor_tensor(xdt[:, t, :, :], A[3][:, t * T:(t + 1) * T].rearrange("p (a b) -> p a b", a=HPG),
                                          heads(t, g).to_broadcast([P, HPG, HD]), ALU.mult)
                    ins.then_inc(xdt_ready, 1)

            def decayed_scores(g):
                dve.wait_ge(dec_ready, g + 1)
                dve.wait_ge(cb_used, g + 1)
                V.tensor_tensor(dec[:, :, :], dec[:, :, :], cbm[:, :].unsqueeze(1).to_broadcast([P, HPG, 3 * P]),
                                ALU.mult).then_inc(m_ready, 1)

            def y_gated(g):
                dyn = not isinstance(g, int)
                dve.wait_ge(y_ready, g + 1)
                for c in range(2):
                    d = dcol("d_skip", g * 2 + c) if dyn else col("d_skip", g * 2 + c)
                    own.up(V.scalar_tensor_tensor(y[:, c, :], gb[:, 2 + c, :], d, A[3][:, c * T:(c + 1) * T],
                                                  ALU.mult, ALU.add))
                after(own.value())
                dve.wait_ge(drained, g * 6 + 6)
                V.tensor_tensor(y[:, :, :], y[:, :, :], zs[:, :, :], ALU.mult).then_inc(yz_ready, 1)

            def y_mean(g):
                mean_of(g + 2, 2 * P, RMS_EPS).then_inc(mean_ready, 1)

            def y_normed(g):
                dyn = not isinstance(g, int)
                dve.wait_ge(rstd_ready, g + 2)
                for c in range(2):
                    w = dcol("ssm_norm_g", g * 2 + c) if dyn else col("ssm_norm_g", g * 2 + c)
                    ins = V.scalar_tensor_tensor(y[:, c, :], y[:, c, :], w, rstd, ALU.mult, ALU.mult)
                    if c == 0:
                        own.up(ins)
                ins.then_inc(scale_read, 1)

            def y_low(g):
                dve.wait_ge(ynhi_ready, g + 1)
                for c in range(2):
                    V.tensor_tensor(yn_lo[:, c, :], y[:, c, :], yn_hi[:, c, :].bitcast(F32),
                                    ALU.subtract).then_inc(yn_ready, 1)

            def group_turn(g, first=False):
                conv_inputs(g, (0, 1), g * 6)
                if not first:
                    y_low(g - 1)
                conv_inputs(g, (2, 3), g * 6)
                masked_scores(g)
                taps(g, LOOP_TAPS[:6])
                x_by_dt(g)
                decayed_scores(g)
                more_taps(g, LOOP_TAPS[6:12])
                y_gated(g)
                more_taps(g, LOOP_TAPS[12:16])
                y_mean(g)
                more_taps(g, LOOP_TAPS[16:])
                add_parts(g)
                y_normed(g)

            group_turn(0, True)
            with dve.Fori(0, GROUPS - 2) as i:
                own.enter(i, 4 * (SSM_K - 1) + len(LOOP_TAPS) + 2 + 2 + 1)
                group_turn(i + 1)
                own.leave(GROUPS - 2)

            g = GROUPS - 1
            group_turn(g)
            y_low(g)
            V.memset(part[:, 0], 0.0).then_inc(conv_sum_ready, 1)
            dve.wait_ge(sums_ready, 10)
            after(own.up(V.tensor_scalar(mean[:, :], A[3][:, 0:T], 1.0 / D, None, ALU.mult)))
            for c in range(KD):
                V.tensor_tensor(acc[:, c, :], acc[:, c, :], mean[:, :], ALU.subtract).then_inc(centred, 1)
            mean_of(11, D, LN_EPS).then_inc(mean_ready, 1)
            dve.wait_ge(rstd_ready, 10)
            for c in range(KD):
                V.scalar_tensor_tensor(acc[:, c, :], acc[:, c, :], col("conv_ln_g", c), rstd, ALU.mult,
                                       ALU.mult).then_inc(conv_norm, 1)
            for c in range(KD):
                operand_low(KD + c, stage[:, c % 2, :], conv_hi[:, c, :], conv_lo[:, c, :])

            dve.wait_ge(pieces_done, PW0)
            staged_n = KD
            hi_n = 2 * KD
            for m in range(KD):
                dve.wait_ge(pieces_done, PW0 + m + 1)
                n = own.up(V.tensor_tensor(stage2[:, 0, :], acc_out(m), gates[:, KD + m, :], ALU.mult))
                V.scalar_tensor_tensor(stage2[:, 1, :], A[(64 + m) % 3][:, 0:T], col("conv_pw_b", m), gates[:, m, :],
                                       ALU.add, ALU.mult).then_inc(mix_drained, 1)
                after(n)
                dve.wait_ge(mix_drained, m + 1)
                V.tensor_tensor(stage[:, m % 2, :], stage2[:, 0, :], stage2[:, 1, :], ALU.add).then_inc(staged, 1)
                operand_low(hi_n + m, stage[:, m % 2, :], h_hi[:, m, :], h_lo[:, m, :])
            staged_n += KD
            hi_n += KD

            def residual_norm(sums_n, norm_n, gain):
                mean_of(sums_n, D, RMS_EPS, B_SUMS if sums_n < 14 else A_SUMS).then_inc(mean_ready, 1)
                dve.wait_ge(rstd_ready, norm_n)
                last = []
                for c in range(KD + 1):
                    if c < KD:
                        last.append(own.up(V.scalar_tensor_tensor(m_wide[:, c, :], m_wide[:, c, :], col(gain, c),
                                                                  rstd, ALU.mult, ALU.mult)))
                    if c:
                        after(last[c - 1])
                        V.tensor_tensor(x[:, c - 1, :], x[:, c - 1, :], m_wide[:, c - 1, :],
                                        ALU.add).then_inc(x_new, 1)

            def normed_operand(sums_n, norm_n, gain, hi_n):
                mean_of(sums_n, D, RMS_EPS, B_SUMS if sums_n < 14 else A_SUMS).then_inc(mean_ready, 1)
                dve.wait_ge(rstd_ready, norm_n)

                def low(k):
                    operand_low(hi_n + k, stage[:, k % 2, :], h_hi[:, k, :], h_lo[:, k, :])

                for k in range(KD):
                    if k >= 2:
                        dve.wait_ge(operand_ready, hi_n + k - 1)
                    V.scalar_tensor_tensor(stage[:, k % 2, :], x[:, k, :], col(gain, k), rstd, ALU.mult,
                                           ALU.mult).then_inc(staged, 1)
                    if k >= 1:
                        low(k - 1)
                low(KD - 1)

            dve.wait_ge(squares_ready, 3 * KD)
            residual_norm(12, 11, "mix_post_g")
            normed_operand(13, 12, "ffn_pre_g", hi_n)
            hi_n += KD
            staged_n += KD

            dve.wait_ge(lo_ready, UP1 + LEAD)

            def ffn_pair(p, turn, pair, hi, lo):
                b = (p // 2) % 2
                split_lo(p + LEAD, turn)
                dve.wait_ge(pieces_done, p + 2 + 8 * turn)
                dve.wait_ge(gate_ready, pair + (KD + 1))
                V.tensor_tensor(stage[:, b, :], stage2[:, b, :], A[2 * b + 1][:, 0:T], ALU.mult).then_inc(staged, 1)
                split_lo(p + 1 + LEAD, turn)
                dve.wait_ge(stage_hi, pair + (hi_n + 1))
                V.tensor_tensor(lo, stage[:, b, :], hi.bitcast(F32), ALU.subtract).then_inc(operand_ready, 1)

            with dve.Fori(0, UP1_TURNS) as i:
                for j in range(4):
                    at = bass.ds(i * 4 + j, 1)
                    ffn_pair(UP1 + 2 * j, i, i * 4 + j, hid_hi[:, at, :].rearrange("p a t -> p (a t)"),
                             hid_lo[:, at, :].rearrange("p a t -> p (a t)"))
            for j in range(4 * UP1_TURNS, KF):
                ffn_pair(UP1 + 2 * j, 0, j, hid_hi[:, j, :], hid_lo[:, j, :])
            hi_n += KF
            staged_n += KF
            for p in range(DOWN1, LRUX0):
                split_lo(p + LEAD)
            dve.wait_ge(squares_ready, 5 * KD)
            residual_norm(14, 13, "ffn_post_g")

            dve.wait_ge(sp_exp, 1)
            log1p_terms(sp[:, 1, :], sp[:, 2, :], sp[:, 3, :], sp[:, 4, :], sp[:, 5, :], sp[:, 6, :])
            n = own.up(V.tensor_scalar(sp[:, 2, :], col("lru_lambda_2", 0, KD), -1.0, 0.0, ALU.mult, ALU.max))
            after(n)
            n = own.up(V.tensor_tensor(sp[:, 3, :], sp[:, 2, :], sp[:, 6, :], ALU.add))
            after(n)
            V.tensor_scalar(sp[:, 7, :], sp[:, 3, :], -RG_C, None, ALU.mult).then_inc(c_ready, 1)
            n = own.up(V.memset(u2[:, :, 0:LRU_K - 1], 0.0))
            after(n)
            normed_operand(15, 14, "norm1_g_2", hi_n)
            hi_n += KD
            staged_n += KD

            def lru_conv(c):
                dve.wait_ge(copied, c + 1)
                n = own.up(V.tensor_scalar(xp[:, c, 0:T], u2[:, c % 2, 0:T], col("lru_conv_w_2", c * LRU_K),
                                           col("lru_conv_b_2", c), ALU.mult, ALU.add))
                for k in range(1, LRU_K):
                    after(n)
                    ins = V.scalar_tensor_tensor(xp[:, c, 0:T], u2[:, c % 2, k:k + T], col("lru_conv_w_2", c * LRU_K + k),
                                                 xp[:, c, 0:T], ALU.mult, ALU.add)
                    if k < LRU_K - 1:
                        n = own.up(ins)
                    else:
                        ins.then_inc(xp_ready, 1)

            for c in range(KD):
                lru_conv(c)
            prod = u2
            for n_ in range(3 * KSC):
                k, j = n_ // 3, n_ % 3
                if j == 1:
                    dve.wait_ge(sc_copied, k + 1)
                    dve.wait_ge(pieces_done, SC0 + n_ + 1)
                    if k == 0:
                        dve.wait_ge(xp_ready, KD)
                    n = own.up(V.tensor_tensor(prod[:, 0, SC_K:SC_K + T], stage2[:, k % 2, :], A[n_ % 4][:, 0:T],
                                               ALU.mult))
                    after(n)
                    n = own.up(V.tensor_scalar(sc_sum[:, :], prod[:, 0, 1:1 + T], col("sc_conv_w_2", k * SC_K), None,
                                               ALU.mult))
                    for q in range(1, SC_K):
                        after(n)
                        n = own.up(V.scalar_tensor_tensor(sc_sum[:, :], prod[:, 0, 1 + q:1 + q + T],
                                                          col("sc_conv_w_2", k * SC_K + q), sc_sum[:, :], ALU.mult,
                                                          ALU.add))
                if j == 2:
                    dve.wait_ge(pieces_done, SC0 + n_ + 1)
                    after(n)
                    V.tensor_tensor(stage[:, (staged_n + k) % 2, :], sc_sum[:, :], A[n_ % 4][:, 0:T],
                                    ALU.mult).then_inc(staged, 1)
                    operand_low(hi_n + k, stage[:, (staged_n + k) % 2, :], sc_hi[:, k, :], sc_lo[:, k, :])
                if n_ == 3:
                    dve.wait_ge(bd_drained, KD)
                    own.up(V.tensor_tensor(ig[:, :, :], ig[:, :, :], xp[:, :, 0:T], ALU.mult))
                if n_ == 6:
                    dve.wait_ge(a_ready, 1)
                    V.scalar_tensor_tensor(th[:, :, :], rg[:, :, :], 1.0, th[:, :, :], ALU.add,
                                           ALU.mult).then_inc(m2_ready, 1)
                if n_ == 9:
                    dve.wait_ge(mult_ready, 1)
                    after(own.up(V.tensor_tensor(ig[:, :, :], ig[:, :, :], th[:, :, :], ALU.mult)))
                    for c in range(KD):
                        last = own.up(V.tensor_tensor_scan(xp[:, c, 0:T], a_t[:, c, :], ig[:, c, :], 0.0, ALU.mult,
                                                           ALU.add))
                    lru_scanned = last
            hi_n += KSC
            staged_n += KSC
            after(lru_scanned)
            for c in range(KD):
                dve.wait_ge(gelu_ready, c + 1)
                V.tensor_tensor(stage[:, (staged_n + c) % 2, :], xp[:, c, 0:T], stage2[:, c % 2, :],
                                ALU.mult).then_inc(staged, 1)
                operand_low(hi_n + c, stage[:, (staged_n + c) % 2, :], lru_hi[:, c, :], lru_lo[:, c, :])
            hi_n += KD
            staged_n += KD
            dve.wait_ge(lo_ready, OUT2 + LEAD)
            for p in range(OUT2, UP2):
                split_lo(p + LEAD)

            def add_accumulated(p_last):
                for m in range(KD):
                    dve.wait_ge(pieces_done, p_last + (m | 1) + 1)
                    V.tensor_tensor(x[:, m, :], x[:, m, :], acc_out(m), ALU.add).then_inc(x_new, 1)

            add_accumulated(OUT2 + KSC)
            normed_operand(16, 15, "norm2_g_2", hi_n)
            hi_n += KD
            staged_n += KD

            tap = (stage2, stage3)

            def hid2_product(n, b):
                dve.wait_ge(gelu_ready, n + (KD + 1))
                dve.wait_ge(pairs_drained, n + (KD + 1))
                V.tensor_tensor(stage[:, b, :], tap[0][:, b, :], tap[1][:, b, :], ALU.mult).then_inc(staged, 1)

            def hid2_low(n, b):
                dve.wait_ge(stage_hi, n + (hi_n + 1))
                at = slice(n, n + 1) if isinstance(n, int) else bass.ds(n, 1)
                V.tensor_tensor(hid_lo[:, at, :].rearrange("p a t -> p (a t)"), stage[:, b, :],
                                hid_hi[:, at, :].rearrange("p a t -> p (a t)").bitcast(F32),
                                ALU.subtract).then_inc(operand_ready, 1)

            def ffn2_pair(j, i, first=False):
                p = UP2 + 2 * j
                b = j % 2
                n = i * 4 + j
                last = {}
                for k, half_ in ((1, 0), (1, 1), (0, 0), (0, 1)):
                    if k == 1:
                        dve.wait_ge(tap_ready, n * 2 + (half_ + 1))
                    else:
                        after(last[half_])
                    sh = FFN_K - 1 - k
                    at = n * (2 * FFN_K) + (half_ * FFN_K + k)
                    w = col("ffn_conv_w_2", at) if isinstance(n, int) else dcol("ffn_conv_w_2", at)
                    ins = V.scalar_tensor_tensor(tap[half_][:, b, sh:], A[2 * b + half_][:, 0:T - sh], w,
                                                 tap[half_][:, b, sh:], ALU.mult, ALU.add)
                    if k == 1:
                        last[half_] = own.up(ins)
                    elif half_ == 0:
                        ins.then_inc(conv2_ready, 1)
                    else:
                        ins.then_inc(pairs_drained, 1)
                    if k == 1 and half_ == 0:
                        if not first:
                            hid2_product(n - 1, 1 - b)
                        split_lo(p + LEAD, i)
                if not first:
                    hid2_low(n - 1, 1 - b)
                split_lo(p + 1 + LEAD, i)

            for j in range(4):
                ffn2_pair(j, 0, j == 0)
            with dve.Fori(1, UP2_TURNS) as i:
                own.enter(i - 1, 8)
                for j in range(4):
                    ffn2_pair(j, i)
                own.leave(UP2_TURNS - 1)
            hid2_product(KF2 - 1, 1)
            hid2_low(KF2 - 1, 1)
            for p in range(DOWN2, PIECES):
                split_lo(p + LEAD)
            add_accumulated(DOWN2 + 2 * KD)
            mean_of(17, D, RMS_EPS, A_SUMS).then_inc(mean_ready, 1)
            dve.wait_ge(rstd_ready, 16)
            dve.wait_ge(x_new, 4 * KD)
            for c in range(KD):
                V.scalar_tensor_tensor(m_wide[:, c, :], x[:, c, :], col("final_g_2", c), rstd, ALU.mult,
                                       ALU.mult).then_inc(out_ready, 1)


def _pieces(w):
    m = w.shape[1] // P
    return [w[:, c * P:(c + 1) * P].reshape(8, P, P).transpose(1, 0, 2).reshape(P, PIECE) for c in range(m)]


def _tiles(w, ks, by_row=False):
    order = [(k, m) for k in ks for m in range(8)] if by_row else [(k, m) for m in range(8) for k in ks]
    cut = [w[k * P:(k + 1) * P, m * P:(m + 1) * P] for k, m in order]
    return [np.concatenate(cut[i:i + 8], axis=1) for i in range(0, len(cut), 8)]


def pack_weights(a):
    w_in, w2 = a["w_in"][0], a["w_in_2"][0]
    w_ssm = a["ssm_out_w"][0]

    def chunk(w, at):
        return _pieces(w[:, at:at + P])

    def group(g):
        xbc = 2 * D + D_INNER
        s = chunk(w_in, xbc + D_INNER + g * P) + chunk(w_in, xbc + D_INNER + GROUPS * P + g * P)
        for base in (xbc, 2 * D):
            for c in range(2):
                s += chunk(w_in, base + (2 * g + c) * P)
        return s

    s = []
    for c in range(KD):
        s += chunk(w_in, D + c * P) + chunk(w_in, c * P)
    s += group(0)
    s += group(1)
    for i in range(1, GROUPS - 1):
        n, o = group(i + 1), _tiles(w_ssm, (2 * i - 2, 2 * i - 1), True)
        s += n[:2] + o[:1] + n[2:4] + o[1:] + n[4:]
    n = _pieces(w_in[:, w_in.shape[1] - 2 * D:])
    o = _tiles(w_ssm, (2 * GROUPS - 4, 2 * GROUPS - 3), True)
    s += n[:2] + o[:1] + n[2:4] + o[1:] + n[4:]
    s += _tiles(w_ssm, (2 * GROUPS - 2, 2 * GROUPS - 1), True)
    s += _pieces(a["conv_pw_w"][0]) + _pieces(a["w_out"][0])
    wu = a["w_gate_up"][0]
    for j in range(KF):
        s += chunk(wu, j * P) + chunk(wu, FFN + j * P)
    wd = a["w_down"][0]
    for t in range(KF // 8):
        s += _tiles(wd, range(8 * t, 8 * t + 8))
    s += _tiles(wd, range(8 * (KF // 8), KF))
    s += _pieces(w2[:, :D_LRU])
    for k in range(KSC):
        for part in (1, 2, 0):
            s += chunk(w2, 2 * D_LRU + part * D_SC + k * P)
    s += _pieces(w2[:, D_LRU:2 * D_LRU])
    wo = a["w_out_2"][0]
    s += _tiles(wo, range(KD, KD + KSC)) + _tiles(wo, range(KD))
    wu = a["w_up_2"][0]
    for j in range(KF2):
        s += chunk(wu, j * P) + chunk(wu, FFN2 + j * P)
    wd = a["w_down_2"][0]
    for t in range(KF2 // 8):
        s += _tiles(wd, range(8 * t, 8 * t + 8))
    assert len(s) == PIECES
    return np.stack(s).reshape(PIECES // 2, 2, P, PIECE).transpose(0, 2, 1, 3)


def pack_params(a):
    def cols(v):
        return v.reshape(-1, P).T

    def taps(w):
        return w.reshape(w.shape[0], -1, P).transpose(2, 1, 0).reshape(P, -1)

    def grouped(w):
        t = w.reshape(w.shape[0], -1, P)
        nx = D_INNER // P
        order = [c for g in range(GROUPS) for c in (nx + g, nx + GROUPS + g, 2 * g, 2 * g + 1)]
        return t[:, order].transpose(2, 1, 0).reshape(P, -1)

    def head_column(v):
        return np.concatenate([v, np.zeros(P - HEADS, v.dtype)]).reshape(P, 1)

    made = {
        "conv_dw_w": taps(a["conv_dw_w"][0]), "ssm_conv_w": grouped(a["ssm_conv_w"][0]),
        "ssm_conv_b": grouped(a["ssm_conv_b"]), "d_skip": cols(np.repeat(a["d_skip"][0], HD)),
        "lru_conv_w_2": taps(a["lru_conv_w_2"][0]), "sc_conv_w_2": taps(a["sc_conv_w_2"][0]),
        "dt_bias": head_column(a["dt_bias"][0]), "a_log": head_column(a["a_log"][0]),
        "ffn_conv_w_2": a["ffn_conv_w_2"][0].reshape(FFN_K, 2, KF2, P).transpose(3, 2, 1, 0).reshape(P, -1),
    }
    return np.concatenate([made[n] if n in made else cols(a[n]) for n, _ in PARAMS], axis=1)


def kernel(**inputs):
    import concourse.bacc as _bacc
    from concourse.bass_utils import run_bass_kernel_spmd as _run

    a = {k: np.asarray(v) for k, v in inputs.items()}
    at = 2 * D + D_INNER + 2 * D_INNER
    lru = np.zeros((P, KD, 2, P), np.float32)
    for j, name in enumerate(("lru_wa_2", "lru_wx_2")):
        for h in range(2 * KD):
            o = HD * (h % 2)
            lru[o:o + HD, h // 2, j, o:o + HD] = a[name][0, h]
    tri = np.triu(np.ones((P, P), np.float32))
    one = np.ones((P, P), np.float32)
    arrays = {
        "x": a["x"][0].T.reshape(KD, P, T).transpose(1, 0, 2),
        "weights": pack_weights(a),
        "params": pack_params(a),
        "w_dt": a["w_in"][0][:, at:at + HEADS].reshape(KD, P, HEADS).transpose(1, 0, 2),
        "lru_w": lru,
        "consts": np.concatenate([np.eye(P, dtype=np.float32), one, tri, one, tri], axis=1),
    }
    arrays = {f"in_{k}_dram": np.ascontiguousarray(v) for k, v in arrays.items()}
    nc = _bacc.Bacc("TRN2", target_bir_lowering=False, num_devices=1)
    args = [nc.dram_tensor(k, v.shape, mybir.dt.from_np(v.dtype), kind="ExternalInput").ap() for k, v in arrays.items()]
    args.append(nc.dram_tensor("out_0_dram", (P, KD, T), F32, kind="ExternalOutput").ap())
    hybrid_kernel(nc, *args)
    r = _run(nc, [arrays], core_ids=[0])
    got = r.results[0]["out_0_dram"]
    return np.ascontiguousarray(got.transpose(2, 1, 0).reshape(1, T, D))
```

```python
from contextlib import ExitStack

import numpy as np

import concourse.bass as bass
from concourse import mybir

F32 = mybir.dt.float32
F32R = mybir.dt.float32r
ALU = mybir.AluOpType
ACT = mybir.ActivationFunctionType

P = 128
T = 256
D = 1024
KD = D // P
TT = T // P
PIECE = 8 * P
RING = 8
LEAD = 6
PAIRS = RING // 2

CONV_K = 31
PAD = CONV_K - 1
GROUPS = 8
HEADS = 32
HPG = HEADS // GROUPS
HD = 64
D_INNER = 2 * D
SSM_K = 4
FFN = 2816
KF = FFN // P
D_LRU = 1024
D_SC = 512
KSC = D_SC // P
LRU_K = 4
SC_K = 3
FFN2 = 3 * D
KF2 = FFN2 // P
FFN_K = 3
RMS_EPS = 1e-6
LN_EPS = 1e-5
RG_C = 8.0

GLU0 = 0
SSM0 = GLU0 + 2 * KD
TURN0 = SSM0 + 6
LOOP0 = TURN0 + 6
GATES0 = LOOP0 + 8 * (GROUPS - 2)
TAIL0 = GATES0 + 2 * KD + 2
IN_AT, OUT_AT = (0, 1, 3, 4, 6, 7), (2, 5)
PW0 = TAIL0 + 2
MIX0 = PW0 + KD
UP1 = MIX0 + KD
DOWN1 = UP1 + 2 * KF
LRUX0 = DOWN1 + KF
SC0 = LRUX0 + KD
LRUG0 = SC0 + 3 * KSC
OUT2 = LRUG0 + KD
UP2 = OUT2 + KD + KSC
DOWN2 = UP2 + 2 * KF2
PIECES = DOWN2 + KF2
UP1_TURNS = 2 * KF // RING
UP2_TURNS = 2 * KF2 // RING
DOWN1_REST = KF - 2 * KD

PARAMS = [("mix_pre_g", KD), ("glu_b", 2 * KD), ("conv_dw_w", KD * CONV_K), ("conv_dw_b", KD),
          ("conv_ln_g", KD), ("conv_ln_b", KD), ("conv_pw_b", KD), ("ssm_conv_w", 32 * SSM_K),
          ("ssm_conv_b", 32), ("d_skip", 16), ("ssm_norm_g", 16), ("gate_b", 2 * KD), ("mix_post_g", KD),
          ("ffn_pre_g", KD), ("ffn_post_g", KD), ("norm1_g_2", KD), ("lru_conv_w_2", KD * LRU_K),
          ("lru_conv_b_2", KD), ("lru_ba_2", KD), ("lru_bx_2", KD), ("lru_lambda_2", KD),
          ("sc_conv_w_2", KSC * SC_K), ("norm2_g_2", KD), ("ffn_conv_w_2", 2 * KF2 * FFN_K),
          ("final_g_2", KD), ("dt_bias", 1), ("a_log", 1)]
AT = {}
NPAR = 0
for _name, _n in PARAMS:
    AT[_name] = NPAR
    NPAR += _n


STAGED_MIX = KD
STAGED_FFN1 = STAGED_MIX + KD
STAGED_SC = STAGED_FFN1 + KF
STAGED_LRU = STAGED_SC + KSC


class Count:

    def __init__(self, sem):
        self.sem, self.n, self.turn = sem, 0, None

    def value(self):
        return self.n if self.turn is None else self.n + self.per * self.turn

    def up(self, instruction):
        instruction.then_inc(self.sem, 1)
        self.n += 1
        return self.value()

    def enter(self, turn, per):
        self.turn, self.per, self.start = turn, per, self.n

    def leave(self, turns):
        assert self.n - self.start == self.per, (self.n - self.start, self.per)
        self.n, self.turn = self.start + self.per * turns, None


def hybrid_kernel(nc, x_in, weights, params_in, w_dt, lru_w, consts, out):
    cs_dram = nc.dram_tensor("cs_dram", [HEADS + HPG, T], F32).ap()
    stack = ExitStack()
    with stack:
        def sb(name, shape, dt=F32, scope=stack):
            return scope.enter_context(nc.sbuf_tensor(name, shape, dt))

        def sem(name):
            return stack.enter_context(nc.semaphore(name))

        raw = sb("raw", [P, RING, PIECE])
        w_hi = sb("w_hi", [P, RING, PIECE], F32R)
        w_lo = sb("w_lo", [P, RING, PIECE], F32R)
        x = sb("x", [P, KD, T])
        h_hi = sb("h_hi", [P, KD, T], F32R)
        h_lo = sb("h_lo", [P, KD, T], F32R)
        par = sb("par", [P, NPAR])
        cst = sb("cst", [P, 5 * P])
        half = sb("half", [P, TT])
        zero = sb("zero", [P, P], F32R)
        mean = sb("mean", [P, T])
        sq_sum = sb("sq_sum", [P, 2, T])
        moment = sb("moment", [P, TT])
        scale = sb("scale", [P, TT])
        stage = sb("stage", [P, 2, T])
        stage2 = sb("stage2", [P, 2, T])
        ident = cst[:, 0:P]
        ones = cst[:, P:2 * P]
        mask = cst[:, 2 * P:5 * P]

        s1 = ExitStack()
        v = sb("v", [P, KD, PAD + T], scope=s1)
        acc = sb("acc", [P, KD, T], scope=s1)
        s1.close()
        s2 = ExitStack()
        conv_hi = sb("conv_hi", [P, KD, T], F32R, s2)
        sb("conv_room", [P, KD * PAD], scope=s2)
        conv_lo = sb("conv_lo", [P, KD, T], F32R, s2)
        s2.close()
        sq_wide = sb("sq_wide", [P, KD, PAD + T])
        m_wide = sb("m_wide", [P, KD, T])

        s3 = ExitStack()
        gates = sb("gates", [P, 2 * KD, T], scope=s3)
        ubuf = sb("ubuf", [P, 4, SSM_K - 1 + T], scope=s3)
        gb = sb("gb", [P, 4, T], scope=s3)
        zs = sb("zs", [P, 2, T], scope=s3)
        csrow = sb("csrow", [P, HPG, T], scope=s3)
        dec = sb("dec", [P, HPG, 3 * P], scope=s3)
        xdt = sb("xdt", [P, TT, HPG, HD], scope=s3)
        cbm = sb("cbm", [P, 3 * P], scope=s3)
        y = sb("y", [P, 2, T], scope=s3)
        ysq = sb("ysq", [P, 2, T], scope=s3)
        yn_hi = sb("yn_hi", [P, 2, T], F32R, s3)
        yn_lo = sb("yn_lo", [P, 2, T], F32R, s3)
        part = sb("part", [P, 2, T], scope=s3)
        wdt = sb("wdt", [P, KD, HEADS], scope=s3)
        tok = sb("tok", [P, 5, HEADS], scope=s3)
        s3.close()
        s4 = ExitStack()
        hid_hi = sb("hid_hi", [P, KF2, T], F32R, s4)
        hid_lo = sb("hid_lo", [P, KF2, T], F32R, s4)
        stage3 = sb("stage3", [P, 2, T], scope=s4)
        s4.close()
        s5 = ExitStack()
        ig = sb("ig", [P, KD, T], scope=s5)
        a_t = sb("a_t", [P, KD, T], scope=s5)
        th = sb("th", [P, KD, T], scope=s5)
        bd = sb("bd", [P, KD, 2, P], scope=s5)
        sc_hi = sb("sc_hi", [P, KSC, T], F32R, s5)
        sc_lo = sb("sc_lo", [P, KSC, T], F32R, s5)
        sc_sum = sb("sc_sum", [P, T], scope=s5)
        u2 = sb("u2", [P, 2, LRU_K - 1 + T], scope=s5)
        sp = sb("sp", [P, 8, KD], scope=s5)
        s5.close()
        s6 = ExitStack()
        lru_hi = sb("lru_hi", [P, KD, T], F32R, s6)
        lru_lo = sb("lru_lo", [P, KD, T], F32R, s6)
        s6.close()
        xp, rg = sq_wide, m_wide
        def staging(k):
            return (stage if k % 4 < 2 else stage2)[:, k % 2, :]

        rs, rs2 = mean[:, :], sq_sum[:, 1, :]

        A = [stack.enter_context(nc.psum_tensor(f"A{i}", [P, 512], F32)) for i in range(4)]
        B = stack.enter_context(nc.psum_tensor("B", [P, 4, 512], F32))

        sums = A[3][:, 0:TT]
        rstd = A[3][:, T:2 * T]


        def acc_out(m):
            return B[:, m // 2, (m % 2) * T:(m % 2 + 1) * T]

        def down1_done(m):
            return DOWN1 + 2 * KD + (DOWN1_REST * (m | 1) + DOWN1_REST - 1) // 8 + 1

        def out2_done(m):
            return OUT2 + KSC + (m | 1) + 1

        def splits_before(m, done, first, end):
            return range(done(m - 1) + 1 if m else first, min(done(m) + 1, end))

        def eight_banks(n):
            return A[n % 8][:, 0:T] if n % 8 < 4 else B[:, n % 8 - 4, 0:T]

        loaded = [sem(f"loaded{i}") for i in range(PAIRS)]
        x_loaded = [sem("x_loaded0"), sem("x_loaded1")]
        first_loaded = sem("first_loaded")
        const_loaded, wdt_loaded = sem("const_loaded"), sem("wdt_loaded")
        hi_ready, lo_ready, pieces_done = sem("hi_ready"), sem("lo_ready"), sem("pieces_done")
        constants_written = sem("constants_written")
        squares_ready, sums_ready, squares_summed = sem("squares_ready"), sem("sums_ready"), sem("squares_summed")
        mean_ready, scale_ready, rstd_ready = sem("mean_ready"), sem("scale_ready"), sem("rstd_ready")
        staged, stage_hi, operand_ready = sem("staged"), sem("stage_hi"), sem("operand_ready")
        act_steps, dve_steps, pool_steps = sem("act_steps"), sem("dve_steps"), sem("pool_steps")
        dt_raw_ready, dt_raw_used, cs_ready, tok_psum, scale_read = (
            sem("dt_raw_ready"), sem("dt_raw_used"), sem("cs_ready"), sem("tok_psum"), sem("scale_read"))
        gates_ready, rs_ready, rs2_ready, scaled = sem("gates_ready"), sem("rs_ready"), sem("rs2_ready"), sem("scaled")
        dt_abs, dt_exp = sem("dt_abs"), sem("dt_exp")
        cs_stored, csrow_loaded = sem("cs_stored"), sem("csrow_loaded")
        gate_ready, pairs_drained, drained = sem("gate_ready"), sem("pairs_drained"), sem("drained")
        conv_ready, silu_ready = sem("conv_ready"), sem("silu_ready")
        cb_ready, cb_used, xt_ready, xdt_ready = sem("cb_ready"), sem("cb_used"), sem("xt_ready"), sem("xdt_ready")
        dec_ready, m_ready, y_ready, yz_ready = sem("dec_ready"), sem("m_ready"), sem("y_ready"), sem("yz_ready")
        ysq_ready, ynhi_ready, yn_ready = (
            sem("ysq_ready"), sem("ynhi_ready"), sem("yn_ready"))
        conv_sum_ready, centred, conv_norm, mix_drained = (
            sem("conv_sum_ready"), sem("centred"), sem("conv_norm"), sem("mix_drained"))
        x_new, lru_w_loaded, c_ready, sp_exp = sem("x_new"), sem("lru_w_loaded"), sem("c_ready"), sem("sp_exp")
        copied, xp_ready, bd_ready, bd_drained, a_ready, m2_ready, mult_ready, gelu_ready = (
            sem("copied"), sem("xp_ready"), sem("bd_ready"), sem("bd_drained"), sem("a_ready"), sem("m2_ready"),
            sem("mult_ready"), sem("gelu_ready"))
        sc_copied, tap_ready, conv2_ready = sem("sc_copied"), sem("tap_ready"), sem("conv2_ready")
        out_ready, stored = sem("out_ready"), sem("stored")

        def col(name, c, n=1):
            return par[:, AT[name] + c:AT[name] + c + n]

        def dcol(name, c):
            return par[:, bass.ds(c + AT[name], 1)]

        block = stack.enter_context(nc.Block())

        @block.sync
        def _(sp_):
            for half_x in range(2):
                ks = slice(half_x * KD // 2, (half_x + 1) * KD // 2)
                sp_.dma_start(x[:, ks, :], x_in[:, ks, :]).then_inc(x_loaded[half_x], 16)
            sp_.dma_start(par[:, :], params_in).then_inc(const_loaded, 16)
            sp_.dma_start(cst[:, :], consts).then_inc(const_loaded, 16)
            for q in range(PAIRS):
                if q == 0:
                    sp_.dma_start(raw[:, 0, :], weights[0, :, 0, :]).then_inc(first_loaded, 16)
                    sp_.dma_start(raw[:, 1, :], weights[0, :, 1, :]).then_inc(loaded[0], 16)
                    sp_.dma_start(wdt[:, :, :], w_dt).then_inc(wdt_loaded, 16)
                else:
                    sp_.dma_start(raw[:, 2 * q:2 * q + 2, :], weights[q]).then_inc(loaded[q], 16)
            rounds = PIECES // RING
            with sp_.Fori(1, rounds) as r:
                for q in range(PAIRS):
                    sp_.wait_ge(lo_ready, r * RING + (2 * q + 2 - RING))
                    sp_.dma_start(raw[:, 2 * q:2 * q + 2, :],
                                  weights[bass.ds(r * PAIRS + q, 1)].rearrange("a p s n -> p (a s) n")
                                  ).then_inc(loaded[q], 16)
            for q in range(rounds * PAIRS, PIECES // 2):
                s = q % PAIRS
                sp_.wait_ge(lo_ready, 2 * (q - PAIRS) + 2)
                sp_.dma_start(raw[:, 2 * s:2 * s + 2, :], weights[q]).then_inc(loaded[s], 16)
            for c in range(KD):
                sp_.wait_ge(out_ready, c + 1)
                sp_.dma_start(out[:, c, :], m_wide[:, c, :]).then_inc(stored, 16)
            sp_.wait_ge(stored, 16 * KD)

        @block.gpsimd
        def _(pool):
            nc.gpsimd.memset(half[:, :], -0.5).then_inc(constants_written, 1)
            nc.gpsimd.memset(zero[:, :].bitcast(F32), 0.0).then_inc(constants_written, 1)
            nc.gpsimd.memset(v[:, :, 0:PAD], 0.0).then_inc(constants_written, 1)
            nc.gpsimd.memset(ubuf[:, :, 0:SSM_K - 1], 0.0).then_inc(constants_written, 1)
            pool.wait_ge(constants_written, 4)

            def rsqrt(n):
                pool.wait_ge(mean_ready, n)
                nc.gpsimd.tensor_tensor(scale[:, :], moment[:, :], half[:, :], ALU.pow).then_inc(scale_ready, 1)

            def split_lo(p, turn=0):
                s = p % RING
                pool.wait_ge(hi_ready, p + 1 + 8 * turn)
                nc.gpsimd.tensor_tensor(w_lo[:, s, :], raw[:, s, :], w_hi[:, s, :].bitcast(F32),
                                        ALU.subtract).then_inc(lo_ready, 1)

            rsqrt(1)
            split_lo(1)
            pool.wait_ge(lo_ready, LEAD)
            for p in range(GLU0 + LEAD, TURN0 + LEAD):
                split_lo(p)
            for p in range(TURN0, LOOP0):
                split_lo(p + LEAD)
                if p == TURN0 + 4:
                    rsqrt(2)
            with pool.Fori(0, GROUPS - 2) as i:
                for n in range(8):
                    split_lo(LOOP0 + n + LEAD, i)
                    if n == 5:
                        rsqrt(i + 3)
            for p in range(GATES0, UP1):
                split_lo(p + LEAD)
                if p == GATES0 + 5:
                    rsqrt(GROUPS + 1)
                if p == GATES0 + 10:
                    rsqrt(10)
            def sum_squares(n0):
                for c in range(1, KD):
                    pool.wait_ge(squares_ready, n0 + c + 1)
                    if c > 1:
                        pool.wait_ge(pool_steps, (n0 - 3 * KD) // (2 * KD) * (KD - 2) + c - 1)
                    ins = nc.gpsimd.tensor_tensor(sq_sum[:, 0, :], sq_wide[:, c, 0:T],
                                                  sq_wide[:, 0, 0:T] if c == 1 else sq_sum[:, 0, :], ALU.add)
                    ins.then_inc(squares_summed if c == KD - 1 else pool_steps, 1)

            for n in (11, 13):
                rsqrt(n)
                sum_squares((n - 8) * KD)
                rsqrt(n + 1)
            pool.wait_ge(lo_ready, LRUX0 + LEAD)
            for p in range(LRUX0, OUT2):
                split_lo(p + LEAD)
            for n in range(15, 17):
                rsqrt(n)

        @block.tensor
        def _(pe):
            mm = nc.tensor.matmul

            def tile(slot, j, hi, lo, dst, first, last, free=False):
                wh = w_hi[:, slot, j * P:(j + 1) * P]
                wl = w_lo[:, slot, j * P:(j + 1) * P]
                mm(dst, wh, lo, start=first, stop=False, skip_group_check=free)
                mm(dst, wh, hi, start=False, stop=False, skip_group_check=free)
                return mm(dst, wl, hi, start=False, stop=last, skip_group_check=free)

            def chunk_piece(p, turn, dst, hi, lo, operand=None):
                pe.wait_ge(lo_ready, p + 1 + 8 * turn)
                for k in range(KD):
                    if operand is not None:
                        pe.wait_ge(operand_ready, operand + k + 1)
                    ins = tile(p % RING, k, hi[:, k, :], lo[:, k, :], dst, k == 0, k == KD - 1)
                ins.then_inc(pieces_done, 1)

            def clear_accumulators():
                for b in range(4):
                    mm(B[:, b, :], zero[:, :], zero[:, :].unsqueeze(1).to_broadcast([P, 4, P]), start=True,
                       stop=False, skip_group_check=True)

            def first_two(p, operand):
                pe.wait_ge(lo_ready, p + 2)
                for k in range(KD):
                    pe.wait_ge(operand_ready, operand + k + 1)
                    for j in range(2):
                        ins = tile((p + j) % RING, k, h_hi[:, k, :], h_lo[:, k, :], A[j][:, 0:T], k == 0, k == KD - 1)
                        if k == KD - 1:
                            ins.then_inc(pieces_done, 1)

            def scaled_start(p, operand, summed_n, norm_n):
                first_two(p, operand)
                summed_squares(summed_n)
                pe.wait_ge(lo_ready, p + 3)
                for k in range(KD):
                    if k == 5:
                        spread_scale(norm_n)
                    ins = tile((p + 2) % RING, k, h_hi[:, k, :], h_lo[:, k, :], A[2][:, 0:T], k == 0, k == KD - 1)
                ins.then_inc(pieces_done, 1)

            def summed_squares(n):
                pe.wait_ge(squares_summed, n)
                for t in range(TT):
                    ins = mm(sums[:, t:t + 1], sq_sum[:, 0, t * P:(t + 1) * P], ones[:, 0:1], start=True, stop=True)
                ins.then_inc(sums_ready, 1)

            def spread_scale(n):
                pe.wait_ge(scale_ready, n)
                for t in range(TT):
                    ins = mm(rstd[:, t * P:(t + 1) * P], scale[:, t:t + 1].to_broadcast([P, P]), ident, start=True,
                             stop=True)
                ins.then_inc(rstd_ready, 1)

            pe.wait_ge(const_loaded, 32)
            summed_squares(1)
            spread_scale(1)
            first_two(GLU0, 0)
            for c in range(KD):
                for j in range(2 if c else 0):
                    if c >= 2:
                        pe.wait_ge(pairs_drained, c - 1)
                    chunk_piece(GLU0 + 2 * c + j, 0, A[2 * (c % 2) + j][:, 0:T], h_hi, h_lo)
                if c == 0:
                    pe.wait_ge(wdt_loaded, 16)
                    for k in range(KD):
                        pe.wait_ge(operand_ready, k + 1)
                        ins = mm(B[0:HEADS, 0, 0:T], wdt[:, k, :], acc[:, k, :], start=k == 0, stop=k == KD - 1)
                    ins.then_inc(dt_raw_ready, 1)
            pe.wait_ge(dt_raw_used, 1)
            pe.wait_ge(constants_written, 4)
            clear_accumulators()
            pe.wait_ge(cs_ready, 1)
            pe.wait_ge(pairs_drained, KD)
            dtw = gates
            for n, src in enumerate([dtw[0:HEADS, 0, 0:P], dtw[0:HEADS, 0, P:T], dtw[0:HEADS, 1, 0:P],
                                     dtw[0:HEADS, 1, P:T], dtw[0:HEADS, 2, 0:P]]):
                ins = nc.tensor.transpose(A[3][:, n * HEADS:(n + 1) * HEADS], src, ident[0:HEADS, 0:HEADS])
            ins.then_inc(tok_psum, 1)

            def ring_bank(o):
                return A[o % 3][:, 0:T]

            def single(p, o, turn=0, g=0):
                if o >= 3:
                    pe.wait_ge(drained, o - 2 + 6 * g)
                chunk_piece(p, turn, ring_bank(o), h_hi, h_lo)

            for o in range(6):
                single(SSM0 + o, o)

            def cb(g):
                pe.wait_ge(silu_ready, 4 * g + 2)
                pe.wait_ge(scale_read, g + 1)
                mm(A[3][:, 0:T], gb[:, 0, 0:P], gb[:, 1, :], start=True, stop=True)
                mm(A[3][:, T:T + P], gb[:, 0, P:T], gb[:, 1, P:T], start=True, stop=True).then_inc(cb_ready, 1)

            def x_transposes(g):
                pe.wait_ge(silu_ready, 4 * g + 4)
                pe.wait_ge(cb_used, g + 1)
                for t in range(TT):
                    for c in range(2):
                        ins = nc.tensor.transpose(A[3][:, t * T + c * P:t * T + (c + 1) * P],
                                                  gb[:, 2 + c, t * P:(t + 1) * P], ident)
                ins.then_inc(xt_ready, 1)

            def y_products(g):
                pe.wait_ge(m_ready, g + 1)
                for r in range(HPG):
                    rows = slice(HD * (r % 2), HD * (r % 2) + HD)
                    at = (r // 2) * T
                    mm(A[3][rows, at:at + T], xdt[:, 0, r, :], dec[:, r, 0:T], start=True, stop=False)
                    ins = mm(A[3][rows, at + P:at + T], xdt[:, 1, r, :], dec[:, r, T:T + P], start=False, stop=True)
                ins.then_inc(y_ready, 1)

            def y_sums(g):
                pe.wait_ge(ysq_ready, g + 1)
                for t in range(TT):
                    for c in range(2):
                        ins = mm(sums[:, t:t + 1], ysq[:, c, t * P:(t + 1) * P], ones[:, 0:1],
                                 start=c == 0, stop=c == 1)
                ins.then_inc(sums_ready, 1)

            def y_scale(g):
                spread_scale(g + 2)

            def out_piece(p, turn, g, c):
                pe.wait_ge(lo_ready, p + 1 + 8 * turn)
                pe.wait_ge(yn_ready, 2 * g + c + 1)
                for m in range(KD):
                    ins = tile(p % RING, m, yn_hi[:, c, :], yn_lo[:, c, :], acc_out(m), False, False, True)
                ins.then_inc(pieces_done, 1)

            chain = {1: cb, 2: x_transposes, 3: y_products, 4: y_sums, 5: y_scale}

            def group_turn(g, base, t):
                for s in range(6):
                    single(base + IN_AT[s], 6 + s, t, g)
                    if s in (1, 3):
                        out_piece(base + OUT_AT[s // 2], t, g - 1, s // 2)
                    if s in chain:
                        chain[s](g)

            for s in range(6):
                single(TURN0 + s, 6 + s)
                if s in chain:
                    chain[s](0)
            with pe.Fori(0, GROUPS - 2) as i:
                group_turn(i + 1, LOOP0, i)
            g = GROUPS - 1
            for s in range(2 * KD):
                single(GATES0 + s + (s >= 2) + (s >= 4), 6 * GROUPS + s)
                if s in (1, 3):
                    out_piece(GATES0 + OUT_AT[s // 2], 0, g - 1, s // 2)
                if s in chain:
                    chain[s](g)
                if s == 7:
                    pe.wait_ge(scale_read, GROUPS + 1)
                    pe.wait_ge(conv_sum_ready, 1)
                    for b in range(2):
                        ins = mm(A[3][:, 0:T], ones, sq_sum[:, b, :], start=b == 0, stop=b == 1)
                    ins.then_inc(sums_ready, 1)
                if s == 10:
                    summed_squares(2)
                if s == 11:
                    spread_scale(10)
            out_piece(TAIL0, 0, g, 0)
            out_piece(TAIL0 + 1, 0, g, 1)
            for m in range(KD):
                if m < 3:
                    pe.wait_ge(drained, 6 * GROUPS + 2 * KD - 2 + m)
                else:
                    pe.wait_ge(mix_drained, m - 2)
                chunk_piece(PW0 + m, 0, ring_bank(64 + m), conv_hi, conv_lo, KD if m == 0 else None)
            for m in range(KD):
                if m < 3:
                    pe.wait_ge(mix_drained, KD - 2 + m)
                else:
                    pe.wait_ge(squares_ready, 2 * KD + m - 2)
                chunk_piece(MIX0 + m, 0, ring_bank(72 + m), h_hi, h_lo, 2 * KD if m == 0 else None)
            summed_squares(3)
            spread_scale(11)

            def up_pair(base, j, turn, read=None, n=None):
                for half_ in range(2):
                    if n is not None:
                        pe.wait_ge(read, n)
                    chunk_piece(base + 2 * j + half_, turn, A[j % 2 * 2 + half_][:, 0:T], h_hi, h_lo)

            scaled_start(UP1, 3 * KD, 4, 12)
            pe.wait_ge(rs_ready, 1)
            chunk_piece(UP1 + 3, 0, A[3][:, 0:T], h_hi, h_lo)
            for j in range(2, 4):
                up_pair(UP1, j, 0, staged, STAGED_FFN1 + j - 1)
            with pe.Fori(1, UP1_TURNS) as i:
                for j in range(4):
                    up_pair(UP1, j, i, staged, i * 4 + (STAGED_FFN1 + j - 1))
            for j in range(UP1_TURNS * 4, KF):
                up_pair(UP1, j, 0, staged, STAGED_FFN1 + j - 1)

            def down_turns(p, turns, operand):
                with pe.Fori(0, turns) as i:
                    for m in range(KD):
                        pe.wait_ge(lo_ready, p + m + 1 + 8 * i)
                        if m == 0:
                            pe.wait_ge(operand_ready, i * 8 + (operand + 8))
                        for k in range(8):
                            ins = tile((p + m) % RING, k, hid_hi[:, bass.ds(i * 8 + k, 1), :].rearrange("p a t -> p (a t)"),
                                       hid_lo[:, bass.ds(i * 8 + k, 1), :].rearrange("p a t -> p (a t)"),
                                       acc_out(m), False, False, True)
                        ins.then_inc(pieces_done, 1)

            clear_accumulators()
            done1 = 4 * KD
            down_turns(DOWN1, 2, done1)
            for n in range(DOWN1_REST * KD):
                p = DOWN1 + 2 * KD + n // 8
                m, k = n // DOWN1_REST, n % DOWN1_REST
                if n % 8 == 0:
                    pe.wait_ge(lo_ready, p + 1)
                if m == 0:
                    pe.wait_ge(operand_ready, done1 + 2 * KD + k + 1)
                ins = tile(p % RING, n % 8, hid_hi[:, 2 * KD + k, :], hid_lo[:, 2 * KD + k, :], acc_out(m),
                           False, False, True)
                if n % 8 == 7:
                    ins.then_inc(pieces_done, 1)
            summed_squares(5)
            spread_scale(13)

            ops = done1 + KF

            def block_gates(c):
                pe.wait_ge(xp_ready, c + 1)
                if c == 0:
                    pe.wait_ge(lru_w_loaded, 16)
                if c >= 2:
                    pe.wait_ge(bd_drained, c - 1)
                mm(B[:, 2 * (c % 2), 0:T], bd[:, c, 0, :], xp[:, c, 0:T], start=True, stop=True)
                mm(B[:, 2 * (c % 2) + 1, 0:T], bd[:, c, 1, :], xp[:, c, 0:T], start=True,
                   stop=True).then_inc(bd_ready, 1)

            scaled_start(LRUX0, ops, 6, 14)
            for c in range(3, KD):
                pe.wait_ge(copied, c - 2)
                chunk_piece(LRUX0 + c, 0, A[c % 3][:, 0:T], h_hi, h_lo)
                block_gates(c - 3)
            for n in range(3 * KSC):
                if n < 3:
                    pe.wait_ge(copied, KD)
                if n == 4:
                    pe.wait_ge(bd_drained, KD)
                if n >= 8:
                    pe.wait_ge(staged, STAGED_SC + (n - 8) // 3 + 1)
                chunk_piece(SC0 + n, 0, eight_banks(n), h_hi, h_lo)
                if n < 3:
                    block_gates(KD - 3 + n)
            for c in range(KD):
                pe.wait_ge(staged, STAGED_LRU - 1 if c < 4 else STAGED_LRU)
                chunk_piece(LRUG0 + c, 0, eight_banks(c + 4), h_hi, h_lo)
            pe.wait_ge(gelu_ready, 4)
            clear_accumulators()
            ops += KD
            for n in range(KSC * KD):
                p = OUT2 + n // 8
                m, k = n // KSC, n % KSC
                if n % 8 == 0:
                    pe.wait_ge(lo_ready, p + 1)
                if m == 0:
                    pe.wait_ge(operand_ready, ops + k + 1)
                ins = tile(p % RING, n % 8, sc_hi[:, k, :], sc_lo[:, k, :], acc_out(m), False, False, True)
                if n % 8 == 7:
                    ins.then_inc(pieces_done, 1)
            ops += KSC
            for m in range(KD):
                p = OUT2 + KSC + m
                pe.wait_ge(lo_ready, p + 1)
                for k in range(KD):
                    if m == 0:
                        pe.wait_ge(operand_ready, ops + k + 1)
                    ins = tile(p % RING, k, lru_hi[:, k, :], lru_lo[:, k, :], acc_out(m), False, False, True)
                ins.then_inc(pieces_done, 1)
            ops += KD
            summed_squares(7)
            spread_scale(15)
            first_two(UP2, ops)
            up_pair(UP2, 1, 0)
            for j in range(2, 4):
                up_pair(UP2, j, 0, pairs_drained, KD + j - 1)
            with pe.Fori(1, UP2_TURNS) as i:
                for j in range(4):
                    up_pair(UP2, j, i, pairs_drained, i * 4 + (KD + j - 1))
            clear_accumulators()
            down_turns(DOWN2, KF2 // 8, ops + KD)
            summed_squares(8)
            spread_scale(16)

        @block.scalar
        def _(act):
            F = nc.scalar.activation
            own = Count(act_steps)

            def split_hi(p, turn=0):
                if p >= PIECES:
                    return
                s = p % RING
                if p == 0:
                    act.wait_ge(first_loaded, 16)
                elif p % 2 == 0 or p == 1:
                    act.wait_ge(loaded[s // 2], 16 * (p // RING + 1) + 16 * turn)
                if p >= RING:
                    act.wait_ge(pieces_done, p + 1 - RING + 8 * turn)
                F(w_hi[:, s, :], raw[:, s, :], ACT.Copy).then_inc(hi_ready, 1)

            def split_stage(n, dst, turn=0, per=0):
                act.wait_ge(staged, n + 1 + per * turn)
                F(dst, stage[:, n % 2, :], ACT.Copy).then_inc(stage_hi, 1)

            for c in range(KD):
                act.wait_ge(x_loaded[c // (KD // 2)], 16)
                F(acc[:, c, :], x[:, c, :], ACT.Square).then_inc(squares_ready, 1)
            for p in range(2):
                split_hi(p)
            for k in range(KD):
                act.wait_ge(staged, k + 1)
                F(h_hi[:, k, :], acc[:, k, :], ACT.Copy).then_inc(stage_hi, 1)
            for p in range(2, LEAD):
                split_hi(p)
            dtw = gates
            act.wait_ge(const_loaded, 32)
            for c in range(KD):
                p = GLU0 + 2 * c
                split_hi(p + LEAD)
                act.wait_ge(pieces_done, p + 1)
                if c >= 2:
                    act.wait_ge(pairs_drained, c - 1)
                F(stage2[:, c % 2, :], A[2 * (c % 2)][:, 0:T], ACT.Sigmoid,
                  bias=col("glu_b", KD + c)).then_inc(gate_ready, 1)
                split_hi(p + 1 + LEAD)
                if c == 2:
                    act.wait_ge(dt_abs, 1)
                    n = own.up(F(dtw[0:HEADS, 4, :], dtw[0:HEADS, 3, :], ACT.Abs))
                    act.wait_ge(act_steps, n)
                    F(dtw[0:HEADS, 5, :], dtw[0:HEADS, 4, :], ACT.Exp, scale=-1.0).then_inc(dt_exp, 1)
                    F(dtw[0:HEADS, 6, 0:1], par[0:HEADS, AT["a_log"]:AT["a_log"] + 1], ACT.Exp).then_inc(dt_exp, 1)
                if c == 6:
                    act.wait_ge(cs_ready, 1)
                    act.dma_start(cs_dram[0:HEADS, :], dtw[0:HEADS, 1, :]).then_inc(cs_stored, 16)
                    act.dma_start(cs_dram[HEADS:, :], dtw[0:HPG, 1, :]).then_inc(cs_stored, 16)
            act.wait_ge(cs_stored, 32)

            def load_csrow(g):
                at = slice(g * HPG, (g + 1) * HPG) if isinstance(g, int) else bass.ds(g * HPG, HPG)
                src = cs_dram[at, :]
                act.dma_start(csrow[:, :, :], src.partition_broadcast(P)).then_inc(csrow_loaded, 16)

            def drain_input(s, g, p, turn):
                act.wait_ge(pieces_done, p + 1 + 8 * turn)
                if s < 4:
                    F(ubuf[:, s, SSM_K - 1:], ring(s), ACT.Copy).then_inc(drained, 1)
                else:
                    F(zs[:, s - 4, :], ring(s), ACT.Silu).then_inc(drained, 1)

            def ring(o):
                return A[o % 3][:, 0:T]

            load_csrow(0)
            act.wait_ge(constants_written, 4)
            for s in range(6):
                split_hi(SSM0 + s + LEAD)
                drain_input(s, 0, SSM0 + s, 0)

            def silu_bc(g):
                for j in (0, 1):
                    act.wait_ge(conv_ready, 4 * g + (j + 1))
                    F(gb[:, j, :], gb[:, j, :], ACT.Silu).then_inc(silu_ready, 1)

            def silu_x(g):
                for j in (2, 3):
                    act.wait_ge(conv_ready, 4 * g + (j + 1))
                    F(gb[:, j, :], gb[:, j, :], ACT.Silu).then_inc(silu_ready, 1)

            def exponents(g):
                act.wait_ge(csrow_loaded, 16 * g + 16)
                for b, (k, cols) in enumerate(((2, slice(0, P)), (4, slice(P, T)), (3, slice(P, T)))):
                    for r_ in range(HPG):
                        h = g * HPG + r_
                        cs = tok[:, k, h:h + 1] if isinstance(g, int) else tok[:, k, bass.ds(h, 1)]
                        n = own.up(F(dec[:, r_, b * P:(b + 1) * P], csrow[:, r_, cols], ACT.Relu, bias=cs, scale=-1.0))
                act.wait_ge(act_steps, n)
                load_csrow(g + 1)

            def decays(g):
                F(dec[:, :, :], dec[:, :, :], ACT.Exp, scale=-1.0).then_inc(dec_ready, 1)

            def y_squares(g):
                act.wait_ge(yz_ready, g + 1)
                F(ysq[:, :, :], y[:, :, :], ACT.Square).then_inc(ysq_ready, 1)

            def yn_high(g):
                act.wait_ge(scale_read, g + 2)
                F(yn_hi[:, :, :], y[:, :, :], ACT.Copy).then_inc(ynhi_ready, 1)

            act.wait_ge(scale_read, 1)
            exponents(0)

            def group_turn(g, base, t, at, count):
                left = list(range(count))

                def split():
                    if left:
                        split_hi(base + left.pop(0) + LEAD, t)

                silu_bc(g)
                split()
                drain_input(0, g, base + at[0], t)
                silu_x(g)
                split()
                drain_input(1, g, base + at[1], t)
                decays(g)
                split()
                if count == 8:
                    split()
                drain_input(2, g, base + at[2], t)
                split()
                drain_input(3, g, base + at[3], t)
                split()
                if count == 8:
                    split()
                y_squares(g)
                drain_input(4, g, base + at[4], t)
                exponents(g + 1)
                split()
                yn_high(g)
                drain_input(5, g, base + at[5], t)
                while left:
                    split()

            group_turn(0, TURN0, 0, range(6), 6)
            with act.Fori(0, GROUPS - 2) as i:
                own.enter(i, 3 * HPG)
                group_turn(i + 1, LOOP0, i, IN_AT, 8)
                own.leave(GROUPS - 2)

            g = GROUPS - 1
            act.wait_ge(csrow_loaded, 16 * (GROUPS + 1))
            silu_bc(g)

            def conv_operand(c):
                act.wait_ge(conv_norm, c + 1)
                if c >= 2:
                    act.wait_ge(operand_ready, KD + c - 1)
                n = own.up(F(stage[:, c % 2, :], acc[:, c, :], ACT.Silu, bias=col("conv_ln_b", c)))
                act.wait_ge(act_steps, n)
                F(conv_hi[:, c, :], stage[:, c % 2, :], ACT.Copy).then_inc(stage_hi, 1)

            for s in range(2 * KD):
                p = GATES0 + s + (s >= 2) + (s >= 4)
                split_hi(p + LEAD)
                act.wait_ge(pieces_done, p + 1)
                F(gates[:, s, :], ring(s), ACT.Identity, bias=col("gate_b", s)).then_inc(drained, 1)
                if s == 0:
                    silu_x(g)
                if s == 1:
                    decays(g)
                if s in (1, 3):
                    split_hi(p + 1 + LEAD)
                if s == 3:
                    y_squares(g)
                if s == 6:
                    yn_high(g)
                if s == 8:
                    for c in range(KD):
                        act.wait_ge(centred, c + 1)
                        F(v[:, c, 0:T], acc[:, c, :], ACT.Square).then_inc(squares_ready, 1)
                if 11 <= s < 15:
                    conv_operand(2 * s - 22)
                    conv_operand(2 * s - 21)
            split_hi(TAIL0 + LEAD)
            split_hi(TAIL0 + 1 + LEAD)
            act.wait_ge(drained, 6 * GROUPS + 2 * KD)
            for h in range(2):
                F(gates[:, h * KD:(h + 1) * KD, :], gates[:, h * KD:(h + 1) * KD, :], ACT.Sigmoid).then_inc(gates_ready, 1)
            staged_n = KD
            for m in range(KD):
                split_hi(PW0 + m + LEAD)
                split_stage(staged_n + m, h_hi[:, m, :])
            staged_n += KD

            def copy_and_square(src, dst_copy, dst_square):
                if dst_copy is not None:
                    F(dst_copy, src, ACT.Copy).then_inc(act_steps, 1)
                    own.n += 1
                F(dst_square, src, ACT.Square).then_inc(squares_ready, 1)

            for m in range(KD):
                split_hi(MIX0 + m + LEAD)
                act.wait_ge(pieces_done, MIX0 + m + 1)
                copy_and_square(A[(72 + m) % 3][:, 0:T], m_wide[:, m, :], sq_wide[:, m, 0:T])

            def residual_squares(n, first=0, end=0):
                for c in range(KD):
                    for p in splits_before(c, out2_done, first, end):
                        split_hi(p + LEAD)
                    act.wait_ge(x_new, n + c + 1)
                    F(sq_wide[:, c, 0:T], x[:, c, :], ACT.Square).then_inc(squares_ready, 1)

            def scaled_operand(n, gain, norm_n):
                for c in range(KD):
                    act.wait_ge(x_new, n + c + 1)
                    F(h_hi[:, c, :], x[:, c, :], ACT.Identity, scale=col(gain, c)).then_inc(stage_hi, 1)
                    F(sq_wide[:, c, 0:T], x[:, c, :], ACT.Square).then_inc(squares_ready, 1)
                act.wait_ge(rstd_ready, norm_n)
                F(rs, rstd, ACT.Copy).then_inc(rs_ready, 1)

            scaled_operand(0, "ffn_pre_g", 12)

            def ffn_pair(p, turn, n, dst, dyn):
                split_hi(p + LEAD, turn)
                act.wait_ge(scaled, n - (STAGED_FFN1 - 1))
                F(stage2[:, (p // 2) % 2, :], stage2[:, (p // 2) % 2, :], ACT.Silu).then_inc(gate_ready, 1)
                split_hi(p + 1 + LEAD, turn)
                act.wait_ge(staged, n + 1)
                F(dst, stage[:, (p // 2) % 2, :], ACT.Copy).then_inc(stage_hi, 1)

            with act.Fori(0, UP1_TURNS) as i:
                for j in range(4):
                    ffn_pair(UP1 + 2 * j, i, i * 4 + (staged_n + j),
                             hid_hi[:, bass.ds(i * 4 + j, 1), :].rearrange("p a t -> p (a t)"), True)
            for j in range(4 * UP1_TURNS, KF):
                ffn_pair(UP1 + 2 * j, 0, staged_n + j, hid_hi[:, j, :], False)
            staged_n += KF
            for m in range(KD):
                for p in splits_before(m, down1_done, DOWN1, LRUX0):
                    split_hi(p + LEAD)
                act.wait_ge(pieces_done, down1_done(m))
                copy_and_square(acc_out(m), m_wide[:, m, :], sq_wide[:, m, 0:T])
            act.dma_start(bd[:, :, :, :], lru_w).then_inc(lru_w_loaded, 16)
            n = own.up(F(sp[:, 0, :], col("lru_lambda_2", 0, KD), ACT.Abs))
            act.wait_ge(act_steps, n)
            F(sp[:, 1, :], sp[:, 0, :], ACT.Exp, scale=-1.0).then_inc(sp_exp, 1)
            scaled_operand(KD, "norm1_g_2", 14)

            def lru_gates(c):
                act.wait_ge(bd_ready, c + 1)
                F(rg[:, c, :], B[:, 2 * (c % 2), 0:T], ACT.Sigmoid, bias=col("lru_ba_2", c)).then_inc(act_steps, 1)
                own.n += 1
                F(ig[:, c, :], B[:, 2 * (c % 2) + 1, 0:T], ACT.Sigmoid, bias=col("lru_bx_2", c)).then_inc(bd_drained, 1)

            for c in range(KD):
                split_hi(LRUX0 + c + LEAD)
                if c >= 2:
                    lru_gates(c - 2)
            for n in range(3 * KSC):
                split_hi(SC0 + n + LEAD)
                k, j = n // 3, n % 3
                if j == 2:
                    split_stage(staged_n + k, sc_hi[:, k, :])
                if n < 2:
                    lru_gates(KD - 2 + n)
                if 2 <= n < 6:
                    act.wait_ge(c_ready, 1)
                    act.wait_ge(bd_drained, KD)
                    for c in range(2 * n - 4, 2 * n - 2):
                        last = own.up(F(a_t[:, c, :], rg[:, c, :], ACT.Exp, scale=sp[:, 7, c:c + 1]))
                        F(th[:, c, :], rg[:, c, :], ACT.Tanh, scale=sp[:, 7, c:c + 1]).then_inc(act_steps, 1)
                        own.n += 1
                if n == 5:
                    act.wait_ge(act_steps, own.n)
                    F(rg[:, :, :], a_t[:, :, :], ACT.Square).then_inc(a_ready, 1)
                if n == 7:
                    act.wait_ge(m2_ready, 1)
                    F(th[:, :, :], th[:, :, :], ACT.Sqrt, scale=-1.0).then_inc(mult_ready, 1)
            staged_n += KSC
            for c in range(KD):
                split_hi(LRUG0 + c + LEAD)
                act.wait_ge(scaled, KF + c + 1)
                F(stage2[:, c % 2, :], stage2[:, c % 2, :], ACT.Gelu_apprx_tanh).then_inc(gelu_ready, 1)
                split_stage(staged_n + c, lru_hi[:, c, :])
            staged_n += KD
            residual_squares(2 * KD, OUT2, UP2)
            for k in range(KD):
                act.wait_ge(staged, staged_n + k + 1)
                F(h_hi[:, k, :], staging(k), ACT.Copy).then_inc(stage_hi, 1)
            staged_n += KD

            def hid2_high(n, b):
                act.wait_ge(staged, n + (staged_n + 1))
                at = slice(n, n + 1) if isinstance(n, int) else bass.ds(n, 1)
                F(hid_hi[:, at, :].rearrange("p a t -> p (a t)"), stage[:, b, :], ACT.Copy).then_inc(stage_hi, 1)

            def gelu2(n, b):
                act.wait_ge(conv2_ready, n + 1)
                F(tap[0][:, b, :], tap[0][:, b, :], ACT.Gelu_apprx_tanh).then_inc(gelu_ready, 1)

            def ffn2_pair(j, i, first=False):
                p = UP2 + 2 * j
                b = j % 2
                n = i * 4 + j
                for half_ in range(2):
                    act.wait_ge(pieces_done, p + half_ + 1 + 8 * i)
                    if half_ == 0:
                        act.wait_ge(staged, n + (staged_n - 1))
                    at = n * (2 * FFN_K) + (half_ * FFN_K + 2)
                    w2 = col("ffn_conv_w_2", at) if isinstance(n, int) else dcol("ffn_conv_w_2", at)
                    F(tap[half_][:, b, :], A[2 * b + half_][:, 0:T], ACT.Identity, scale=w2).then_inc(tap_ready, 1)
                    if half_ == 0 and not first:
                        gelu2(n - 1, 1 - b)
                    if half_ == 1 and not first:
                        hid2_high(n - 1, 1 - b)
                    split_hi(p + half_ + LEAD, i)

            tap = (stage2, stage3)
            for j in range(4):
                ffn2_pair(j, 0, j == 0)
            with act.Fori(1, UP2_TURNS) as i:
                for j in range(4):
                    ffn2_pair(j, i)
            gelu2(KF2 - 1, 1)
            hid2_high(KF2 - 1, 1)
            staged_n += KF2
            for p in range(DOWN2, PIECES):
                split_hi(p + LEAD)
            residual_squares(3 * KD)

        @block.vector
        def _(dve):
            V = nc.vector
            own = Count(dve_steps)

            def after(value):
                dve.wait_ge(dve_steps, value)

            def split_lo(p, turn=0):
                if p >= PIECES:
                    return
                s = p % RING
                dve.wait_ge(hi_ready, p + 1 + 8 * turn)
                V.tensor_tensor(w_lo[:, s, :], raw[:, s, :], w_hi[:, s, :].bitcast(F32), ALU.subtract).then_inc(lo_ready, 1)

            def operand_low(n, src, hi, lo):
                dve.wait_ge(stage_hi, n + 1)
                V.tensor_tensor(lo, src, hi.bitcast(F32), ALU.subtract).then_inc(operand_ready, 1)

            def moment_of(n, count, eps):
                dve.wait_ge(sums_ready, n)
                return V.tensor_scalar(moment[:, :], sums, 1.0 / count, eps, ALU.mult, ALU.add)

            def taps(c, ks, bias=None, fresh=True):
                dyn = not isinstance(c, int)

                def vs(k):
                    if dyn:
                        return v[:, bass.ds(c, 1), k:k + T].rearrange("p a t -> p (a t)")
                    return v[:, c, k:k + T]

                def w(k):
                    return dcol("conv_dw_w", c * CONV_K + k) if dyn else col("conv_dw_w", c * CONV_K + k)

                parts = (part[:, 0], part[:, 1])
                last = [None, None] if fresh else [own.value()] * 2
                for n, k in enumerate(ks):
                    dst = parts[n % 2]
                    if n < 2 and fresh:
                        b = bias if n == 0 else None
                        ins = V.tensor_scalar(dst, vs(k), w(k), b, ALU.mult,
                                              ALU.add if b is not None else ALU.bypass)
                    else:
                        after(last[n % 2])
                        ins = V.scalar_tensor_tensor(dst, vs(k), w(k), dst, ALU.mult, ALU.add)
                    last[n % 2] = own.up(ins)
                after(last[(len(ks) - 1) % 2])
                return own.value()

            def more_taps(c, ks):
                taps(c, ks, fresh=False)

            def add_parts(c, first=False):
                dyn = not isinstance(c, int)
                a = acc[:, bass.ds(c, 1), :].rearrange("p a t -> p (a t)") if dyn else acc[:, c, :]
                if first:
                    own.up(V.tensor_tensor(a, part[:, 0], part[:, 1], ALU.add))
                    return
                n = own.up(V.tensor_tensor(part[:, 0], part[:, 0], part[:, 1], ALU.add))
                after(n)
                n = own.up(V.tensor_tensor(a, a, part[:, 0], ALU.add))
                after(n)

            square_sum_at = [None, None]

            def add_square(src, n0, c):
                b = c % 2
                if c < 2:
                    return
                dve.wait_ge(squares_ready, n0 + c + 1)
                if c >= 4:
                    after(square_sum_at[b])
                square_sum_at[b] = own.up(V.tensor_tensor(sq_sum[:, b, :], src[:, c, 0:T],
                                                          src[:, b, 0:T] if c < 4 else sq_sum[:, b, :], ALU.add))

            def add_squares_up():
                after(square_sum_at[1])
                V.tensor_tensor(sq_sum[:, 0, :], sq_sum[:, 0, :], sq_sum[:, 1, :], ALU.add).then_inc(squares_summed, 1)

            def sum_squares(src, n0):
                for c in range(KD):
                    add_square(src, n0, c)
                add_squares_up()

            sum_squares(acc, 0)
            moment_of(1, D, RMS_EPS).then_inc(mean_ready, 1)
            split_lo(0)
            for half_x in x_loaded:
                dve.wait_ge(half_x, 16)
            dve.wait_ge(const_loaded, 32)
            dve.wait_ge(rstd_ready, 1)
            for k in range(KD):
                V.scalar_tensor_tensor(acc[:, k, :], x[:, k, :], col("mix_pre_g", k), rstd, ALU.mult,
                                       ALU.mult).then_inc(staged, 1)
                if k > 1:
                    operand_low(k - 2, acc[:, k - 2, :], h_hi[:, k - 2, :], h_lo[:, k - 2, :])
            for k in range(KD - 2, KD):
                operand_low(k, acc[:, k, :], h_hi[:, k, :], h_lo[:, k, :])
            dve.wait_ge(lo_ready, 2)
            for p in range(2, LEAD):
                split_lo(p)

            def log1p_first(e, t1, t2, t3, t4):
                after(own.up(V.tensor_scalar(t1, e, 2.0, None, ALU.add)))
                after(own.up(V.reciprocal(t2, t1)))
                after(own.up(V.tensor_tensor(t3, e, t2, ALU.mult)))
                own.up(V.tensor_scalar(t1, t3, 2.0, None, ALU.mult))
                after(own.up(V.tensor_tensor(t4, t3, t3, ALU.mult)))
                after(own.up(V.tensor_scalar(t2, t4, 1.0 / 15, None, ALU.mult)))

            def log1p_powers(t2, t4, ds):
                for d in ds:
                    after(own.up(V.scalar_tensor_tensor(t2, t2, 1.0 / d, t4, ALU.add, ALU.mult)))

            def log1p_last(t1, t2, dst):
                after(own.up(V.scalar_tensor_tensor(dst, t2, 1.0, t1, ALU.add, ALU.mult)))

            dw = [gates[0:HEADS, j, :] for j in range(2 * KD)]

            def step_sizes(part_n):
                if part_n == 0:
                    dve.wait_ge(dt_raw_ready, 1)
                    after(own.up(V.tensor_scalar(dw[3], B[0:HEADS, 0, 0:T],
                                                 par[0:HEADS, AT["dt_bias"]:AT["dt_bias"] + 1], None, ALU.add)))
                    V.tensor_copy(dw[7], dw[3]).then_inc(dt_abs, 1)
                    own.up(V.memset(dw[8], 1.0))
                    V.memset(dw[9], 0.0).then_inc(dt_raw_used, 1)
                if part_n == 1:
                    dve.wait_ge(dt_exp, 1)
                    log1p_first(dw[5], dw[10], dw[11], dw[12], dw[13])
                if part_n == 2:
                    log1p_powers(dw[11], dw[13], (13, 11, 9, 7, 5, 3))
                if part_n == 3:
                    log1p_last(dw[10], dw[11], dw[14])
                    after(own.up(V.scalar_tensor_tensor(dw[0], dw[3], 0.0, dw[14], ALU.max, ALU.add)))
                    dve.wait_ge(dt_exp, 2)
                    after(own.up(V.tensor_scalar(dw[15], dw[0], dw[6][:, 0:1], -1.0, ALU.mult, ALU.mult)))
                    for t in range(TT):
                        own.up(V.tensor_tensor_scan(dw[1][:, t * P:(t + 1) * P], dw[8][:, 0:P],
                                                    dw[15][:, t * P:(t + 1) * P], 0.0, ALU.mult, ALU.add))
                    after(own.value())
                    V.tensor_scalar(dw[2][:, 0:P], dw[1][:, 0:P], dw[1][:, P - 1:P], None,
                                    ALU.subtract).then_inc(cs_ready, 1)

            GLU_TAPS, LOOP_TAPS, LATE_TAPS = range(7), range(7, CONV_K - 4), range(CONV_K - 4, CONV_K)
            dve.wait_ge(constants_written, 4)
            for c in range(KD):
                p = GLU0 + 2 * c
                dve.wait_ge(pieces_done, p + 2)
                dve.wait_ge(gate_ready, c + 1)
                V.scalar_tensor_tensor(v[:, c, PAD:], A[2 * (c % 2) + 1][:, 0:T], col("glu_b", c), stage2[:, c % 2, :],
                                       ALU.add, ALU.mult).then_inc(pairs_drained, 1)
                dve.wait_ge(pairs_drained, c + 1)
                taps(c, GLU_TAPS, col("conv_dw_b", c))
                if c == 0:
                    dve.wait_ge(dt_raw_ready, 1)
                add_parts(c, True)
                if 1 <= c <= 4:
                    step_sizes(c - 1)
            dve.wait_ge(tok_psum, 1)
            V.tensor_copy(tok[:, :, :], A[3][:, 0:5 * HEADS].rearrange("p (a b) -> p a b", a=5)).then_inc(scale_read, 1)

            def conv_inputs(g, js, drained_n):
                dyn = not isinstance(g, int)

                def w(j, k):
                    at = (g * 4 + j) * SSM_K + k
                    return dcol("ssm_conv_w", at) if dyn else col("ssm_conv_w", at)

                last = {}
                for k in range(SSM_K):
                    for j in js:
                        src = ubuf[:, j, k:k + T]
                        if k == 0:
                            dve.wait_ge(drained, drained_n + j + 1)
                            b = dcol("ssm_conv_b", g * 4 + j) if dyn else col("ssm_conv_b", g * 4 + j)
                            ins = V.tensor_scalar(gb[:, j, :], src, w(j, k), b, ALU.mult, ALU.add)
                        else:
                            after(last[j])
                            ins = V.scalar_tensor_tensor(gb[:, j, :], src, w(j, k), gb[:, j, :], ALU.mult, ALU.add)
                        if k < SSM_K - 1:
                            last[j] = own.up(ins)
                        else:
                            ins.then_inc(conv_ready, 1)

            def heads(k, g):
                t = tok[:, k, bass.ds(g * HPG, HPG)] if not isinstance(g, int) else tok[:, k, g * HPG:(g + 1) * HPG]
                return t.unsqueeze(2)

            def masked_scores(g):
                dve.wait_ge(cb_ready, g + 1)
                V.tensor_tensor(cbm[:, :], A[3][:, 0:3 * P], mask, ALU.mult).then_inc(cb_used, 1)

            def x_by_dt(g):
                dve.wait_ge(xt_ready, g + 1)
                for t in range(TT):
                    ins = V.tensor_tensor(xdt[:, t, :, :], A[3][:, t * T:(t + 1) * T].rearrange("p (a b) -> p a b", a=HPG),
                                          heads(t, g).to_broadcast([P, HPG, HD]), ALU.mult)
                    ins.then_inc(xdt_ready, 1)

            def decayed_scores(g):
                dve.wait_ge(dec_ready, g + 1)
                dve.wait_ge(cb_used, g + 1)
                V.tensor_tensor(dec[:, :, :], dec[:, :, :], cbm[:, :].unsqueeze(1).to_broadcast([P, HPG, 3 * P]),
                                ALU.mult).then_inc(m_ready, 1)

            def y_gated(g):
                dyn = not isinstance(g, int)
                dve.wait_ge(y_ready, g + 1)
                for c in range(2):
                    d = dcol("d_skip", g * 2 + c) if dyn else col("d_skip", g * 2 + c)
                    own.up(V.scalar_tensor_tensor(y[:, c, :], gb[:, 2 + c, :], d, A[3][:, c * T:(c + 1) * T],
                                                  ALU.mult, ALU.add))
                after(own.value())
                dve.wait_ge(drained, g * 6 + 6)
                V.tensor_tensor(y[:, :, :], y[:, :, :], zs[:, :, :], ALU.mult).then_inc(yz_ready, 1)

            def y_mean(g):
                moment_of(g + 2, 2 * P, RMS_EPS).then_inc(mean_ready, 1)

            def y_normed(g):
                dyn = not isinstance(g, int)
                dve.wait_ge(rstd_ready, g + 2)
                for c in range(2):
                    w = dcol("ssm_norm_g", g * 2 + c) if dyn else col("ssm_norm_g", g * 2 + c)
                    ins = V.scalar_tensor_tensor(y[:, c, :], y[:, c, :], w, rstd, ALU.mult, ALU.mult)
                    if c == 0:
                        own.up(ins)
                ins.then_inc(scale_read, 1)

            def y_low(g):
                dve.wait_ge(ynhi_ready, g + 1)
                for c in range(2):
                    V.tensor_tensor(yn_lo[:, c, :], y[:, c, :], yn_hi[:, c, :].bitcast(F32),
                                    ALU.subtract).then_inc(yn_ready, 1)

            def late_taps(cs):
                last = {c: own.value() for c in cs}
                for k in LATE_TAPS:
                    for c in cs:
                        after(last[c])
                        last[c] = own.up(V.scalar_tensor_tensor(acc[:, c, :], v[:, c, k:k + T],
                                                                col("conv_dw_w", c * CONV_K + k), acc[:, c, :],
                                                                ALU.mult, ALU.add))

            def group_turn(g, first=False, more=True):
                conv_inputs(g, (0, 1), g * 6)
                if not first:
                    y_low(g - 1)
                conv_inputs(g, (2, 3), g * 6)
                masked_scores(g)
                if more:
                    taps(g + 1, LOOP_TAPS[:6])
                else:
                    late_taps((0, 1))
                x_by_dt(g)
                decayed_scores(g)
                if more:
                    more_taps(g + 1, LOOP_TAPS[6:12])
                else:
                    late_taps((2, 3, 4))
                y_gated(g)
                if more:
                    more_taps(g + 1, LOOP_TAPS[12:16])
                else:
                    late_taps((5, 6))
                y_mean(g)
                if more:
                    more_taps(g + 1, LOOP_TAPS[16:])
                    add_parts(g + 1)
                else:
                    late_taps((7,))
                y_normed(g)

            after(own.value())
            taps(0, LOOP_TAPS)
            add_parts(0)
            group_turn(0, True)
            with dve.Fori(0, GROUPS - 2) as i:
                own.enter(i, 4 * (SSM_K - 1) + len(LOOP_TAPS) + 2 + 2 + 1)
                group_turn(i + 1)
                own.leave(GROUPS - 2)

            g = GROUPS - 1
            group_turn(g, more=False)
            after(own.value())
            last = [None, None]
            for c in range(2, KD):
                b = c % 2
                if c >= 4:
                    after(last[b])
                last[b] = own.up(V.tensor_tensor(sq_sum[:, b, :], acc[:, c, :], acc[:, b, :] if c < 4 else sq_sum[:, b, :],
                                                 ALU.add))
            for n in last:
                after(n)
            V.memset(part[:, 0], 0.0).then_inc(conv_sum_ready, 1)
            y_low(g)
            dve.wait_ge(sums_ready, 10)
            after(own.up(V.tensor_scalar(mean[:, :], A[3][:, 0:T], 1.0 / D, None, ALU.mult)))
            for c in range(KD):
                V.tensor_tensor(acc[:, c, :], acc[:, c, :], mean[:, :], ALU.subtract).then_inc(centred, 1)
            sum_squares(v, KD)
            moment_of(11, D, LN_EPS).then_inc(mean_ready, 1)
            dve.wait_ge(rstd_ready, 10)
            for c in range(KD):
                V.scalar_tensor_tensor(acc[:, c, :], acc[:, c, :], col("conv_ln_g", c), rstd, ALU.mult,
                                       ALU.mult).then_inc(conv_norm, 1)
            for c in range(KD):
                operand_low(KD + c, stage[:, c % 2, :], conv_hi[:, c, :], conv_lo[:, c, :])

            dve.wait_ge(pieces_done, PW0)
            dve.wait_ge(gates_ready, 2)
            staged_n = KD
            hi_n = 2 * KD
            for m in range(KD):
                dve.wait_ge(pieces_done, PW0 + m + 1)
                n = own.up(V.tensor_tensor(stage2[:, 0, :], acc_out(m), gates[:, KD + m, :], ALU.mult))
                V.scalar_tensor_tensor(stage2[:, 1, :], A[(64 + m) % 3][:, 0:T], col("conv_pw_b", m), gates[:, m, :],
                                       ALU.add, ALU.mult).then_inc(mix_drained, 1)
                after(n)
                dve.wait_ge(mix_drained, m + 1)
                V.tensor_tensor(stage[:, m % 2, :], stage2[:, 0, :], stage2[:, 1, :], ALU.add).then_inc(staged, 1)
                operand_low(hi_n + m, stage[:, m % 2, :], h_hi[:, m, :], h_lo[:, m, :])
            staged_n += KD
            hi_n += KD

            def residual_scaled(sums_n, norm_n, gain, next_gain, hi_n):
                moment_of(sums_n, D, RMS_EPS).then_inc(mean_ready, 1)
                dve.wait_ge(rstd_ready, norm_n)
                last = []
                for c in range(KD + 2):
                    if c < KD:
                        last.append(own.up(V.scalar_tensor_tensor(m_wide[:, c, :], m_wide[:, c, :], col(gain, c),
                                                                  rstd, ALU.mult, ALU.mult)))
                    if 1 <= c <= KD:
                        after(last[c - 1])
                        V.tensor_tensor(x[:, c - 1, :], x[:, c - 1, :], m_wide[:, c - 1, :],
                                        ALU.add).then_inc(x_new, 1)
                    if c >= 2:
                        dve.wait_ge(stage_hi, hi_n + c - 1)
                        V.scalar_tensor_tensor(h_lo[:, c - 2, :], x[:, c - 2, :], col(next_gain, c - 2),
                                               h_hi[:, c - 2, :].bitcast(F32), ALU.mult,
                                               ALU.subtract).then_inc(operand_ready, 1)
                moment_of(sums_n + 1, D, RMS_EPS).then_inc(mean_ready, 1)

            def normed_operand(sums_n, norm_n, gain, hi_n):
                moment_of(sums_n, D, RMS_EPS).then_inc(mean_ready, 1)
                dve.wait_ge(rstd_ready, norm_n)

                for k in range(KD + 2):
                    if k >= 2:
                        operand_low(hi_n + k - 2, staging(k - 2), h_hi[:, k - 2, :], h_lo[:, k - 2, :])
                    if k < KD:
                        if k >= 4:
                            dve.wait_ge(operand_ready, hi_n + k - 3)
                        V.scalar_tensor_tensor(staging(k), x[:, k, :], col(gain, k), rstd, ALU.mult,
                                               ALU.mult).then_inc(staged, 1)

            sum_squares(sq_wide, 2 * KD)
            residual_scaled(12, 11, "mix_post_g", "ffn_pre_g", hi_n)
            hi_n += KD

            dve.wait_ge(lo_ready, UP1 + LEAD)

            def ffn_pair(p, turn, pair, hi, lo):
                b = (p // 2) % 2
                dve.wait_ge(pieces_done, p + 1 + 8 * turn)
                dve.wait_ge(staged, pair + (STAGED_FFN1 - 1))
                V.tensor_tensor(stage2[:, b, :], A[2 * b][:, 0:T], rs, ALU.mult).then_inc(scaled, 1)
                split_lo(p + LEAD, turn)
                dve.wait_ge(pieces_done, p + 2 + 8 * turn)
                dve.wait_ge(operand_ready, pair + (hi_n - 1))
                n = own.up(V.tensor_tensor(stage[:, b, :], A[2 * b + 1][:, 0:T], rs, ALU.mult))
                after(n)
                dve.wait_ge(gate_ready, pair + (KD + 1))
                V.tensor_tensor(stage[:, b, :], stage2[:, b, :], stage[:, b, :], ALU.mult).then_inc(staged, 1)
                split_lo(p + 1 + LEAD, turn)
                dve.wait_ge(stage_hi, pair + (hi_n + 1))
                V.tensor_tensor(lo, stage[:, b, :], hi.bitcast(F32), ALU.subtract).then_inc(operand_ready, 1)

            dve.wait_ge(rs_ready, 1)
            with dve.Fori(0, UP1_TURNS) as i:
                own.enter(i, 4)
                for j in range(4):
                    at = bass.ds(i * 4 + j, 1)
                    ffn_pair(UP1 + 2 * j, i, i * 4 + j, hid_hi[:, at, :].rearrange("p a t -> p (a t)"),
                             hid_lo[:, at, :].rearrange("p a t -> p (a t)"))
                own.leave(UP1_TURNS)
            for j in range(4 * UP1_TURNS, KF):
                ffn_pair(UP1 + 2 * j, 0, j, hid_hi[:, j, :], hid_lo[:, j, :])
            hi_n += KF
            staged_n += KF
            for c in range(KD):
                for p in splits_before(c, down1_done, DOWN1, LRUX0):
                    split_lo(p + LEAD)
                add_square(sq_wide, 4 * KD, c)
            add_squares_up()
            residual_scaled(14, 13, "ffn_post_g", "norm1_g_2", hi_n)
            hi_n += KD

            dve.wait_ge(sp_exp, 1)
            log1p_first(sp[:, 1, :], sp[:, 2, :], sp[:, 3, :], sp[:, 4, :], sp[:, 5, :])
            log1p_powers(sp[:, 3, :], sp[:, 5, :], (13, 11, 9, 7, 5, 3))
            log1p_last(sp[:, 2, :], sp[:, 3, :], sp[:, 6, :])
            n = own.up(V.tensor_scalar(sp[:, 2, :], col("lru_lambda_2", 0, KD), -1.0, 0.0, ALU.mult, ALU.max))
            after(n)
            n = own.up(V.tensor_tensor(sp[:, 3, :], sp[:, 2, :], sp[:, 6, :], ALU.add))
            after(n)
            V.tensor_scalar(sp[:, 7, :], sp[:, 3, :], -RG_C, None, ALU.mult).then_inc(c_ready, 1)
            n = own.up(V.memset(u2[:, :, 0:LRU_K - 1], 0.0))
            after(n)
            dve.wait_ge(rs_ready, 2)
            V.tensor_tensor(rs2, rs, rs, ALU.mult).then_inc(rs2_ready, 1)

            def lru_conv(c):
                dve.wait_ge(pieces_done, LRUX0 + c + 1)
                if c >= 2:
                    dve.wait_ge(xp_ready, c - 1)
                V.tensor_tensor(u2[:, c % 2, LRU_K - 1:], A[c % 3][:, 0:T], rs, ALU.mult).then_inc(copied, 1)
                dve.wait_ge(copied, c + 1)
                n = own.up(V.tensor_scalar(xp[:, c, 0:T], u2[:, c % 2, 0:T], col("lru_conv_w_2", c * LRU_K),
                                           col("lru_conv_b_2", c), ALU.mult, ALU.add))
                for k in range(1, LRU_K):
                    after(n)
                    ins = V.scalar_tensor_tensor(xp[:, c, 0:T], u2[:, c % 2, k:k + T], col("lru_conv_w_2", c * LRU_K + k),
                                                 xp[:, c, 0:T], ALU.mult, ALU.add)
                    if k < LRU_K - 1:
                        n = own.up(ins)
                    else:
                        ins.then_inc(xp_ready, 1)

            for c in range(KD):
                lru_conv(c)
            prod = u2
            for n_ in range(3 * KSC):
                k, j = n_ // 3, n_ % 3
                if j == 0:
                    dve.wait_ge(pieces_done, SC0 + n_ + 1)
                    dve.wait_ge(rs2_ready, 1)
                    if k >= 2:
                        dve.wait_ge(staged, STAGED_SC + k - 1)
                    V.tensor_tensor(stage2[:, k % 2, :], eight_banks(n_), rs2, ALU.mult).then_inc(sc_copied, 1)
                if j == 1:
                    dve.wait_ge(sc_copied, k + 1)
                    dve.wait_ge(pieces_done, SC0 + n_ + 1)
                    if k == 0:
                        dve.wait_ge(xp_ready, KD)
                    n = own.up(V.tensor_tensor(prod[:, 0, SC_K:SC_K + T], stage2[:, k % 2, :], eight_banks(n_),
                                               ALU.mult))
                    after(n)
                    n = own.up(V.tensor_scalar(sc_sum[:, :], prod[:, 0, 1:1 + T], col("sc_conv_w_2", k * SC_K), None,
                                               ALU.mult))
                    for q in range(1, SC_K):
                        after(n)
                        n = own.up(V.scalar_tensor_tensor(sc_sum[:, :], prod[:, 0, 1 + q:1 + q + T],
                                                          col("sc_conv_w_2", k * SC_K + q), sc_sum[:, :], ALU.mult,
                                                          ALU.add))
                    after(n)
                    n = own.up(V.tensor_tensor(sc_sum[:, :], sc_sum[:, :], rs, ALU.mult))
                if j == 2:
                    dve.wait_ge(pieces_done, SC0 + n_ + 1)
                    after(n)
                    V.tensor_tensor(stage[:, (staged_n + k) % 2, :], sc_sum[:, :], eight_banks(n_),
                                    ALU.mult).then_inc(staged, 1)
                    operand_low(hi_n + k, stage[:, (staged_n + k) % 2, :], sc_hi[:, k, :], sc_lo[:, k, :])
                if n_ == 3:
                    dve.wait_ge(bd_drained, KD)
                    own.up(V.tensor_tensor(ig[:, :, :], ig[:, :, :], xp[:, :, 0:T], ALU.mult))
                if n_ == 6:
                    dve.wait_ge(a_ready, 1)
                    V.scalar_tensor_tensor(th[:, :, :], rg[:, :, :], 1.0, th[:, :, :], ALU.add,
                                           ALU.mult).then_inc(m2_ready, 1)
                if n_ == 9:
                    dve.wait_ge(mult_ready, 1)
                    inputs_scaled = own.up(V.tensor_tensor(ig[:, :, :], ig[:, :, :], th[:, :, :], ALU.mult))
            after(inputs_scaled)
            for c in range(KD):
                lru_scanned = own.up(V.tensor_tensor_scan(xp[:, c, 0:T], a_t[:, c, :], ig[:, c, :], 0.0, ALU.mult,
                                                          ALU.add))
            hi_n += KSC
            staged_n += KSC
            after(lru_scanned)
            for c in range(KD):
                dve.wait_ge(pieces_done, LRUG0 + c + 1)
                if c >= 2:
                    dve.wait_ge(staged, STAGED_LRU + c - 1)
                V.tensor_tensor(stage2[:, c % 2, :], eight_banks(c + 4), rs, ALU.mult).then_inc(scaled, 1)
                dve.wait_ge(gelu_ready, c + 1)
                V.tensor_tensor(stage[:, (staged_n + c) % 2, :], xp[:, c, 0:T], stage2[:, c % 2, :],
                                ALU.mult).then_inc(staged, 1)
                operand_low(hi_n + c, stage[:, (staged_n + c) % 2, :], lru_hi[:, c, :], lru_lo[:, c, :])
            hi_n += KD
            staged_n += KD
            dve.wait_ge(lo_ready, OUT2 + LEAD)

            def add_accumulated(done, n0, first=0, end=0):
                for m in range(0, KD, 2):
                    for p in splits_before(m, done, first, end):
                        split_lo(p + LEAD)
                    dve.wait_ge(pieces_done, done(m))
                    for c in (m, m + 1):
                        V.tensor_tensor(x[:, c, :], x[:, c, :], acc_out(c), ALU.add).then_inc(x_new, 1)
                    for c in (m, m + 1):
                        add_square(sq_wide, n0, c)
                add_squares_up()

            add_accumulated(out2_done, 6 * KD, OUT2, UP2)
            normed_operand(16, 15, "norm2_g_2", hi_n)
            hi_n += KD
            staged_n += KD

            tap = (stage2, stage3)

            def hid2_product(n, b):
                dve.wait_ge(gelu_ready, n + (KD + 1))
                dve.wait_ge(pairs_drained, n + (KD + 1))
                V.tensor_tensor(stage[:, b, :], tap[0][:, b, :], tap[1][:, b, :], ALU.mult).then_inc(staged, 1)

            def hid2_low(n, b):
                dve.wait_ge(stage_hi, n + (hi_n + 1))
                at = slice(n, n + 1) if isinstance(n, int) else bass.ds(n, 1)
                V.tensor_tensor(hid_lo[:, at, :].rearrange("p a t -> p (a t)"), stage[:, b, :],
                                hid_hi[:, at, :].rearrange("p a t -> p (a t)").bitcast(F32),
                                ALU.subtract).then_inc(operand_ready, 1)

            def ffn2_pair(j, i, first=False):
                p = UP2 + 2 * j
                b = j % 2
                n = i * 4 + j
                last = {}
                for k, half_ in ((1, 0), (1, 1), (0, 0), (0, 1)):
                    if k == 1:
                        dve.wait_ge(tap_ready, n * 2 + (half_ + 1))
                    else:
                        after(last[half_])
                    sh = FFN_K - 1 - k
                    at = n * (2 * FFN_K) + (half_ * FFN_K + k)
                    w = col("ffn_conv_w_2", at) if isinstance(n, int) else dcol("ffn_conv_w_2", at)
                    ins = V.scalar_tensor_tensor(tap[half_][:, b, sh:], A[2 * b + half_][:, 0:T - sh], w,
                                                 tap[half_][:, b, sh:], ALU.mult, ALU.add)
                    if k == 1:
                        last[half_] = own.up(ins)
                    elif half_ == 0:
                        ins.then_inc(conv2_ready, 1)
                    else:
                        ins.then_inc(pairs_drained, 1)
                    if k == 1 and half_ == 0:
                        if not first:
                            hid2_product(n - 1, 1 - b)
                        split_lo(p + LEAD, i)
                if not first:
                    hid2_low(n - 1, 1 - b)
                split_lo(p + 1 + LEAD, i)

            for j in range(4):
                ffn2_pair(j, 0, j == 0)
            with dve.Fori(1, UP2_TURNS) as i:
                own.enter(i - 1, 8)
                for j in range(4):
                    ffn2_pair(j, i)
                own.leave(UP2_TURNS - 1)
            hid2_product(KF2 - 1, 1)
            hid2_low(KF2 - 1, 1)
            for p in range(DOWN2, PIECES):
                split_lo(p + LEAD)
            add_accumulated(lambda m: DOWN2 + 2 * KD + m + 2, 7 * KD)
            moment_of(17, D, RMS_EPS).then_inc(mean_ready, 1)
            dve.wait_ge(rstd_ready, 16)
            dve.wait_ge(x_new, 4 * KD)
            for c in range(KD):
                V.scalar_tensor_tensor(m_wide[:, c, :], x[:, c, :], col("final_g_2", c), rstd, ALU.mult,
                                       ALU.mult).then_inc(out_ready, 1)


def _pieces(w):
    m = w.shape[1] // P
    return [w[:, c * P:(c + 1) * P].reshape(8, P, P).transpose(1, 0, 2).reshape(P, PIECE) for c in range(m)]


def _tiles(w, ks, by_row=False):
    order = [(k, m) for k in ks for m in range(8)] if by_row else [(k, m) for m in range(8) for k in ks]
    cut = [w[k * P:(k + 1) * P, m * P:(m + 1) * P] for k, m in order]
    return [np.concatenate(cut[i:i + 8], axis=1) for i in range(0, len(cut), 8)]


def pack_weights(a):
    w_in, w2 = a["w_in"][0], a["w_in_2"][0]
    w_ssm = a["ssm_out_w"][0]

    def chunk(w, at):
        return _pieces(w[:, at:at + P])

    def group(g):
        xbc = 2 * D + D_INNER
        s = chunk(w_in, xbc + D_INNER + g * P) + chunk(w_in, xbc + D_INNER + GROUPS * P + g * P)
        for base in (xbc, 2 * D):
            for c in range(2):
                s += chunk(w_in, base + (2 * g + c) * P)
        return s

    s = []
    for c in range(KD):
        s += chunk(w_in, D + c * P) + chunk(w_in, c * P)
    s += group(0)
    s += group(1)
    for i in range(1, GROUPS - 1):
        n, o = group(i + 1), _tiles(w_ssm, (2 * i - 2, 2 * i - 1), True)
        s += n[:2] + o[:1] + n[2:4] + o[1:] + n[4:]
    n = _pieces(w_in[:, w_in.shape[1] - 2 * D:])
    o = _tiles(w_ssm, (2 * GROUPS - 4, 2 * GROUPS - 3), True)
    s += n[:2] + o[:1] + n[2:4] + o[1:] + n[4:]
    s += _tiles(w_ssm, (2 * GROUPS - 2, 2 * GROUPS - 1), True)
    s += _pieces(a["conv_pw_w"][0]) + _pieces(a["w_out"][0])
    wu = a["w_gate_up"][0]
    for j in range(KF):
        s += chunk(wu, j * P) + chunk(wu, FFN + j * P)
    wd = a["w_down"][0]
    for t in range(KF // 8):
        s += _tiles(wd, range(8 * t, 8 * t + 8))
    s += _tiles(wd, range(8 * (KF // 8), KF))
    s += _pieces(w2[:, :D_LRU])
    for k in range(KSC):
        for part in (1, 2, 0):
            s += chunk(w2, 2 * D_LRU + part * D_SC + k * P)
    s += _pieces(w2[:, D_LRU:2 * D_LRU])
    wo = a["w_out_2"][0]
    s += _tiles(wo, range(KD, KD + KSC)) + _tiles(wo, range(KD))
    wu = a["w_up_2"][0]
    for j in range(KF2):
        s += chunk(wu, j * P) + chunk(wu, FFN2 + j * P)
    wd = a["w_down_2"][0]
    for t in range(KF2 // 8):
        s += _tiles(wd, range(8 * t, 8 * t + 8))
    assert len(s) == PIECES
    return np.stack(s).reshape(PIECES // 2, 2, P, PIECE).transpose(0, 2, 1, 3)


def pack_params(a):
    def cols(v):
        return v.reshape(-1, P).T

    def taps(w):
        return w.reshape(w.shape[0], -1, P).transpose(2, 1, 0).reshape(P, -1)

    def grouped(w):
        t = w.reshape(w.shape[0], -1, P)
        nx = D_INNER // P
        order = [c for g in range(GROUPS) for c in (nx + g, nx + GROUPS + g, 2 * g, 2 * g + 1)]
        return t[:, order].transpose(2, 1, 0).reshape(P, -1)

    def head_column(v):
        return np.concatenate([v, np.zeros(P - HEADS, v.dtype)]).reshape(P, 1)

    made = {
        "conv_dw_w": taps(a["conv_dw_w"][0]), "ssm_conv_w": grouped(a["ssm_conv_w"][0]),
        "ssm_conv_b": grouped(a["ssm_conv_b"]), "d_skip": cols(np.repeat(a["d_skip"][0], HD)),
        "lru_conv_w_2": taps(a["lru_conv_w_2"][0]), "sc_conv_w_2": taps(a["sc_conv_w_2"][0]),
        "dt_bias": head_column(a["dt_bias"][0]), "a_log": head_column(a["a_log"][0]),
        "ffn_conv_w_2": a["ffn_conv_w_2"][0].reshape(FFN_K, 2, KF2, P).transpose(3, 2, 1, 0).reshape(P, -1),
    }
    return np.concatenate([made[n] if n in made else cols(a[n]) for n, _ in PARAMS], axis=1)


def kernel(**inputs):
    import concourse.bacc as _bacc
    from concourse.bass_utils import run_bass_kernel_spmd as _run

    a = {k: np.asarray(v) for k, v in inputs.items()}
    at = 2 * D + D_INNER + 2 * D_INNER
    lru = np.zeros((P, KD, 2, P), np.float32)
    for j, name in enumerate(("lru_wa_2", "lru_wx_2")):
        for h in range(2 * KD):
            o = HD * (h % 2)
            lru[o:o + HD, h // 2, j, o:o + HD] = a[name][0, h]
    tri = np.triu(np.ones((P, P), np.float32))
    one = np.ones((P, P), np.float32)
    arrays = {
        "x": a["x"][0].T.reshape(KD, P, T).transpose(1, 0, 2),
        "weights": pack_weights(a),
        "params": pack_params(a),
        "w_dt": a["w_in"][0][:, at:at + HEADS].reshape(KD, P, HEADS).transpose(1, 0, 2),
        "lru_w": lru,
        "consts": np.concatenate([np.eye(P, dtype=np.float32), one, tri, one, tri], axis=1),
    }
    arrays = {f"in_{k}_dram": np.ascontiguousarray(v) for k, v in arrays.items()}
    nc = _bacc.Bacc("TRN2", target_bir_lowering=False, num_devices=1)
    args = [nc.dram_tensor(k, v.shape, mybir.dt.from_np(v.dtype), kind="ExternalInput").ap() for k, v in arrays.items()]
    args.append(nc.dram_tensor("out_0_dram", (P, KD, T), F32, kind="ExternalOutput").ap())
    hybrid_kernel(nc, *args)
    r = _run(nc, [arrays], core_ids=[0])
    got = r.results[0]["out_0_dram"]
    return np.ascontiguousarray(got.transpose(2, 1, 0).reshape(1, T, D))
```
